# Optimizing a Trainium2 kernel written in Bass

```python
import jax
import jax.numpy as jnp
from jax import lax
import numpy as np
import math
import jax, jax.numpy as jnp

D_MODEL = 1024
BATCH = 1
SEQ = 256
DEPTH = 2

GRID_W = 64
CTX_LEN = 256
EPS = 1e-6

CONV_DIM = 512
CONV_WIDTH = 31
MLSTM_HEADS = 4
MLSTM_QK = 64
MLSTM_V = 128
MLSTM_CHUNK = 64
AB_SIZES = (CONV_DIM, CONV_DIM, MLSTM_HEADS * MLSTM_QK, MLSTM_HEADS * MLSTM_QK,
            MLSTM_HEADS * MLSTM_V, MLSTM_HEADS * MLSTM_V, 4 * MLSTM_HEADS)
AB_IN = sum(AB_SIZES)
AB_OUT = CONV_DIM + MLSTM_HEADS * MLSTM_V

MLA_HEADS = 16
MLA_Q_LORA = 512
MLA_KV_LORA = 256
MLA_NOPE = 64
MLA_ROPE = 32
MLA_V = 64
MLA_QK = MLA_NOPE + MLA_ROPE
MLA_IN = MLA_Q_LORA + MLA_KV_LORA + MLA_ROPE
ROPE_BASE = 10000.0
ATTN_BLOCK = 128

FFN_DIM = 2816
FFN_CONV_WIDTH = 3


def _split_cols(a, sizes):
    return jnp.split(a, np.cumsum(sizes)[:-1].tolist(), axis=-1)

def _rms(x):
    xf = x.astype(jnp.float32)
    return (xf * lax.rsqrt(jnp.mean(xf * xf, axis=-1, keepdims=True) + EPS)).astype(x.dtype)

def _layer_norm(x, g, b):
    xf = x.astype(jnp.float32)
    mu = jnp.mean(xf, axis=-1, keepdims=True)
    var = jnp.mean(jnp.square(xf - mu), axis=-1, keepdims=True)
    return ((xf - mu) * lax.rsqrt(var + EPS)).astype(x.dtype) * g + b

def _modulate(x, shift, scale):
    return _rms(x) * (1 + scale) + shift

def _dwconv(x, w, b):
    k, ch = w.shape
    pad = (k - 1) // 2
    y = lax.conv_general_dilated(x, w[:, None, :].astype(x.dtype), (1,), [(pad, k - 1 - pad)],
                                 dimension_numbers=('NWC', 'WIO', 'NWC'), feature_group_count=ch)
    return y + b

def _zero_state(batch):
    return (jnp.zeros((batch, MLSTM_HEADS, MLSTM_V, MLSTM_QK), jnp.float32),
            jnp.zeros((batch, MLSTM_HEADS, MLSTM_QK), jnp.float32),
            jnp.zeros((batch, MLSTM_HEADS), jnp.float32))

def _mlstm_chunkwise(q, k, v, log_i, log_f, state):
    bsz, nh, t, _ = q.shape
    nc = t // MLSTM_CHUNK

    def chunks(a):
        return jnp.moveaxis(a.reshape(bsz, nh, nc, MLSTM_CHUNK, *a.shape[3:]), 2, 0)

    lower = jnp.tril(jnp.ones((MLSTM_CHUNK, MLSTM_CHUNK), bool))

    def step(carry, inp):
        c_mat, n_vec, m = carry
        qj, kj, vj, li, lf = inp
        b = jnp.cumsum(lf, axis=-1)
        log_d = jnp.where(lower, b[..., :, None] - b[..., None, :] + li[..., None, :], -jnp.inf)
        log_inter = b + m[..., None]
        m_row = jnp.maximum(log_inter, jnp.max(log_d, axis=-1))
        s = jnp.einsum('bhid,bhjd->bhij', qj, kj) * jnp.exp(log_d - m_row[..., None])
        inter = jnp.exp(log_inter - m_row)
        num = jnp.einsum('bhij,bhjv->bhiv', s, vj) + inter[..., None] * jnp.einsum('bhvd,bhid->bhiv', c_mat, qj)
        den = jnp.sum(s, axis=-1) + inter * jnp.einsum('bhd,bhid->bhi', n_vec, qj)
        h = num / jnp.maximum(jnp.abs(den), jnp.exp(-m_row))[..., None]
        b_last = b[..., -1]
        log_w = b_last[..., None] - b + li
        m_new = jnp.maximum(b_last + m, jnp.max(log_w, axis=-1))
        w = jnp.exp(log_w - m_new[..., None])
        decay = jnp.exp(b_last + m - m_new)
        c_new = decay[..., None, None] * c_mat + jnp.einsum('bhj,bhjv,bhjd->bhvd', w, vj, kj)
        n_new = decay[..., None] * n_vec + jnp.einsum('bhj,bhjd->bhd', w, kj)
        return (c_new, n_new, m_new), h

    state, h = lax.scan(step, state, (chunks(q), chunks(k), chunks(v), chunks(log_i), chunks(log_f)))
    return jnp.moveaxis(h, 0, 2).reshape(bsz, nh, t, -1), state

def _flip(t):
    return jnp.flip(t, axis=2)

def _ab_project(h, w_in, gate_bias):
    a, g, q, k, v, o, gates = _split_cols(h @ w_in, AB_SIZES)

    def heads(t, d):
        return t.reshape(*t.shape[:2], -1, d).transpose(0, 2, 1, 3).astype(jnp.float32)

    q = heads(q, MLSTM_QK)
    k = heads(k, MLSTM_QK) * (MLSTM_QK ** -0.5)
    v = heads(v, MLSTM_V)
    gates = (gates + gate_bias).astype(jnp.float32).transpose(0, 2, 1)
    ig_f, fg_f, ig_b, fg_b = jnp.split(gates, 4, axis=1)
    fwd = (ig_f, jax.nn.log_sigmoid(fg_f))
    bwd = (ig_b, jax.nn.log_sigmoid(fg_b))
    return a, g, q, k, v, o, fwd, bwd

def _conformer_mlstm_mixer(h_lat, h_ctx, w_in, gate_bias, conv_w, conv_b, ln_g, ln_b,
                           head_gain, w_out, with_ctx_out):
    lat = _ab_project(h_lat, w_in, gate_bias)
    ctx = _ab_project(h_ctx, w_in, gate_bias)
    zero = _zero_state(h_lat.shape[0])

    def scans(p, init_f, init_b):
        _, _, q, k, v, _, fwd, bwd = p
        h_f, st_f = _mlstm_chunkwise(q, k, v, fwd[0], fwd[1], init_f)
        h_b, st_b = _mlstm_chunkwise(_flip(q), _flip(k), _flip(v), _flip(bwd[0]), _flip(bwd[1]), init_b)
        return h_f + _flip(h_b), st_f, st_b

    h_ctx_seq, st_f, st_b = scans(ctx, zero, zero)
    h_lat_seq, _, _ = scans(lat, st_f, st_b)

    def merge(p, h_seq):
        a, g, _, _, _, o, _, _ = p
        u = _dwconv(a * jax.nn.sigmoid(g), conv_w, conv_b)
        u = jax.nn.silu(_layer_norm(u, ln_g, ln_b))
        hm = _rms(h_seq).transpose(0, 2, 1, 3)
        hm = hm.reshape(*hm.shape[:2], -1).astype(o.dtype) * head_gain * jax.nn.sigmoid(o)
        return jnp.concatenate([u, hm], axis=-1) @ w_out

    y_lat = merge(lat, h_lat_seq)
    y_ctx = merge(ctx, h_ctx_seq) if with_ctx_out else None
    return y_lat, y_ctx

def _axial_rope_tables(rows):
    row = jnp.repeat(jnp.arange(rows, dtype=jnp.float32), GRID_W)
    col = jnp.tile(jnp.arange(GRID_W, dtype=jnp.float32), rows)
    half = MLA_ROPE // 2
    inv_freq = ROPE_BASE ** (-jnp.arange(0, half, 2, dtype=jnp.float32) / half)
    ang = jnp.concatenate([row[:, None] * inv_freq, col[:, None] * inv_freq], axis=-1)
    return jnp.cos(ang), jnp.sin(ang)

def _rope_tail(t, cos, sin):
    nope, r = t[..., :MLA_NOPE], t[..., MLA_NOPE:]
    r = r.reshape(*r.shape[:-1], -1, 2)
    c = cos[None, :, None, :].astype(t.dtype)
    s = sin[None, :, None, :].astype(t.dtype)
    r1, r2 = r[..., 0], r[..., 1]
    rot = jnp.stack([r1 * c - r2 * s, r1 * s + r2 * c], axis=-1).reshape(*nope.shape[:-1], MLA_ROPE)
    return jnp.concatenate([nope, rot], axis=-1)

def _block_attention(q, k, v):
    bsz, tq, nh, dk = q.shape
    nb = tq // ATTN_BLOCK
    qb = jnp.moveaxis(q.reshape(bsz, nb, ATTN_BLOCK, nh, dk), 1, 0)
    scale = dk ** -0.5

    def one_block(qi):
        s = jnp.einsum('bqhd,bkhd->bhqk', qi, k).astype(jnp.float32) * scale
        p = jax.nn.softmax(s, axis=-1).astype(v.dtype)
        return jnp.einsum('bhqk,bkhd->bqhd', p, v)

    out = lax.map(one_block, qb)
    return jnp.moveaxis(out, 0, 1).reshape(bsz, tq, nh * v.shape[-1])

def _mla_mixer(h_lat, h_ctx, cos, sin, w_in, q_norm, kv_norm, w_uq, w_ukv, q_gain, k_gain,
               w_out, with_ctx_out):
    def queries(cq, rotate):
        q = (_rms(cq) * q_norm) @ w_uq
        q = _rms(q.reshape(*q.shape[:2], MLA_HEADS, MLA_QK)) * q_gain
        return _rope_tail(q, cos, sin) if rotate else q

    def keys_values(ckv, k_rope, rotate):
        ukv = ((_rms(ckv) * kv_norm) @ w_ukv).reshape(*ckv.shape[:2], MLA_HEADS, MLA_NOPE + MLA_V)
        k_nope, v = ukv[..., :MLA_NOPE], ukv[..., MLA_NOPE:]
        k_rope = jnp.broadcast_to(k_rope[:, :, None, :], (*k_nope.shape[:3], MLA_ROPE))
        k = _rms(jnp.concatenate([k_nope, k_rope], axis=-1)) * k_gain
        return (_rope_tail(k, cos, sin) if rotate else k), v

    cq_l, ckv_l, kr_l = _split_cols(h_lat @ w_in, (MLA_Q_LORA, MLA_KV_LORA, MLA_ROPE))
    ckv_c, kr_c = _split_cols(h_ctx @ w_in[:, MLA_Q_LORA:], (MLA_KV_LORA, MLA_ROPE))
    k_l, v_l = keys_values(ckv_l, kr_l, True)
    k_c, v_c = keys_values(ckv_c, kr_c, False)
    k_all = jnp.concatenate([k_c, k_l], axis=1)
    v_all = jnp.concatenate([v_c, v_l], axis=1)
    y_lat = _block_attention(queries(cq_l, True), k_all, v_all) @ w_out
    y_ctx = None
    if with_ctx_out:
        q_c = queries(h_ctx @ w_in[:, :MLA_Q_LORA], False)
        y_ctx = _block_attention(q_c, k_c, v_c) @ w_out
    return y_lat, y_ctx

def _conv_ffn(h, w_in, conv_w, conv_b, w_out):
    g, val = jnp.split(h @ w_in, 2, axis=-1)
    return (jax.nn.gelu(_dwconv(g, conv_w, conv_b), approximate=True) * val) @ w_out

def first_inputs(seed: int = 0) -> dict:
    key = jax.random.key(seed)
    ks = iter(jax.random.split(key, 32))
    n_even = (DEPTH + 1) // 2
    n_odd = DEPTH // 2
    f32 = jnp.float32

    def nrm(shape, scale):
        return jax.random.normal(next(ks), shape, f32) * scale

    def gain(shape):
        return 1.0 + nrm(shape, 0.1)

    inp = {}
    inp['x'] = nrm((BATCH, SEQ, D_MODEL), 1.0)
    inp['c'] = nrm((BATCH, D_MODEL), 1.0)
    inp['ctx'] = nrm((BATCH, CTX_LEN, D_MODEL), 1.0)
    inp['c_ctx'] = nrm((D_MODEL,), 1.0)
    inp['ada_w'] = nrm((DEPTH, D_MODEL, 6 * D_MODEL), 0.5 * D_MODEL ** -0.5)
    inp['ada_b'] = nrm((DEPTH, 6 * D_MODEL), 0.02)
    inp['ab_w_in'] = nrm((n_even, D_MODEL, AB_IN), D_MODEL ** -0.5)
    ig = nrm((n_even, 2, 1, MLSTM_HEADS), 0.1)
    fg = jnp.linspace(3.0, 6.0, MLSTM_HEADS, dtype=f32) + nrm((n_even, 2, 1, MLSTM_HEADS), 0.1)
    inp['ab_gate_bias'] = jnp.concatenate([ig, fg], axis=2).reshape(n_even, 4 * MLSTM_HEADS)
    inp['ab_conv_w'] = nrm((n_even, CONV_WIDTH, CONV_DIM), CONV_WIDTH ** -0.5)
    inp['ab_conv_b'] = nrm((n_even, CONV_DIM), 0.02)
    inp['ab_ln_g'] = gain((n_even, CONV_DIM))
    inp['ab_ln_b'] = nrm((n_even, CONV_DIM), 0.02)
    inp['ab_head_gain'] = gain((n_even, MLSTM_HEADS * MLSTM_V))
    inp['ab_w_out'] = nrm((n_even, AB_OUT, D_MODEL), AB_OUT ** -0.5)
    inp['mla_w_in'] = nrm((n_odd, D_MODEL, MLA_IN), D_MODEL ** -0.5)
    inp['mla_q_norm'] = gain((n_odd, MLA_Q_LORA))
    inp['mla_kv_norm'] = gain((n_odd, MLA_KV_LORA))
    inp['mla_w_uq'] = nrm((n_odd, MLA_Q_LORA, MLA_HEADS * MLA_QK), MLA_Q_LORA ** -0.5)
    inp['mla_w_ukv'] = nrm((n_odd, MLA_KV_LORA, MLA_HEADS * (MLA_NOPE + MLA_V)), MLA_KV_LORA ** -0.5)
    inp['mla_q_gain'] = gain((n_odd, MLA_QK))
    inp['mla_k_gain'] = gain((n_odd, MLA_QK))
    inp['mla_w_out'] = nrm((n_odd, MLA_HEADS * MLA_V, D_MODEL), (MLA_HEADS * MLA_V) ** -0.5)
    inp['ffn_w_in'] = nrm((DEPTH, D_MODEL, 2 * FFN_DIM), D_MODEL ** -0.5)
    inp['ffn_conv_w'] = nrm((DEPTH, FFN_CONV_WIDTH, FFN_DIM), FFN_CONV_WIDTH ** -0.5)
    inp['ffn_conv_b'] = nrm((DEPTH, FFN_DIM), 0.02)
    inp['ffn_w_out'] = nrm((DEPTH, FFN_DIM, D_MODEL), FFN_DIM ** -0.5)
    return inp

def first_block(x, c, ctx, c_ctx, ada_w, ada_b, ab_w_in, ab_gate_bias, ab_conv_w, ab_conv_b,
              ab_ln_g, ab_ln_b, ab_head_gain, ab_w_out, mla_w_in, mla_q_norm, mla_kv_norm,
              mla_w_uq, mla_w_ukv, mla_q_gain, mla_k_gain, mla_w_out, ffn_w_in, ffn_conv_w,
              ffn_conv_b, ffn_w_out):
    rows = x.shape[1] // GRID_W
    cos, sin = _axial_rope_tables(rows)
    xl, xc = x, ctx
    for layer in range(DEPTH):
        last = layer == DEPTH - 1
        j = layer // 2
        mod_l = jnp.split((jax.nn.silu(c) @ ada_w[layer] + ada_b[layer])[:, None, :], 6, axis=-1)
        mod_c = jnp.split(jax.nn.silu(c_ctx) @ ada_w[layer] + ada_b[layer], 6, axis=-1)
        h_lat = _modulate(xl, mod_l[0], mod_l[1])
        h_ctx = _modulate(xc, mod_c[0], mod_c[1])
        if layer % 2 == 0:
            y_lat, y_ctx = _conformer_mlstm_mixer(
                h_lat, h_ctx, ab_w_in[j], ab_gate_bias[j], ab_conv_w[j], ab_conv_b[j],
                ab_ln_g[j], ab_ln_b[j], ab_head_gain[j], ab_w_out[j], not last)
        else:
            y_lat, y_ctx = _mla_mixer(
                h_lat, h_ctx, cos, sin, mla_w_in[j], mla_q_norm[j], mla_kv_norm[j], mla_w_uq[j],
                mla_w_ukv[j], mla_q_gain[j], mla_k_gain[j], mla_w_out[j], not last)
        xl = xl + mod_l[2] * y_lat
        xl = xl + mod_l[5] * _conv_ffn(_modulate(xl, mod_l[3], mod_l[4]), ffn_w_in[layer],
                                       ffn_conv_w[layer], ffn_conv_b[layer], ffn_w_out[layer])
        if not last:
            xc = xc + mod_c[2] * y_ctx
            xc = xc + mod_c[5] * _conv_ffn(_modulate(xc, mod_c[3], mod_c[4]), ffn_w_in[layer],
                                           ffn_conv_w[layer], ffn_conv_b[layer], ffn_w_out[layer])
    return xl


HEAD_DIM = 64
ROPE_THETA = 10000.0
SWA_HEADS = 16
SWA_KV_HEADS = 4
SWA_WINDOW = 128
SWA_BLOCK = 128
SWA_Q = SWA_HEADS * HEAD_DIM
SWA_KV = SWA_KV_HEADS * HEAD_DIM
SWA_IN = SWA_Q + 2 * SWA_KV
NSA_HEADS = 16
NSA_KV_HEADS = 4
CMP_LEN = 32
CMP_STRIDE = 16
CMP_HIDDEN = 256
SEL_BLOCK = 64
SEL_TOPN = 16
NSA_WINDOW = 512
NSA_QCHUNK = 32
SEL_FORCE = 1e4
NSA_Q = NSA_HEADS * HEAD_DIM
NSA_KV = NSA_KV_HEADS * HEAD_DIM
NSA_IN = NSA_Q + 6 * NSA_KV + 3 * NSA_HEADS
D_FF = 3584
N_EXPERTS = 8
TOP_K = 2
DN_ALPHA = (2 * DEPTH) ** 0.25
DN_BETA = (8 * DEPTH) ** -0.25
LN_EPS = 1e-5
NEG_INF = -1e30
N_EVEN = (DEPTH + 1) // 2
N_ODD = DEPTH // 2


def _layer_norm_2(x, g, b):
    xf = x.astype(jnp.float32)
    mu = jnp.mean(xf, axis=-1, keepdims=True)
    var = jnp.mean(jnp.square(xf - mu), axis=-1, keepdims=True)
    return ((xf - mu) * lax.rsqrt(var + LN_EPS)).astype(x.dtype) * g + b

def _rope_tables(seq):
    inv = 1.0 / (ROPE_THETA ** (jnp.arange(0, HEAD_DIM, 2, dtype=jnp.float32) / HEAD_DIM))
    ang = jnp.arange(seq, dtype=jnp.float32)[:, None] * inv[None, :]
    return jnp.cos(ang), jnp.sin(ang)

def _rope(x, cos, sin):
    c = cos[None, :, None, :].astype(x.dtype)
    s = sin[None, :, None, :].astype(x.dtype)
    x1, x2 = jnp.split(x, 2, axis=-1)
    return jnp.concatenate([x1 * c - x2 * s, x2 * c + x1 * s], axis=-1)

def _masked_softmax(s, mask):
    s = jnp.where(mask, s, NEG_INF)
    m = jnp.max(s, axis=-1, keepdims=True)
    p = jnp.where(mask, jnp.exp(s - m), 0.0)
    return p / jnp.maximum(jnp.sum(p, axis=-1, keepdims=True), 1e-30)

def _swa_sink_attention(x, w_in, w_out, sinks, cos, sin):
    B, S, _ = x.shape
    G = SWA_HEADS // SWA_KV_HEADS
    nb = S // SWA_BLOCK
    proj = x @ w_in
    q, k, v = jnp.split(proj, [SWA_Q, SWA_Q + SWA_KV], axis=-1)
    q = _rope(q.reshape(B, S, SWA_HEADS, HEAD_DIM), cos, sin)
    k = _rope(k.reshape(B, S, SWA_KV_HEADS, HEAD_DIM), cos, sin)
    v = v.reshape(B, S, SWA_KV_HEADS, HEAD_DIM)
    qb = q.reshape(B, nb, SWA_BLOCK, SWA_KV_HEADS, G, HEAD_DIM)
    kb = k.reshape(B, nb, SWA_BLOCK, SWA_KV_HEADS, HEAD_DIM)
    vb = v.reshape(B, nb, SWA_BLOCK, SWA_KV_HEADS, HEAD_DIM)
    kk = jnp.concatenate([jnp.concatenate([jnp.zeros_like(kb[:, :1]), kb[:, :-1]], axis=1), kb], axis=2)
    vv = jnp.concatenate([jnp.concatenate([jnp.zeros_like(vb[:, :1]), vb[:, :-1]], axis=1), vb], axis=2)
    scores = jnp.einsum('bnqkgd,bnskd->bnkgqs', qb, kk).astype(jnp.float32) * (HEAD_DIM ** -0.5)
    n_i = jnp.arange(nb)[:, None, None]
    q_i = jnp.arange(SWA_BLOCK)[None, :, None] + SWA_BLOCK
    s_i = jnp.arange(2 * SWA_BLOCK)[None, None, :]
    diff = q_i - s_i
    abs_s = n_i * SWA_BLOCK - SWA_BLOCK + s_i
    mask = ((diff >= 0) & (diff < SWA_WINDOW) & (abs_s >= 0))[None, :, None, None]
    sink = sinks.astype(jnp.float32).reshape(1, 1, SWA_KV_HEADS, G, 1, 1)
    s = jnp.where(mask, scores, NEG_INF)
    m = jnp.maximum(jnp.max(s, axis=-1, keepdims=True), sink)
    p = jnp.where(mask, jnp.exp(s - m), 0.0)
    probs = p / (jnp.sum(p, axis=-1, keepdims=True) + jnp.exp(sink - m))
    o = jnp.einsum('bnkgqs,bnskd->bnqkgd', probs.astype(vv.dtype), vv)
    return o.reshape(B, S, SWA_Q) @ w_out

def _overlap_matrix(nc, nsel):
    cs = CMP_STRIDE * np.arange(nc)
    ce = cs + CMP_LEN
    ss = SEL_BLOCK * np.arange(nsel)
    se = ss + SEL_BLOCK
    ov = np.clip(np.minimum(ce[:, None], se[None, :]) - np.maximum(cs[:, None], ss[None, :]), 0, None)
    return jnp.asarray(ov / CMP_STRIDE, dtype=jnp.float32)

def _nsa_attention(x, w_in, w_out, pos_k, pos_v, ck_w1, ck_w2, cv_w1, cv_w2, cos, sin):
    B, S, _ = x.shape
    Hkv = NSA_KV_HEADS
    G = NSA_HEADS // NSA_KV_HEADS
    scale = HEAD_DIM ** -0.5
    proj = x @ w_in
    splits = [NSA_Q + i * NSA_KV for i in range(7)]
    q, kc, vc, ks, vs, kw, vw, gl = jnp.split(proj, splits, axis=-1)
    q = _rope(q.reshape(B, S, NSA_HEADS, HEAD_DIM), cos, sin)
    kc = _rope(kc.reshape(B, S, Hkv, HEAD_DIM), cos, sin)
    ks = _rope(ks.reshape(B, S, Hkv, HEAD_DIM), cos, sin)
    kw = _rope(kw.reshape(B, S, Hkv, HEAD_DIM), cos, sin)
    vc = vc.reshape(B, S, Hkv, HEAD_DIM)
    vs = vs.reshape(B, S, Hkv, HEAD_DIM)
    vw = vw.reshape(B, S, Hkv, HEAD_DIM)
    gates = jax.nn.sigmoid(gl).reshape(B, S, Hkv, G, 3)

    nc = (S - CMP_LEN) // CMP_STRIDE + 1
    idx = CMP_STRIDE * np.arange(nc)[:, None] + np.arange(CMP_LEN)[None, :]

    def compress(t, pos, w1, w2):
        blk = t[:, idx] + pos[None, None, :, None, :]
        flat = blk.transpose(0, 1, 3, 2, 4).reshape(B, nc, Hkv, CMP_LEN * HEAD_DIM)
        return jax.nn.gelu(flat @ w1) @ w2

    kcc = compress(kc, pos_k, ck_w1, ck_w2)
    vcc = compress(vc, pos_v, cv_w1, cv_w2)
    cmp_end = jnp.asarray(idx[:, -1])

    nsel = S // SEL_BLOCK
    topn = min(SEL_TOPN, nsel)
    ov = _overlap_matrix(nc, nsel)
    kblk = ks.reshape(B, nsel, SEL_BLOCK, Hkv, HEAD_DIM).transpose(0, 3, 1, 2, 4)
    vblk = vs.reshape(B, nsel, SEL_BLOCK, Hkv, HEAD_DIM).transpose(0, 3, 1, 2, 4)
    b_i = jnp.arange(B)[:, None, None, None]
    h_i = jnp.arange(Hkv)[None, :, None, None]
    blk_ids = jnp.arange(nsel)

    kw_pad = jnp.pad(kw, ((0, 0), (NSA_WINDOW, 0), (0, 0), (0, 0)))
    vw_pad = jnp.pad(vw, ((0, 0), (NSA_WINDOW, 0), (0, 0), (0, 0)))

    def chunk(ci):
        c0 = ci * NSA_QCHUNK
        tpos = c0 + jnp.arange(NSA_QCHUNK)
        qc = lax.dynamic_slice_in_dim(q, c0, NSA_QCHUNK, axis=1).reshape(B, NSA_QCHUNK, Hkv, G, HEAD_DIM)
        s_c = jnp.einsum('bqkgd,bckd->bkgqc', qc, kcc).astype(jnp.float32) * scale
        p_c = _masked_softmax(s_c, cmp_end[None, :] <= tpos[:, None])
        o_c = jnp.einsum('bkgqc,bckd->bqkgd', p_c.astype(vcc.dtype), vcc)
        imp = jnp.sum(p_c, axis=2) @ ov
        cur = (tpos // SEL_BLOCK)[:, None]
        forced = (blk_ids[None, :] == 0) | (blk_ids[None, :] == cur) | (blk_ids[None, :] == cur - 1)
        imp = jnp.where(forced, SEL_FORCE, imp)
        imp = jnp.where(blk_ids[None, :] <= cur, imp, -1.0)
        _, sel = lax.top_k(imp, topn)
        ksel = kblk[b_i, h_i, sel].reshape(B, Hkv, NSA_QCHUNK, topn * SEL_BLOCK, HEAD_DIM)
        vsel = vblk[b_i, h_i, sel].reshape(B, Hkv, NSA_QCHUNK, topn * SEL_BLOCK, HEAD_DIM)
        spos = (sel[..., None] * SEL_BLOCK + jnp.arange(SEL_BLOCK)).reshape(B, Hkv, NSA_QCHUNK, topn * SEL_BLOCK)
        mask_s = (spos <= tpos[None, None, :, None])[:, :, None]
        s_s = jnp.einsum('bqkgd,bkqsd->bkgqs', qc, ksel).astype(jnp.float32) * scale
        p_s = _masked_softmax(s_s, mask_s)
        o_s = jnp.einsum('bkgqs,bkqsd->bqkgd', p_s.astype(vsel.dtype), vsel)
        kwc = lax.dynamic_slice_in_dim(kw_pad, c0, NSA_WINDOW + NSA_QCHUNK, axis=1)
        vwc = lax.dynamic_slice_in_dim(vw_pad, c0, NSA_WINDOW + NSA_QCHUNK, axis=1)
        wpos = c0 - NSA_WINDOW + jnp.arange(NSA_WINDOW + NSA_QCHUNK)
        diff = tpos[:, None] - wpos[None, :]
        mask_w = (diff >= 0) & (diff < NSA_WINDOW) & (wpos[None, :] >= 0)
        s_w = jnp.einsum('bqkgd,bskd->bkgqs', qc, kwc).astype(jnp.float32) * scale
        p_w = _masked_softmax(s_w, mask_w)
        o_w = jnp.einsum('bkgqs,bskd->bqkgd', p_w.astype(vwc.dtype), vwc)
        g = lax.dynamic_slice_in_dim(gates, c0, NSA_QCHUNK, axis=1)
        o = g[..., 0:1] * o_c + g[..., 1:2] * o_s + g[..., 2:3] * o_w
        return o.reshape(B, NSA_QCHUNK, NSA_Q)

    outs = lax.map(chunk, jnp.arange(S // NSA_QCHUNK))
    o = outs.transpose(1, 0, 2, 3).reshape(B, S, NSA_Q)
    return o @ w_out

def _swiglu(x, w_gate, w_up, w_down):
    return (jax.nn.silu(x @ w_gate) * (x @ w_up)) @ w_down

def _moe(x, router, w_gate, w_up, w_down):
    B, S, D = x.shape
    xt = x.reshape(B * S, D)
    logits = (xt @ router).astype(jnp.float32)
    vals, ids = lax.top_k(logits, TOP_K)
    w = jax.nn.softmax(vals, axis=-1)
    gate = jnp.sum(jax.nn.one_hot(ids, N_EXPERTS, dtype=jnp.float32) * w[..., None], axis=1)
    out = jnp.zeros_like(xt)
    for e in range(N_EXPERTS):
        out = out + gate[:, e:e + 1].astype(xt.dtype) * _swiglu(xt, w_gate[e], w_up[e], w_down[e])
    return out.reshape(B, S, D)

def _normal(k, shape, scale):
    return jax.random.normal(k, shape, jnp.float32) * scale

def second_inputs(seed: int = 0) -> dict:
    key = jax.random.key(seed)
    ks = jax.random.split(key, 24)
    D = D_MODEL
    a_col = jnp.concatenate([jnp.ones((SWA_Q + SWA_KV,), jnp.float32), jnp.full((SWA_KV,), DN_BETA, jnp.float32)])
    b_col = jnp.concatenate([
        jnp.ones((NSA_Q + NSA_KV,), jnp.float32),
        jnp.full((NSA_KV,), DN_BETA, jnp.float32),
        jnp.ones((NSA_KV,), jnp.float32),
        jnp.full((NSA_KV,), DN_BETA, jnp.float32),
        jnp.ones((NSA_KV,), jnp.float32),
        jnp.full((NSA_KV,), DN_BETA, jnp.float32),
        jnp.ones((3 * NSA_HEADS,), jnp.float32)])
    return {
        'x': _normal(ks[0], (BATCH, SEQ, D), 1.0),
        'a_w_in': _normal(ks[1], (N_EVEN, D, SWA_IN), D ** -0.5) * a_col,
        'a_w_out': _normal(ks[2], (N_EVEN, SWA_Q, D), DN_BETA * SWA_Q ** -0.5),
        'a_sinks': _normal(ks[3], (N_EVEN, SWA_HEADS), 1.0),
        'b_w_in': _normal(ks[4], (N_ODD, D, NSA_IN), D ** -0.5) * b_col,
        'b_w_out': _normal(ks[5], (N_ODD, NSA_Q, D), DN_BETA * NSA_Q ** -0.5),
        'b_cmp_pos_k': _normal(ks[6], (N_ODD, CMP_LEN, HEAD_DIM), 0.1),
        'b_cmp_pos_v': _normal(ks[7], (N_ODD, CMP_LEN, HEAD_DIM), 0.1),
        'b_cmp_k_w1': _normal(ks[8], (N_ODD, CMP_LEN * HEAD_DIM, CMP_HIDDEN), (CMP_LEN * HEAD_DIM) ** -0.5),
        'b_cmp_k_w2': _normal(ks[9], (N_ODD, CMP_HIDDEN, HEAD_DIM), CMP_HIDDEN ** -0.5),
        'b_cmp_v_w1': _normal(ks[10], (N_ODD, CMP_LEN * HEAD_DIM, CMP_HIDDEN), (CMP_LEN * HEAD_DIM) ** -0.5),
        'b_cmp_v_w2': _normal(ks[11], (N_ODD, CMP_HIDDEN, HEAD_DIM), CMP_HIDDEN ** -0.5),
        'ffn_w_gate': _normal(ks[12], (N_EVEN, D, D_FF), D ** -0.5),
        'ffn_w_up': _normal(ks[13], (N_EVEN, D, D_FF), D ** -0.5),
        'ffn_w_down': _normal(ks[14], (N_EVEN, D_FF, D), DN_BETA * D_FF ** -0.5),
        'moe_router': _normal(ks[15], (N_ODD, D, N_EXPERTS), D ** -0.5),
        'moe_w_gate': _normal(ks[16], (N_ODD, N_EXPERTS, D, D_FF), D ** -0.5),
        'moe_w_up': _normal(ks[17], (N_ODD, N_EXPERTS, D, D_FF), D ** -0.5),
        'moe_w_down': _normal(ks[18], (N_ODD, N_EXPERTS, D_FF, D), DN_BETA * D_FF ** -0.5),
        'ln_gain': 1.0 + _normal(ks[19], (DEPTH, 2, D), 0.02),
        'ln_bias': _normal(ks[20], (DEPTH, 2, D), 0.02),
    }

def second_block(x, a_w_in, a_w_out, a_sinks, b_w_in, b_w_out, b_cmp_pos_k, b_cmp_pos_v,
              b_cmp_k_w1, b_cmp_k_w2, b_cmp_v_w1, b_cmp_v_w2, ffn_w_gate, ffn_w_up, ffn_w_down,
              moe_router, moe_w_gate, moe_w_up, moe_w_down, ln_gain, ln_bias):
    cos, sin = _rope_tables(x.shape[1])
    for i in range(DEPTH):
        j = i // 2
        if i % 2 == 0:
            h = _swa_sink_attention(x, a_w_in[j], a_w_out[j], a_sinks[j], cos, sin)
        else:
            h = _nsa_attention(x, b_w_in[j], b_w_out[j], b_cmp_pos_k[j], b_cmp_pos_v[j],
                               b_cmp_k_w1[j], b_cmp_k_w2[j], b_cmp_v_w1[j], b_cmp_v_w2[j], cos, sin)
        x = _layer_norm_2(DN_ALPHA * x + h, ln_gain[i, 0], ln_bias[i, 0])
        if i % 2 == 0:
            f = _swiglu(x, ffn_w_gate[j], ffn_w_up[j], ffn_w_down[j])
        else:
            f = _moe(x, moe_router[j], moe_w_gate[j], moe_w_up[j], moe_w_down[j])
        x = _layer_norm_2(DN_ALPHA * x + f, ln_gain[i, 1], ln_bias[i, 1])
    return x


def setup_inputs(seed=0):
    out = dict(first_inputs(seed))
    for name, value in second_inputs(seed + 1).items():
        if name != "x":
            out[name + "_2"] = value
    return out


def reference(
    x, c, ctx, c_ctx, ada_w, ada_b, ab_w_in, ab_gate_bias, ab_conv_w, ab_conv_b, ab_ln_g,
    ab_ln_b, ab_head_gain, ab_w_out, mla_w_in, mla_q_norm, mla_kv_norm, mla_w_uq, mla_w_ukv,
    mla_q_gain, mla_k_gain, mla_w_out, ffn_w_in, ffn_conv_w, ffn_conv_b, ffn_w_out, a_w_in_2,
    a_w_out_2, a_sinks_2, b_w_in_2, b_w_out_2, b_cmp_pos_k_2, b_cmp_pos_v_2, b_cmp_k_w1_2,
    b_cmp_k_w2_2, b_cmp_v_w1_2, b_cmp_v_w2_2, ffn_w_gate_2, ffn_w_up_2, ffn_w_down_2,
    moe_router_2, moe_w_gate_2, moe_w_up_2, moe_w_down_2, ln_gain_2, ln_bias_2,
):
    x = first_block(
        x, c, ctx, c_ctx, ada_w, ada_b, ab_w_in, ab_gate_bias, ab_conv_w, ab_conv_b, ab_ln_g,
        ab_ln_b, ab_head_gain, ab_w_out, mla_w_in, mla_q_norm, mla_kv_norm, mla_w_uq, mla_w_ukv,
        mla_q_gain, mla_k_gain, mla_w_out, ffn_w_in, ffn_conv_w, ffn_conv_b, ffn_w_out,
    )
    return second_block(
        x, a_w_in_2, a_w_out_2, a_sinks_2, b_w_in_2, b_w_out_2, b_cmp_pos_k_2, b_cmp_pos_v_2,
        b_cmp_k_w1_2, b_cmp_k_w2_2, b_cmp_v_w1_2, b_cmp_v_w2_2, ffn_w_gate_2, ffn_w_up_2,
        ffn_w_down_2, moe_router_2, moe_w_gate_2, moe_w_up_2, moe_w_down_2, ln_gain_2,
        ln_bias_2,
    )


_drawn_inputs = setup_inputs


def setup_inputs(seed=0):
    import zlib

    import numpy as np

    out = dict(_drawn_inputs(seed))
    spreads = {}
    factors = {'ab_conv_b': 6.993,
     'ab_ln_b': 8.0,
     'ab_head_gain': 3.324,
     'mla_q_norm': 7.595,
     'mla_kv_norm': 4.507,
     'mla_q_gain': 8.0,
     'mla_k_gain': 8.0,
     'ffn_conv_b': 6.928,
     'a_sinks_2': 22.32,
     'b_cmp_pos_k_2': 8.0,
     'b_cmp_pos_v_2': 3.825,
     'b_cmp_k_w1_2': 4.328,
     'b_cmp_k_w2_2': 3.83}
    for name, (base, spread) in spreads.items():
        noise = np.random.default_rng([zlib.crc32(name.encode()), seed]).standard_normal(out[name].shape)
        drawn = base * np.exp(spread * noise) if base else spread * noise
        out[name] = jnp.asarray(drawn.astype(out[name].dtype))
    for name, factor in factors.items():
        out[name] = (out[name] * factor).astype(out[name].dtype)
    return out
```

```python
import math

import numpy as np

import concourse.bass as bass
from concourse import mybir
from concourse.alu_op_type import AluOpType as ALU

F32 = mybir.dt.float32
BF16 = mybir.dt.bfloat16
U32 = mybir.dt.uint32
ACT = mybir.ActivationFunctionType
AX = mybir.AxisListType

P = 128
D = 1024
KD = D // P
T = 256
TT = T // P
NTOK = 2 * T
CONV, TAPS = 512, 31
PAD = (TAPS - 1) // 2
HEADS_M, QK_M, V_M = 4, 64, 128
H_MLA, NOPE, ROPE, V_MLA = 16, 64, 32, 64
QK_MLA = NOPE + ROPE
QL, KVL = 512, 256
FFN = 2816
FC = FFN // P
H2, HD, KV2 = 16, 64, 4
G2 = H2 // KV2
FF2 = 3584
F2 = FF2 // P
NEXP = 8
CMP_LEN, CMP_STRIDE, CMP_HID = 32, 16, 256
NCMP = (T - CMP_LEN) // CMP_STRIDE + 1
LP = CMP_LEN * HD // P
ALPHA = (2 * 2) ** 0.25
NEG = -1e30

NS = 7
SLOT = 2048
UNIT = KD * P
DUNIT = 256
UPS = SLOT // UNIT
DPS = SLOT // DUNIT
DQ = D // DUNIT

PLAN = [
    ("ada0", 24), ("ab", 11), ("ada1", 24), ("ab_out", 4),
    ("ffn0_up", FC), ("ffn0_down", FC * DQ // DPS),
    ("mla_in", 3), ("mla_uq", 3), ("mla_ukv", 2), ("mla_out", 4),
    ("ffn1_up", FC), ("ffn1_down", FC * DQ // DPS),
    ("swa_in", 6), ("swa_out", 4),
    ("swiglu_up", F2), ("swiglu_down", F2 * DQ // DPS),
    ("nsa_in", 10), ("nsa_cmp", 4), ("nsa_out", 4),
    ("moe", NEXP * (F2 + F2 * DQ // DPS)),
]
BASE = {}
NSLOT = 0
for _name, _count in PLAN:
    BASE[_name] = NSLOT
    NSLOT += _count

TABLE = [
    ("c", 16), ("ada_b", 96), ("conv_w", 4 * TAPS), ("conv_b", 4), ("ln_g", 4), ("ln_b", 4),
    ("head_gain", 4), ("gate_b", 1), ("q_norm", 4), ("kv_norm", 2), ("q_gain", QK_MLA),
    ("k_gain", QK_MLA), ("ffn_cw", 2 * FC * 3), ("ffn_cb", 2 * FC), ("kr_w", KD * ROPE),
    ("ng_w", KD * 48), ("w2k", 2 * P), ("w2v", 2 * HD), ("router", KD * NEXP), ("sinks", H2),
    ("pos_k", LP), ("pos_v", LP), ("ln2_g", 4 * KD), ("ln2_b", 4 * KD),
    ("ident", P), ("over1024", P), ("over512", P), ("over256", P),
    ("rot", P), ("dup0", P), ("dup1", P), ("rdup0", P), ("rdup1", P),
    ("cos2", T), ("sin2", T), ("cos1", TT * 16), ("sin1", TT * 16),
    ("causal", P), ("band", P), ("m_mask", 2 * P), ("cmp_mask", TT * 16), ("cmp_valid", TT),
    ("iota", NEXP), ("eps6", 1), ("eps5", 1),
]
COL = {}
NTAB = 0
for _name, _count in TABLE:
    COL[_name] = (NTAB, _count)
    NTAB += _count

ARENA = 24600


def program(nc, stream, table, x_in, out, upto=None):
    ctx_sems = {}

    def sem(name):
        if name not in ctx_sems:
            ctx_sems[name] = nc.alloc_semaphore(name)
        return ctx_sems[name]

    ring = nc.alloc_sbuf_tensor("ring", [P, NS, SLOT], F32)
    x = nc.alloc_sbuf_tensor("x", [P, KD, NTOK], F32)
    h = nc.alloc_sbuf_tensor("h", [P, KD, NTOK], F32)
    tab = nc.alloc_sbuf_tensor("tab", [P, NTAB], F32)
    mods = nc.alloc_sbuf_tensor("mods", [P, 2, 48, 2], F32)
    silu_c = nc.alloc_sbuf_tensor("silu_c", [P, KD, 2], F32)
    ident_b = nc.alloc_sbuf_tensor("ident_b", [P, P], BF16)
    causal_b = nc.alloc_sbuf_tensor("causal_b", [P, P], BF16)
    band_b = nc.alloc_sbuf_tensor("band_b", [P, P], BF16)
    cmpm_b = nc.alloc_sbuf_tensor("cmpm_b", [P, TT * 16], BF16)
    arena = nc.alloc_sbuf_tensor("arena", [P, ARENA], F32)
    ps = nc.alloc_psum_tensor("ps", [P, 8, 512], F32)

    def col(name):
        a, n = COL[name]
        return tab[:, a:a + n]

    def carve(*sizes):
        at, found = 0, []
        for n in sizes:
            found.append(arena[:, at:at + n])
            at += n
        assert at <= ARENA, at
        return found

    ident = col("ident")
    table_ready, x_ready = sem("table_ready"), sem("x_ready")
    masks_ready, slot_read, out_stored = sem("masks_ready"), sem("slot_read"), sem("out_stored")
    weights_ready = [sem(f"weights_ready_{s}") for s in range(NS)]

    class Steps:

        def __init__(self, eng, name):
            self.eng, self.sem, self.n = eng, sem(name), 0

        def add(self, ins):
            ins.then_inc(self.sem, 1)
            self.n += 1
            return self.n

        def settle(self, n=None):
            self.eng.wait_ge(self.sem, self.n if n is None else n)

    class Slots:

        def __init__(self, pe):
            self.pe, self.n = pe, 0

        def take(self):
            s = self.n % NS
            self.pe.wait_ge(weights_ready[s], 16 * (self.n // NS + 1))
            self.n += 1
            return ring[:, s, :]

    taken = {}
    signals = {}

    class Signals:

        def __init__(self, kind, name, **adds):
            self.kind = kind
            self.base = {k: taken.get((kind, k), 0) for k in adds}
            for k, n in adds.items():
                taken[kind, k] = self.base[k] + n
            signals[name] = self

        def __getitem__(self, key):
            return sem(f"{self.kind}_{key}")

        def wait(self, eng, key, n):
            eng.wait_ge(self[key], self.base[key] + n)

    def slots_read(eng, stage, n):
        eng.wait_ge(slot_read, BASE[stage] + n)

    def units(slot):
        return slot.rearrange("p (u k c) -> p u k c", u=UPS, k=KD)

    stages = []

    def start():
        def scalar(act):
            act.eng.wait_ge(table_ready, 16)
            nc.scalar.activation(silu_c[:, :, :], col("c").rearrange("p (k s) -> p k s", k=KD),
                                 ACT.Silu).then_inc(sem("silu_c_ready"), 1)

        def vector(dve):
            dve.eng.wait_ge(table_ready, 16)
            nc.vector.tensor_copy(ident_b[:, :], ident)
            nc.vector.tensor_copy(causal_b[:, :], col("causal"))
            nc.vector.tensor_copy(band_b[:, :], col("band"))
            nc.vector.tensor_copy(cmpm_b[:, :], col("cmp_mask")).then_inc(masks_ready, 1)

        def tensor(pe):
            pe.eng.wait_ge(table_ready, 16)

        return dict(name="start", scalar=scalar, vector=vector, tensor=tensor)

    def ada_products(pe, layer, first, count):
        if first == 0:
            pe.eng.wait_ge(sem("silu_c_ready"), 1)
            if layer == 1:
                pe.eng.wait_ge(sem("mods0_ready"), 1)
        for s in range(first, first + count):
            w = units(pe.slots.take())
            for u in range(UPS):
                blk = s * UPS + u
                for k in range(KD):
                    mm = nc.tensor.matmul(ps[:, 7, 2 * blk:2 * blk + 2], w[:, u, k, :], silu_c[:, k, :],
                                          start=(k == 0), stop=(k == KD - 1))
            mm.then_inc(slot_read, 1)

    def ada_vectors(dve, layer):
        slots_read(dve.eng, f"ada{layer}", 24)
        b = col("ada_b").rearrange("p (l j o) -> p l j o", l=2, o=1)[:, layer]
        dve.add(nc.vector.tensor_tensor(mods[:, layer, :, :], ps[:, 7, 0:96].rearrange("p (j s) -> p j s", s=2),
                                        b.to_broadcast([P, 48, 2]), ALU.add))
        dve.settle()
        v = mods[:, layer, :, :].rearrange("p (a b) s -> p a b s", a=2)[:, :, 8:16, :]
        nc.vector.tensor_scalar(v, v, 1.0, None, ALU.add).then_inc(sem(f"mods{layer}_ready"), 1)

    def ada0():
        return dict(name="ada0", tensor=lambda pe: ada_products(pe, 0, 0, 24),
                    vector=lambda dve: ada_vectors(dve, 0))

    def modulate(name, layer, c0, shift, after):
        W = NTOK - c0
        G = Signals("norm", name, square=KD, meansq=1, std=1, scaled=KD, h=KD * (2 if c0 == 0 else 1))
        segs = [(0, 0), (T, 1)] if c0 == 0 else [(T, 1)]
        sq, std, rstd, tmp = carve(KD * W, W, W, KD * W)
        sq = sq.rearrange("p (k t) -> p k t", k=KD)
        tmp = tmp.rearrange("p (k t) -> p k t", k=KD)

        def scalar(act):
            after(act.eng)
            for k in range(KD):
                nc.scalar.activation(sq[:, k, :], x[:, k, c0:NTOK], ACT.Square)\
                  .then_inc(G["square"], 1)
            G.wait(act.eng, "meansq", 1)
            nc.scalar.activation(std, ps[:, 6, 0:W], ACT.Sqrt, bias=col("eps6")).then_inc(G["std"], 1)
            act.eng.wait_ge(sem(f"mods{layer}_ready"), 1)
            for k in range(KD):
                G.wait(act.eng, "scaled", k + 1)
                for t0, s in segs:
                    nc.scalar.activation(h[:, k, t0:t0 + T], tmp[:, k, t0 - c0:t0 - c0 + T], ACT.Identity,
                                         scale=mods[:, layer, (shift + 1) * 8 + k, s:s + 1],
                                         bias=mods[:, layer, shift * 8 + k, s:s + 1])\
                      .then_inc(G["h"], 1)

        def tensor(pe):
            for k in range(KD):
                G.wait(pe.eng, "square", k + 1)
                mm = nc.tensor.matmul(ps[:, 6, 0:W], col("over1024"), sq[:, k, :],
                                      start=(k == 0), stop=(k == KD - 1))
            mm.then_inc(G["meansq"], 1)

        def vector(dve):
            after(dve.eng)
            G.wait(dve.eng, "std", 1)
            dve.add(nc.vector.reciprocal(rstd, std))
            dve.settle()
            for k in range(KD):
                nc.vector.tensor_tensor(tmp[:, k, :], x[:, k, c0:NTOK], rstd, ALU.mult)\
                  .then_inc(G["scaled"], 1)

        return dict(name=name, tensor=tensor, scalar=scalar, vector=vector)

    def h_block_ready(pe, name, c0, k):
        signals[name].wait(pe.eng, "h", (k + 1) * (2 if c0 == 0 else 1))

    def mixer0():
        UW = T + 2 * PAD
        (u0, u, qk, v1, sig_o, gi, lfs, cum, rows, mx, neg, zero, gcol, ecol, dg, dec, hs, tmp) = carve(
            4 * 2 * UW, 4 * NTOK, 4 * NTOK, 4 * HEADS_M * (V_M + 1), 4 * NTOK, NTOK, NTOK, NTOK, NTOK,
            NTOK, NTOK, NTOK, 4 * P, 32, 4 * P, 2 * 4 * NTOK // 2 * 1, 4 * NTOK, 4 * NTOK)
        u0 = u0.rearrange("p (b s t) -> p b s t", b=4, s=2)
        u = u.rearrange("p (b t) -> p b t", b=4)
        qk = qk.rearrange("p (b t) -> p b t", b=4)
        v1 = v1.rearrange("p (t h v) -> p t h v", t=4, h=HEADS_M)
        sig_o = sig_o.rearrange("p (b t) -> p b t", b=4)
        gcol = gcol.rearrange("p (t r) -> p t r", t=4)
        ecol = ecol.rearrange("p (t d h) -> p t d h", t=4, d=2)
        dg = dg.rearrange("p (j t) -> p j t", j=4)
        dec = dec.rearrange("p (j t) -> p j t", j=4)
        hs = hs.rearrange("p (t h v) -> p t h v", t=4, h=HEADS_M)
        tmp4 = tmp.rearrange("p (t h v) -> p t h v", t=4, h=HEADS_M)
        sg = tmp.rearrange("p (b t) -> p b t", b=4)
        sm = col("m_mask").rearrange("p (d t) -> p d t", d=2)
        small = nc.alloc_sbuf_tensor("m_small", [P, 64], F32)
        spans = {0: {0: [(0, 4)], 1: [(1, 4)], 2: [(2, 4)], 3: [(3, 4)]},
                 1: {0: [(0, 1), (2, 4)], 1: [(0, 4)], 2: [(2, 3)], 3: [(2, 4)]}}
        off = {0: {0: [(1, 4)], 1: [(2, 4)], 2: [(3, 4)], 3: []},
               1: {0: [(2, 4)], 1: [(0, 1), (2, 4)], 2: [], 3: [(2, 3)]}}
        sources = {d: {t: [j for j in range(4) if any(a <= t < b for a, b in spans[d][j])]
                       for t in range(4)} for d in (0, 1)}
        name = "mix0"

        def tensor(pe):
            eng = pe.eng
            for b in range(4):
                w = units(pe.slots.take())
                if b >= 2:
                    eng.wait_ge(sem("conv_in_ready"), b - 1)
                for c in range(2):
                    for k in range(KD):
                        if b == 0 and c == 0:
                            h_block_ready(pe, name + "_mod", 0, k)
                        mm = nc.tensor.matmul(ps[:, 2 * (b % 2) + c, :], w[:, c, k, :], h[:, k, :],
                                              start=(k == 0), stop=(k == KD - 1))
                mm.then_inc(slot_read, 1)
            w = units(pe.slots.take())
            for k in range(KD):
                mm = nc.tensor.matmul(ps[:, 4, :], w[:, 0, k, :], h[:, k, :], start=(k == 0), stop=(k == KD - 1))
            mm.then_inc(slot_read, 1)
            for s, banks in enumerate([(5, 6), (0, 1)]):
                w = units(pe.slots.take())
                if s == 1:
                    eng.wait_ge(sem("conv_in_ready"), 3)
                for c in range(2):
                    for k in range(KD):
                        mm = nc.tensor.matmul(ps[:, banks[c], :], w[:, c, k, :], h[:, k, :],
                                              start=(k == 0), stop=(k == KD - 1))
                mm.then_inc(slot_read, 1)
            eng.wait_ge(sem("conv_in_ready"), 4)
            eng.wait_ge(sem("m_qk_ready"), 2)
            for s in range(2):
                w = pe.slots.take().rearrange("p (k c) -> p k c", k=4)
                for t, bank in enumerate((2, 3, 5, 6)):
                    for k in range(4):
                        mm = nc.tensor.matmul(ps[:, bank, :], h[:, 4 * s + k, t * P:(t + 1) * P], w[:, k, :],
                                              start=(s == 0 and k == 0), stop=(s == 1 and k == 3))
                mm.then_inc(slot_read, 1)
            eng.wait_ge(sem("m_qk_ready"), 4)
            eng.wait_ge(sem("gates_taken"), 1)
            eng.wait_ge(sem("m_v_ready"), 1)
            for s, banks in enumerate([(0, 1), (4, 2)]):
                w = units(pe.slots.take())
                for c in range(2):
                    for k in range(KD):
                        mm = nc.tensor.matmul(ps[:, banks[c], :], w[:, c, k, :], h[:, k, :],
                                              start=(k == 0), stop=(k == KD - 1))
                mm.then_inc(slot_read, 1)
            eng.wait_ge(sem("m_v_ready"), 4)
            eng.wait_ge(sem("m_rows_ready"), 1)
            for t in range(4):
                mm = nc.tensor.transpose(ps[:, 3, t * P:(t + 1) * P], rows[:, t * P:(t + 1) * P], ident)
            mm.then_inc(sem("m_cols_done"), 1)
            for i in range(2 * HEADS_M):
                hd, d = i // 2, i % 2
                half = slice(64 * (hd % 2), 64 * (hd % 2) + 64)
                rr = slice(64 * d, 64 * d + HEADS_M)
                if i == 0:
                    eng.wait_ge(sem("m_sig_o_ready"), 4)
                    eng.wait_ge(sem("m_gcol_ready"), 1)
                if d == 0:
                    if i:
                        eng.wait_ge(sem("m_weights_ready"), i)
                    for j in range(4):
                        t0 = 0 if j < 2 else T
                        mm = nc.tensor.matmul(ps[:, j, t0:NTOK], qk[half, 2 + hd // 2, j * P:(j + 1) * P],
                                              qk[half, hd // 2, t0:NTOK], start=True, stop=True)
                if i:
                    eng.wait_ge(sem("m_decay_ready"), i)
                mm = nc.tensor.matmul(ps[:, 4, :], ident[rr, 64 * d + hd:64 * d + hd + 1].to_broadcast([HEADS_M, P]),
                                      neg[rr, :], start=True, stop=True)
                mm.then_inc(sem("m_scores_done"), 1)
                ada_products(pe, 1, 3 * i, 3)
                eng.wait_ge(sem("m_weights_ready"), i + 1)
                if i:
                    eng.wait_ge(sem("m_h_taken"), i)
                for t in range(4):
                    src = sources[d][t]
                    for n, j in enumerate(src):
                        c = (t % 2) * 256
                        mm = nc.tensor.matmul(ps[:, 5 + t // 2, c:c + V_M + 1], dec[:, j, t * P:(t + 1) * P],
                                              v1[:, j, hd, :], start=(n == 0), stop=(n == len(src) - 1))
                mm.then_inc(sem("m_h_done"), 1)
            eng.wait_ge(sem("conv_done"), 1)
            eng.wait_ge(sem("mods1_ready"), 1)
            for b in range(4):
                mm = nc.tensor.matmul(ps[:, 7, :], col("over512"), u[:, b, :], start=(b == 0), stop=(b == 3))
            mm.then_inc(sem("conv_mean_done"), 1)
            for b in range(4):
                eng.wait_ge(sem("conv_square_ready"), b + 1)
                mm = nc.tensor.matmul(ps[:, 4, :], col("over512"), sg[:, b, :], start=(b == 0), stop=(b == 3))
            mm.then_inc(sem("conv_var_done"), 1)
            eng.wait_ge(sem("m_hs_ready"), 1)
            for hd in range(HEADS_M):
                for t in range(4):
                    mm = nc.tensor.transpose(ps[:, hd, t * P:(t + 1) * P], hs[:, t, hd, :], ident)
                mm.then_inc(sem("m_hT_done"), 1)

        def scalar(act):
            eng = act.eng
            for b in range(4):
                slots_read(eng, "ab", b + 1)
                nc.scalar.activation(sg[:, b, :], ps[:, 2 * (b % 2) + 1, :], ACT.Sigmoid)\
                  .then_inc(sem("conv_gate_ready"), 1)
            slots_read(eng, "ab", 5)
            nc.scalar.activation(gi, ps[:, 4, :], ACT.Identity, bias=col("gate_b")).then_inc(sem("gates_taken"), 1)
            eng.wait_ge(sem("gates_taken"), 1)
            act.add(nc.scalar.activation(lfs, gi, ACT.Abs))
            act.settle()
            act.add(nc.scalar.activation(rows, lfs, ACT.Exp, scale=-1.0))
            act.settle()
            nc.scalar.activation(lfs, rows, ACT.Ln, bias=1.0).then_inc(sem("m_ln_ready"), 1)
            for n, bank in enumerate((5, 6, 0, 1)):
                slots_read(eng, "ab", 6 + n // 2)
                nc.scalar.activation(qk[:, n, :], ps[:, bank, :], ACT.Copy,
                                     scale=(1.0 if n < 2 else QK_M ** -0.5)).then_inc(sem("m_qk_ready"), 1)
            slots_read(eng, "ab", 9)
            for t, bank in enumerate((2, 3, 5, 6)):
                nc.scalar.activation(v1[:, t, :, 0:V_M], ps[:, bank, :].rearrange("p (h v) -> p h v", h=HEADS_M),
                                     ACT.Copy).then_inc(sem("m_v_ready"), 1)
            for n, bank in enumerate((0, 1, 4, 2)):
                slots_read(eng, "ab", 10 + n // 2)
                nc.scalar.activation(sig_o[:, n, :], ps[:, bank, :], ACT.Sigmoid).then_inc(sem("m_sig_o_ready"), 1)
            eng.wait_ge(sem("m_cols_done"), 1)
            nc.scalar.activation(gcol[:, :, :], ps[:, 3, :].rearrange("p (t r) -> p t r", t=4), ACT.Copy)\
              .then_inc(sem("m_gcol_ready"), 1)
            eng.wait_ge(sem("m_gcol_ready"), 1)
            for d in range(2):
                ins = nc.scalar.activation(ecol[:, :, d, :], gcol[:, :, 32 + 64 * d:32 + 64 * d + HEADS_M], ACT.Exp)
            ins.then_inc(sem("m_ecol_ready"), 1)
            for i in range(2 * HEADS_M):
                hd, d = i // 2, i % 2
                eng.wait_ge(sem("m_scores_done"), i + 1)
                if i:
                    eng.wait_ge(sem("m_h_done"), i)
                eng.wait_ge(sem("m_diag_ready"), i + 1)
                for j in range(4):
                    bias = gcol[:, j, 64 * d + hd:64 * d + hd + 1]
                    for a, b in off[d][j]:
                        nc.scalar.activation(dec[:, j, a * P:b * P], ps[:, 4, a * P:b * P], ACT.Exp, bias=bias)
                for j in range(4):
                    ins = nc.scalar.activation(dec[:, j, j * P:(j + 1) * P], dg[:, j, :], ACT.Exp,
                                               bias=gcol[:, j, 64 * d + hd:64 * d + hd + 1])
                ins.then_inc(sem("m_decay_ready"), 1)
            for b in range(4):
                eng.wait_ge(sem("conv_centred"), b + 1)
                nc.scalar.activation(sg[:, b, :], u[:, b, :], ACT.Square).then_inc(sem("conv_square_ready"), 1)
            eng.wait_ge(sem("conv_var_done"), 1)
            nc.scalar.activation(gi, ps[:, 4, :], ACT.Sqrt, bias=col("eps6")).then_inc(sem("conv_std_ready"), 1)
            eng.wait_ge(sem("m_ss_ready"), 1)
            nc.scalar.activation(small[:, 16:32], small[:, 0:16], ACT.Sqrt, scale=1.0 / V_M, bias=col("eps6"))\
              .then_inc(sem("m_rms_ready"), 1)
            for b in range(4):
                eng.wait_ge(sem("conv_scaled"), b + 1)
                nc.scalar.activation(h[:, b, :], u[:, b, :], ACT.Silu, scale=col("ln_g")[:, b:b + 1],
                                     bias=col("ln_b")[:, b:b + 1]).then_inc(sem("mix0_cat"), 1)

        def gpsimd(pool):
            signals["mix0_mod"].wait(pool.eng, "h", 2 * KD)
            nc.gpsimd.memset(u0[:, :, :, 0:PAD], 0.0)
            nc.gpsimd.memset(u0[:, :, :, PAD + T:UW], 0.0)
            nc.gpsimd.memset(v1[:, :, :, V_M:V_M + 1], 1.0)
            nc.gpsimd.memset(zero, 0.0).then_inc(sem("m_borders_ready"), 1)

        def vector(dve):
            eng = dve.eng
            eng.wait_ge(sem("m_borders_ready"), 1)
            for b in range(4):
                eng.wait_ge(sem("conv_gate_ready"), b + 1)
                nc.vector.tensor_tensor(u0[:, b, :, PAD:PAD + T],
                                        ps[:, 2 * (b % 2), :].rearrange("p (s t) -> p s t", s=2),
                                        sg[:, b, :].rearrange("p (s t) -> p s t", s=2), ALU.mult)\
                  .then_inc(sem("conv_in_ready"), 1)
            eng.wait_ge(sem("m_ln_ready"), 1)
            dve.add(nc.vector.tensor_scalar(mx, gi, 0.0, None, ALU.min))
            dve.settle()
            dve.add(nc.vector.tensor_tensor(mx, mx, lfs, ALU.subtract))
            dve.settle()
            dve.add(nc.vector.tensor_copy(lfs[0:4, :], mx[32:36, :]))
            dve.add(nc.vector.tensor_copy(lfs[64:68, :], mx[96:100, :]))
            dve.settle()
            f, g = slice(0, 4), slice(64, 68)
            ctx_r, lat_r = slice(T - 1, None, -1), slice(NTOK - 1, T - 1, -1)
            dve.add(nc.vector.memset(rows, 0.0))
            dve.add(nc.vector.tensor_tensor_scan(cum[f, :], lfs[f, :], zero[f, :], 0.0, ALU.add, ALU.add))
            dve.add(nc.vector.tensor_tensor_scan(cum[g, ctx_r], lfs[g, ctx_r], zero[g, ctx_r], 0.0, ALU.add, ALU.add))
            dve.settle()
            dve.add(nc.vector.tensor_tensor_scan(cum[g, lat_r], lfs[g, lat_r], zero[g, lat_r], cum[g, 0:1],
                                                 ALU.add, ALU.add))
            dve.settle()
            for r in (f, g):
                dve.add(nc.vector.tensor_tensor(rows[r, :], gi[r, :], cum[r, :], ALU.subtract))
            dve.settle()
            dve.add(nc.vector.tensor_tensor_scan(mx[f, :], rows[f, :], rows[f, :], 0.0, ALU.max, ALU.max))
            dve.add(nc.vector.tensor_tensor_scan(mx[g, ctx_r], rows[g, ctx_r], rows[g, ctx_r], 0.0, ALU.max, ALU.max))
            dve.settle()
            dve.add(nc.vector.tensor_tensor_scan(mx[g, lat_r], rows[g, lat_r], rows[g, lat_r], mx[g, 0:1],
                                                 ALU.max, ALU.max))
            dve.settle()
            for r in (f, g):
                nc.vector.tensor_scalar(neg[r, :], mx[r, :], -1.0, None, ALU.mult)
            nc.vector.scalar_tensor_tensor(rows[32:36, :], cum[f, :], -1.0, mx[f, :], ALU.mult, ALU.subtract)
            nc.vector.scalar_tensor_tensor(rows[96:100, :], cum[g, :], -1.0, mx[g, :], ALU.mult, ALU.subtract)\
              .then_inc(sem("m_rows_ready"), 1)

            cw = col("conv_w").rearrange("p (b t) -> p b t", b=4)
            last = [0] * 4

            def taps(a, b_):
                for t in range(a, min(b_, TAPS)):
                    for b in range(4):
                        o = u[:, b, :].rearrange("p (s t) -> p s t", s=2)
                        i = u0[:, b, :, t:t + T]
                        if t == 0:
                            last[b] = dve.add(nc.vector.tensor_scalar(o, i, cw[:, b, 0:1], col("conv_b")[:, b:b + 1],
                                                                      ALU.mult, ALU.add))
                        else:
                            dve.settle(last[b])
                            last[b] = dve.add(nc.vector.scalar_tensor_tensor(o, i, cw[:, b, t:t + 1], o,
                                                                             ALU.mult, ALU.add))

            eng.wait_ge(sem("conv_in_ready"), 4)
            taps(0, 3)
            for i in range(2 * HEADS_M):
                hd, d = i // 2, i % 2
                eng.wait_ge(sem("m_scores_done"), i + 1)
                if i:
                    eng.wait_ge(sem("m_decay_ready"), i)
                nc.vector.tensor_tensor(dg[:, :, :], ps[:, 4, :].rearrange("p (j t) -> p j t", j=4),
                                        sm[:, d:d + 1, :].to_broadcast([P, 4, P]), ALU.add)\
                  .then_inc(sem("m_diag_ready"), 1)
                taps(3 + 4 * i, 5 + 4 * i)
                eng.wait_ge(sem("m_decay_ready"), i + 1)
                for j in range(4):
                    for a, b in spans[d][j]:
                        ins = nc.vector.tensor_tensor(dec[:, j, a * P:b * P], dec[:, j, a * P:b * P],
                                                      ps[:, j, a * P:b * P], ALU.mult)
                ins.then_inc(sem("m_weights_ready"), 1)
                taps(5 + 4 * i, 7 + 4 * i)
                eng.wait_ge(sem("m_h_done"), i + 1)
                if i == 0:
                    eng.wait_ge(sem("m_ecol_ready"), 1)
                o = ps[:, 5:7, :].rearrange("p a (b c) -> p (a b) c", b=2)
                sc = small[:, 32:36].rearrange("p (t o) -> p t o", o=1)
                sc2 = small[:, 36:40].rearrange("p (t o) -> p t o", o=1)
                dve.add(nc.vector.tensor_scalar(sc, o[:, :, V_M:V_M + 1], -1.0, None, ALU.mult))
                dve.settle()
                dve.add(nc.vector.tensor_tensor(sc, o[:, :, V_M:V_M + 1], sc, ALU.max))
                dve.settle()
                dve.add(nc.vector.tensor_tensor(sc, sc, ecol[:, :, d, hd:hd + 1], ALU.max))
                dve.settle()
                dve.add(nc.vector.reciprocal(sc2, sc))
                dve.settle()
                dst = hs if d == 0 else tmp4
                nc.vector.tensor_tensor(dst[:, :, hd, :], o[:, :, 0:V_M], sc2.to_broadcast([P, 4, V_M]), ALU.mult)\
                  .then_inc(sem("m_h_taken"), 1)
                if d == 1:
                    eng.wait_ge(sem("m_h_taken"), i + 1)
                    dve.add(nc.vector.tensor_tensor(hs[:, :, hd, :], hs[:, :, hd, :], tmp4[:, :, hd, :], ALU.add))
            dve.settle()
            nc.vector.tensor_copy(small[:, 60:61], u[:, 3, 0:1]).then_inc(sem("conv_done"), 1)
            ada_vectors(dve, 1)
            dve.add(nc.vector.tensor_tensor(tmp, hs.rearrange("p t h v -> p (t h v)"),
                                            hs.rearrange("p t h v -> p (t h v)"), ALU.mult))
            dve.settle()
            nc.vector.tensor_reduce(small[:, 0:16], tmp.rearrange("p (g v) -> p g v", v=V_M), AX.X, ALU.add)\
              .then_inc(sem("m_ss_ready"), 1)
            eng.wait_ge(sem("conv_mean_done"), 1)
            eng.wait_ge(sem("m_ss_ready"), 1)
            for b in range(4):
                nc.vector.tensor_tensor(u[:, b, :], u[:, b, :], ps[:, 7, :], ALU.subtract)\
                  .then_inc(sem("conv_centred"), 1)
            eng.wait_ge(sem("m_rms_ready"), 1)
            dve.add(nc.vector.reciprocal(small[:, 0:16], small[:, 16:32]))
            dve.settle()
            hg = hs.rearrange("p t h v -> p (t h) v")
            nc.vector.tensor_tensor(hg, hg, small[:, 0:16].rearrange("p (g o) -> p g o", o=1).to_broadcast([P, 16, V_M]),
                                    ALU.mult).then_inc(sem("m_hs_ready"), 1)
            eng.wait_ge(sem("conv_std_ready"), 1)
            dve.add(nc.vector.reciprocal(lfs, gi))
            dve.settle()
            eng.wait_ge(sem("conv_square_ready"), 4)
            for b in range(4):
                nc.vector.tensor_tensor(u[:, b, :], u[:, b, :], lfs, ALU.mult).then_inc(sem("conv_scaled"), 1)
            for hd in range(HEADS_M):
                eng.wait_ge(sem("m_hT_done"), hd + 1)
                nc.vector.scalar_tensor_tensor(h[:, 4 + hd, :], ps[:, hd, :], col("head_gain")[:, hd:hd + 1],
                                               sig_o[:, hd, :], ALU.mult, ALU.mult).then_inc(sem("mix0_cat_h"), 1)

        return dict(name=name, tensor=tensor, scalar=scalar, vector=vector, gpsimd=gpsimd)

    def out_proj(name, plan, c0, ready, layer=None, gate=None, src=None):
        G = Signals("residual", name, x=KD)
        W = NTOK - c0
        src = h if src is None else src

        def tensor(pe):
            ready(pe.eng)
            for s in range(KD // UPS):
                w = units(pe.slots.take())
                for u in range(UPS):
                    for k in range(KD):
                        mm = nc.tensor.matmul(ps[:, s * UPS + u, 0:W], w[:, u, k, :], src[:, k, c0:NTOK],
                                              start=(k == 0), stop=(k == KD - 1))
                mm.then_inc(slot_read, 1)

        def vector(dve):
            for m in range(KD):
                slots_read(dve.eng, plan, m // UPS + 1)
                residual(m, ps[:, m, 0:W], c0, layer, gate, G["x"])

        return dict(name=name, tensor=tensor, vector=vector)

    def residual(m, y, c0, layer, gate, signal):
        if gate is None:
            nc.vector.scalar_tensor_tensor(x[:, m, c0:NTOK], x[:, m, c0:NTOK], ALPHA, y, ALU.mult, ALU.add)\
              .then_inc(signal, 1)
            return
        segs = [(0, 0), (T, 1)] if c0 == 0 else [(T, 1)]
        for t0, s in segs:
            ins = nc.vector.scalar_tensor_tensor(x[:, m, t0:t0 + T], y[:, t0 - c0:t0 - c0 + T],
                                                 mods[:, layer, gate * 8 + m, s:s + 1], x[:, m, t0:t0 + T],
                                                 ALU.mult, ALU.add)
        ins.then_inc(signal, 1)

    def ffn(name, nblk, c0, conv, layer, gate, h_ready, src):
        W = NTOK - c0
        nseg = W // T
        G = Signals("ffn", name, hidden=nblk, conv=nblk if conv else 0, act=nblk)
        R = Signals("residual", name, x=KD)
        hid, t1, t2 = carve(nblk * W, 2 * W, 2 * W)
        hid = hid.rearrange("p (f t) -> p f t", f=nblk)
        t1 = t1.rearrange("p (b t) -> p b t", b=2)
        t2 = t2.rearrange("p (b t) -> p b t", b=2)
        cw = col("ffn_cw").rearrange("p (l f w) -> p l f w", l=2, w=3)
        cb = col("ffn_cb").rearrange("p (l f) -> p l f", l=2)

        def tensor(pe):
            for f in range(nblk):
                w = units(pe.slots.take())
                if f >= 2:
                    G.wait(pe.eng, "hidden", f - 1)
                for c in range(2):
                    for k in range(KD):
                        if f == 0 and c == 0:
                            h_ready(pe, k)
                        mm = nc.tensor.matmul(ps[:, 2 * (f % 2) + c, 0:W], w[:, c, k, :], src[:, k, c0:NTOK],
                                              start=(k == 0), stop=(k == KD - 1))
                mm.then_inc(slot_read, 1)
            G.wait(pe.eng, "hidden", nblk)
            w = None
            for q in range(DQ):
                if q >= 2:
                    R.wait(pe.eng, "x", 2 * (q - 1))
                for f in range(nblk):
                    n = q * nblk + f
                    if n % DPS == 0:
                        w = pe.slots.take().rearrange("p (n m c) -> p n m c", n=DPS, m=2)
                    for m in range(2):
                        mm = nc.tensor.matmul(ps[:, 4 + 2 * (q % 2) + m, 0:W], w[:, n % DPS, m, :], hid[:, f, :],
                                              start=(f == 0), stop=(f == nblk - 1))
                    if n % DPS == DPS - 1:
                        mm.then_inc(slot_read, 1)

        def scalar(act):
            for f in range(nblk):
                if conv:
                    G.wait(act.eng, "conv", f + 1)
                    nc.scalar.activation(t2[:, f % 2, :], t1[:, f % 2, :], ACT.Gelu_apprx_tanh)\
                      .then_inc(G["act"], 1)
                else:
                    slots_read(act.eng, f"{name}_up", f + 1)
                    if f >= 2:
                        G.wait(act.eng, "hidden", f - 1)
                    nc.scalar.activation(t2[:, f % 2, :], ps[:, 2 * (f % 2), 0:W], ACT.Silu)\
                      .then_inc(G["act"], 1)

        def vector(dve):
            for f in range(nblk):
                slots_read(dve.eng, f"{name}_up", f + 1)
                if conv:
                    g = ps[:, 2 * (f % 2), 0:W].rearrange("p (s t) -> p s t", s=nseg)
                    t = t1[:, f % 2, :].rearrange("p (s t) -> p s t", s=nseg)
                    dve.add(nc.vector.tensor_scalar(t, g, cw[:, layer, f, 1:2], cb[:, layer, f:f + 1],
                                                    ALU.mult, ALU.add))
                    dve.settle()
                    dve.add(nc.vector.scalar_tensor_tensor(t[:, :, 1:T], g[:, :, 0:T - 1], cw[:, layer, f, 0:1],
                                                           t[:, :, 1:T], ALU.mult, ALU.add))
                    dve.settle()
                    nc.vector.scalar_tensor_tensor(t[:, :, 0:T - 1], g[:, :, 1:T], cw[:, layer, f, 2:3],
                                                   t[:, :, 0:T - 1], ALU.mult, ALU.add)\
                      .then_inc(G["conv"], 1)
                G.wait(dve.eng, "act", f + 1)
                nc.vector.tensor_tensor(hid[:, f, :], t2[:, f % 2, :], ps[:, 2 * (f % 2) + 1, 0:W], ALU.mult)\
                  .then_inc(G["hidden"], 1)
            for q in range(DQ):
                slots_read(dve.eng, f"{name}_down", -(-(q + 1) * nblk // DPS))
                for m in range(2):
                    residual(2 * q + m, ps[:, 4 + 2 * (q % 2) + m, 0:W], c0, layer, gate, R["x"])

        return dict(name=name, tensor=tensor, scalar=scalar, vector=vector)

    def attention(name, n_it, scores, segments, factors, values, exp_scale, before):
        nseg = max(len(segments(i)) for i in range(n_it))
        G = Signals("attention", name, scores=n_it, max=n_it, exp=n_it, probs=n_it, turn=n_it, turned=n_it,
                    out=n_it, pair=n_it // (2 * TT))
        PW = 528
        base = ATT_BASE
        p = arena[:, base:base + 2 * PW].rearrange("p (b c) -> p b c", b=2)
        pt = arena[:, base + 2 * PW:base + 2 * PW + 2 * 640].rearrange("p (b j t) -> p b j t", b=2, j=5)
        st = arena[:, base + 2 * PW + 1280:base + 2 * PW + 1280 + 64].rearrange("p (b c) -> p b c", b=2)

        def tensor(pe):
            before(pe.eng)
            for step in range(n_it + 2):
                if step < n_it:
                    if step >= 2:
                        G.wait(pe.eng, "exp", step - 1)
                        G.wait(pe.eng, "turned", step - 1)
                    scores(step).then_inc(G["scores"], 1)
                if 1 <= step <= n_it:
                    it = step - 1
                    G.wait(pe.eng, "probs", it + 1)
                    if it >= 2:
                        G.wait(pe.eng, "turned", it - 1)
                    for j, (c, n, _) in enumerate(values(it)):
                        dst = ps[0:n, 4 + it % 2, j * P:(j + 1) * P] if j < 4 else ps[0:n, 2 + it % 2, P:2 * P]
                        mm = nc.tensor.transpose(dst, p[:, it % 2, c:c + n], ident)
                    mm.then_inc(G["turn"], 1)
                if step >= 2:
                    it = step - 2
                    head, i = it // TT, it % TT
                    pair = head // 2
                    G.wait(pe.eng, "turned", it + 1)
                    if pair >= 2 and head % 2 == 0 and i == 0:
                        G.wait(pe.eng, "pair", pair - 1)
                    vs = values(it)
                    for j, (c, n, v) in enumerate(vs):
                        mm = nc.tensor.matmul(ps[64 * (head % 2):64 * (head % 2) + 64, 6 + pair % 2, i * P:(i + 1) * P],
                                              v, pt[0:n, it % 2, j, :], start=(j == 0), stop=(j == len(vs) - 1))
                    mm.then_inc(G["out"], 1)

        def scalar(act):
            for step in range(n_it + 2):
                if step < n_it:
                    it = step
                    G.wait(act.eng, "max", it + 1)
                    if it >= 2:
                        G.wait(act.eng, "turn", it - 1)
                    segs = segments(it)
                    for n, (bank, c0, w, pc) in enumerate(segs):
                        ins = nc.scalar.activation(p[:, it % 2, pc:pc + w], ps[:, bank, c0:c0 + w], ACT.Exp,
                                                   scale=exp_scale, bias=st[:, it % 2, 4 + n:5 + n],
                                                   accum_out=st[:, it % 2, 8 + n:9 + n])
                        if n < len(segs) - 1:
                            continue
                        if name == "swa":
                            ins = nc.scalar.activation(st[:, it % 2, 12:13], col("sinks")[:, it // TT:it // TT + 1],
                                                       ACT.Exp, bias=st[:, it % 2, 4:5])
                        ins.then_inc(G["exp"], 1)
                if step >= 2:
                    it = step - 2
                    head, i = it // TT, it % TT
                    if head % 2 == 1 and i == TT - 1:
                        G.wait(act.eng, "out", it + 1)
                        nc.scalar.activation(h[:, head // 2, T:NTOK], ps[:, 6 + (head // 2) % 2, 0:T], ACT.Copy)\
                          .then_inc(G["pair"], 1)

        def vector(dve):
            for step in range(n_it + 2):
                if step >= 2:
                    it = step - 2
                    b = it % 2
                    G.wait(dve.eng, "turn", it + 1)
                    if it >= 2:
                        G.wait(dve.eng, "out", it - 1)
                    vs = values(it)
                    full = [j for j, (_, n, _) in enumerate(vs) if n == P]
                    ins = nc.vector.tensor_copy(pt[:, b, 0:len(full), :],
                                                ps[:, 4 + b, 0:len(full) * P].rearrange("p (j t) -> p j t", t=P))
                    for j, (c, n, _) in enumerate(vs):
                        if n != P:
                            srcp = ps[0:n, 4 + b, j * P:(j + 1) * P] if j < 4 else ps[0:n, 2 + b, P:2 * P]
                            ins = nc.vector.tensor_copy(pt[0:n, b, j, :], srcp)
                    ins.then_inc(G["turned"], 1)
                if step < n_it:
                    it = step
                    b = it % 2
                    G.wait(dve.eng, "scores", it + 1)
                    segs = segments(it)
                    n = 0
                    while n < len(segs):
                        bank, c0, w, _ = segs[n]
                        many = 2 if n + 1 < len(segs) and segs[n + 1][0] == bank else 1
                        dve.add(nc.vector.tensor_reduce(st[:, b, n:n + many],
                                                        ps[:, bank, c0:c0 + many * w].rearrange("p (a w) -> p a w", a=many),
                                                        AX.X, ALU.max))
                        n += many
                    dve.settle()
                    if name == "swa":
                        dve.add(nc.vector.tensor_scalar(st[:, b, 0:1], st[:, b, 0:1], exp_scale,
                                                        col("sinks")[:, it // TT:it // TT + 1], ALU.mult, ALU.max))
                        dve.settle()
                        neg_scale = -1.0
                    else:
                        neg_scale = -exp_scale
                    nc.vector.tensor_scalar(st[:, b, 4:4 + nseg], st[:, b, 0:nseg], neg_scale, None, ALU.mult)\
                      .then_inc(G["max"], 1)
                if 1 <= step <= n_it:
                    it = step - 1
                    b = it % 2
                    G.wait(dve.eng, "exp", it + 1)
                    if name == "swa":
                        dve.add(nc.vector.tensor_tensor(st[:, b, 8:9], st[:, b, 8:9], st[:, b, 12:13], ALU.add))
                        dve.settle()
                    dve.add(nc.vector.reciprocal(st[:, b, 16:16 + nseg], st[:, b, 8:8 + nseg]))
                    dve.settle()
                    factors(dve, it, st[:, b, 16:16 + nseg])
                    segs = segments(it)
                    for n, (bank, c0, w, pc) in enumerate(segs):
                        ins = nc.vector.tensor_scalar(p[:, b, pc:pc + w], p[:, b, pc:pc + w], st[:, b, 16 + n:17 + n],
                                                      None, ALU.mult)
                    ins.then_inc(G["probs"], 1)

        return dict(name=name, tensor=tensor, scalar=scalar, vector=vector)

    KT0, QT0, V0 = 0, H_MLA * NTOK, H_MLA * NTOK + H_MLA * T
    ATT_BASE = V0 + 4 * H_MLA * V_MLA

    def mla_proj():
        name = "mla"
        kT = arena[0:QK_MLA, KT0:QT0].rearrange("p (h t) -> p h t", h=H_MLA)
        qT = arena[0:QK_MLA, QT0:V0].rearrange("p (h t) -> p h t", h=H_MLA)
        v = arena[:, V0:ATT_BASE].rearrange("p (t h c) -> p t h c", t=4, h=H_MLA)
        at = ATT_BASE
        w96 = H_MLA * QK_MLA
        tile = arena[:, at:at + w96].rearrange("p (h c) -> p h c", h=H_MLA)
        sq = arena[:, at + w96:at + 2 * w96].rearrange("p (h c) -> p h c", h=H_MLA)
        at += 2 * w96
        kr = arena[:, at:at + 4 * ROPE].rearrange("p (t c) -> p t c", t=4)
        st = arena[:, at + 128:at + 128 + 64]
        at += 192
        q_raw = arena[:, at:at + 2 * w96].rearrange("p (t c) -> p t c", t=2)
        assert at + 2 * w96 <= ARENA, at + 2 * w96
        cqn = arena[:, KT0:KT0 + 4 * T].rearrange("p (b t) -> p b t", b=4)
        sqq = arena[:, KT0 + 1024:KT0 + 2048].rearrange("p (b t) -> p b t", b=4)
        sqk = arena[:, KT0 + 2048:KT0 + 3072].rearrange("p (b t) -> p b t", b=2)
        stq, rq = arena[:, KT0 + 3072:KT0 + 3328], arena[:, KT0 + 3328:KT0 + 3584]
        stk, rk = arena[:, KT0 + 3584:KT0 + 4096], arena[:, KT0 + 4096:KT0 + 4608]
        ckn = h
        tiles = [("q", 0), ("q", 1)] + [("k", t) for t in range(4)]
        S = lambda s: sem(f"mla_{s}")

        def tensor(pe):
            eng = pe.eng
            for s in range(2):
                w = units(pe.slots.take())
                for u in range(UPS):
                    for k in range(KD):
                        if s == 0 and u == 0:
                            h_block_ready(pe, "mla_mod", 0, k)
                        mm = nc.tensor.matmul(ps[:, 2 * s + u, 0:T], w[:, u, k, :], h[:, k, T:NTOK],
                                              start=(k == 0), stop=(k == KD - 1))
                mm.then_inc(slot_read, 1)
            w = units(pe.slots.take())
            for u in range(UPS):
                for k in range(KD):
                    mm = nc.tensor.matmul(ps[:, 4 + u, :], w[:, u, k, :], h[:, k, :],
                                          start=(k == 0), stop=(k == KD - 1))
            mm.then_inc(slot_read, 1)
            krw = col("kr_w").rearrange("p (k c) -> p k c", k=KD)
            for t in range(4):
                for k in range(KD):
                    mm = nc.tensor.matmul(ps[:, 6, t * ROPE:(t + 1) * ROPE], h[:, k, t * P:(t + 1) * P], krw[:, k, :],
                                          start=(k == 0), stop=(k == KD - 1))
            mm.then_inc(S("kr_done"), 1)
            for b in range(2):
                eng.wait_ge(S("sqk"), b + 1)
                mm = nc.tensor.matmul(ps[:, 7, :], col("over256"), sqk[:, b, :], start=(b == 0), stop=(b == 1))
            mm.then_inc(S("msk"), 1)
            eng.wait_ge(S("kr"), 1)
            for b in range(4):
                eng.wait_ge(S("sqq"), b + 1)
                mm = nc.tensor.matmul(ps[:, 6, 0:T], col("over512"), sqq[:, b, :], start=(b == 0), stop=(b == 3))
            mm.then_inc(S("msq"), 1)
            eng.wait_ge(S("cqn"), 4)
            eng.wait_ge(S("ckn"), 2)
            for n in range(3):
                w = pe.slots.take().rearrange("p (k c) -> p k c", k=4)
                for t in range(2):
                    for k in range(4):
                        mm = nc.tensor.matmul(ps[:, 2 * n + t, :], cqn[:, k, t * P:(t + 1) * P], w[:, k, :],
                                              start=(k == 0), stop=(k == 3))
                mm.then_inc(slot_read, 1)
            w0 = pe.slots.take().rearrange("p (n k c) -> p n k c", n=2, k=2)
            w1 = pe.slots.take().rearrange("p (n k c) -> p n k c", n=2, k=2)
            for n, (kind, t) in enumerate(tiles):
                if kind == "k":
                    eng.wait_ge(S("q_raw"), 6)
                    if t:
                        eng.wait_ge(S("k_taken"), 4 * t)
                        eng.wait_ge(S("v_taken"), 4 * t)
                    for c in range(4):
                        w = (w0 if c < 2 else w1)[:, c % 2]
                        for k in range(2):
                            mm = nc.tensor.matmul(ps[:, c, :], ckn[:, k, t * P:(t + 1) * P], w[:, k, :],
                                                  start=(k == 0), stop=(k == 1))
                        if t < 3 or c % 2 == 0:
                            mm.then_inc(S("ukv_done"), 1)
                        else:
                            mm.then_inc(slot_read, 1)
                eng.wait_ge(S("rotated"), n + 1)
                for hd in range(H_MLA):
                    if hd % 4 == 0 and n:
                        eng.wait_ge(S("turned"), 4 * (n - 1) + hd // 4 + 1)
                    mm = nc.tensor.transpose(ps[0:QK_MLA, 4 + hd // 4, (hd % 4) * P:(hd % 4 + 1) * P],
                                             tile[:, hd, :], ident)
                    if hd % 4 == 3:
                        mm.then_inc(S("turn"), 1)

        def scalar(act):
            eng = act.eng
            for b in range(2):
                slots_read(eng, "mla_in", 3)
                nc.scalar.activation(sqk[:, b, :], ps[:, 4 + b, :], ACT.Square).then_inc(S("sqk"), 1)
            for b in range(4):
                nc.scalar.activation(sqq[:, b, :], ps[:, b, 0:T], ACT.Square).then_inc(S("sqq"), 1)
            eng.wait_ge(S("kr_done"), 1)
            nc.scalar.activation(kr[:, :, :], ps[:, 6, 0:4 * ROPE].rearrange("p (t c) -> p t c", t=4), ACT.Copy)\
              .then_inc(S("kr"), 1)
            eng.wait_ge(S("msk"), 1)
            nc.scalar.activation(stk, ps[:, 7, :], ACT.Sqrt, bias=col("eps6")).then_inc(S("stk"), 1)
            eng.wait_ge(S("msq"), 1)
            nc.scalar.activation(stq, ps[:, 6, 0:T], ACT.Sqrt, bias=col("eps6")).then_inc(S("stq"), 1)
            for n in range(3):
                slots_read(eng, "mla_uq", n + 1)
                for t in range(2):
                    nc.scalar.activation(q_raw[:, t, n * 512:(n + 1) * 512], ps[:, 2 * n + t, :], ACT.Copy)\
                      .then_inc(S("q_raw"), 1)
            for n, (kind, t) in enumerate(tiles):
                if n:
                    eng.wait_ge(S("turn"), 4 * n)
                if kind == "q":
                    eng.wait_ge(S("q_raw"), 6)
                    nc.scalar.activation(tile.rearrange("p h c -> p (h c)"), q_raw[:, t, :], ACT.Copy)\
                      .then_inc(S("tile"), 1)
                else:
                    for c in range(4):
                        ukv_chunk_done(eng, t, c)
                        nc.scalar.activation(tile[:, 4 * c:4 * c + 4, 0:NOPE],
                                             ps[:, c, :].rearrange("p (h c) -> p h c", h=4)[:, :, 0:NOPE], ACT.Copy)\
                          .then_inc(S("k_taken"), 1)
                    nc.scalar.activation(tile[:, :, NOPE:QK_MLA], kr[:, t:t + 1, :].to_broadcast([P, H_MLA, ROPE]),
                                         ACT.Copy).then_inc(S("tile"), 1)
                eng.wait_ge(S("tile"), n + 1)
                if kind == "k":
                    eng.wait_ge(S("k_taken"), 4 * t + 4)
                nc.scalar.activation(sq[:, :, :], tile[:, :, :], ACT.Square).then_inc(S("sq"), 1)
                eng.wait_ge(S("ss"), n + 1)
                nc.scalar.activation(st[:, 16:32], st[:, 0:16], ACT.Sqrt, scale=1.0 / QK_MLA, bias=col("eps6"))\
                  .then_inc(S("rms"), 1)
                for c in range(0, 4, 2):
                    turned_out(eng, nc.scalar, n, c)

        def ukv_chunk_done(eng, t, c):
            if t == 3 and c % 2 == 1:
                slots_read(eng, "mla_ukv", c // 2 + 1)
            else:
                eng.wait_ge(S("ukv_done"), 4 * t + c + 1 if t < 3 else 13 + c // 2)

        def turned_out(eng, unit, n, c):
            kind, t = tiles[n]
            dst = (qT if kind == "q" else kT)[:, 4 * c:4 * c + 4, t * P:(t + 1) * P]
            src = ps[0:QK_MLA, 4 + c, :].rearrange("p (h t) -> p h t", h=4)
            eng.wait_ge(S("turn"), 4 * n + c + 1)
            if unit is nc.scalar:
                if 4 * n + c:
                    eng.wait_ge(S("turned"), 4 * n + c)
                nc.scalar.activation(dst, src, ACT.Copy).then_inc(S("turned"), 1)
            else:
                eng.wait_ge(S("turned"), 4 * n + c)
                nc.vector.tensor_copy(dst, src).then_inc(S("turned"), 1)

        def vector(dve):
            eng = dve.eng
            slots_read(eng, "mla_in", 3)
            eng.wait_ge(S("stk"), 1)
            dve.add(nc.vector.reciprocal(rk, stk))
            dve.settle()
            eng.wait_ge(S("kr_done"), 1)
            for b in range(2):
                nc.vector.scalar_tensor_tensor(ckn[:, b, :], ps[:, 4 + b, :], col("kv_norm")[:, b:b + 1], rk,
                                               ALU.mult, ALU.mult).then_inc(S("ckn"), 1)
            eng.wait_ge(S("stq"), 1)
            dve.add(nc.vector.reciprocal(rq, stq))
            dve.settle()
            for b in range(4):
                nc.vector.scalar_tensor_tensor(cqn[:, b, :], ps[:, b, 0:T], col("q_norm")[:, b:b + 1], rq,
                                               ALU.mult, ALU.mult).then_inc(S("cqn"), 1)
            c1 = col("cos1").rearrange("p (t o c) -> p t o c", t=TT, o=1)
            s1 = col("sin1").rearrange("p (t o c) -> p t o c", t=TT, o=1)
            for n, (kind, t) in enumerate(tiles):
                if kind == "k":
                    for c in range(4):
                        eng.wait_ge(S("k_taken"), 4 * t + c + 1)
                        nc.vector.tensor_copy(v[:, t, 4 * c:4 * c + 4, :],
                                              ps[:, c, :].rearrange("p (h c) -> p h c", h=4)[:, :, NOPE:2 * NOPE])\
                          .then_inc(S("v_taken"), 1)
                eng.wait_ge(S("sq"), n + 1)
                nc.vector.tensor_reduce(st[:, 0:16], sq[:, :, :], AX.X, ALU.add).then_inc(S("ss"), 1)
                eng.wait_ge(S("rms"), n + 1)
                dve.add(nc.vector.reciprocal(st[:, 32:48], st[:, 16:32]))
                dve.settle()
                dve.add(nc.vector.tensor_tensor(tile[:, :, :], tile[:, :, :],
                                                st[:, 32:48].rearrange("p (h o) -> p h o", o=1)
                                                .to_broadcast([P, H_MLA, QK_MLA]), ALU.mult))
                dve.settle()
                gain = col("q_gain" if kind == "q" else "k_gain").rearrange("p (o c) -> p o c", o=1)
                rotate = kind == "q" or t >= 2
                ins = nc.vector.tensor_tensor(tile[:, :, :], tile[:, :, :], gain.to_broadcast([P, H_MLA, QK_MLA]),
                                              ALU.mult)
                if not rotate:
                    ins.then_inc(S("rotated"), 1)
                else:
                    dve.add(ins)
                    dve.settle()
                    ti = t if kind == "q" else t - 2
                    r = tile[:, :, NOPE:QK_MLA].rearrange("p h (c two) -> p h c two", two=2)
                    r1, r2 = r[:, :, :, 0], r[:, :, :, 1]
                    tm = sq.rearrange("p h c -> p (h c)")[:, 0:1024].rearrange("p (n h c) -> p n h c", n=4, h=H_MLA)
                    cb, sb = c1[:, ti].to_broadcast([P, H_MLA, 16]), s1[:, ti].to_broadcast([P, H_MLA, 16])
                    for m, (a, b) in enumerate([(r1, cb), (r2, sb), (r1, sb), (r2, cb)]):
                        dve.add(nc.vector.tensor_tensor(tm[:, m], a, b, ALU.mult))
                    dve.settle()
                    nc.vector.tensor_tensor(r1, tm[:, 0], tm[:, 1], ALU.subtract)
                    nc.vector.tensor_tensor(r2, tm[:, 2], tm[:, 3], ALU.add).then_inc(S("rotated"), 1)
                for c in range(1, 4, 2):
                    turned_out(eng, nc.vector, n, c)

        return dict(name=name, tensor=tensor, scalar=scalar, vector=vector)

    def mla_attention():
        kT = arena[0:QK_MLA, KT0:QT0].rearrange("p (h t) -> p h t", h=H_MLA)
        qT = arena[0:QK_MLA, QT0:V0].rearrange("p (h t) -> p h t", h=H_MLA)
        v = arena[:, V0:ATT_BASE].rearrange("p (t h c) -> p t h c", t=4, h=H_MLA)

        def scores(it):
            head, i = it // TT, it % TT
            return nc.tensor.matmul(ps[:, it % 2, :], qT[:, head, i * P:(i + 1) * P], kT[:, head, :],
                                    start=True, stop=True)

        return attention("mla_att", H_MLA * TT, scores, lambda it: [(it % 2, 0, NTOK, 0)],
                         lambda dve, it, rec: None,
                         lambda it: [(j * P, P, v[:, j, it // TT, :]) for j in range(4)],
                         QK_MLA ** -0.5, lambda eng: eng.wait_ge(sem("mla_turned"), 24))

    def layer_norm(name, after, which):
        G = Signals("ln", name, mean=1, square=KD, var=1, centred=KD, std=1, scaled=KD, x=KD)
        sq, cen, std, rstd = carve(KD * T, KD * T, T, T)
        sq = sq.rearrange("p (k t) -> p k t", k=KD)
        cen = cen.rearrange("p (k t) -> p k t", k=KD)

        def tensor(pe):
            for k in range(KD):
                after(pe.eng, k + 1)
                mm = nc.tensor.matmul(ps[:, 0, 0:T], col("over1024"), x[:, k, T:NTOK], start=(k == 0), stop=(k == KD - 1))
            mm.then_inc(G["mean"], 1)
            for k in range(KD):
                G.wait(pe.eng, "square", k + 1)
                mm = nc.tensor.matmul(ps[:, 1, 0:T], col("over1024"), sq[:, k, :], start=(k == 0), stop=(k == KD - 1))
            mm.then_inc(G["var"], 1)

        def vector(dve):
            after(dve.eng, KD)
            G.wait(dve.eng, "mean", 1)
            for k in range(KD):
                nc.vector.tensor_tensor(cen[:, k, :], x[:, k, T:NTOK], ps[:, 0, 0:T], ALU.subtract)\
                  .then_inc(G["centred"], 1)
            G.wait(dve.eng, "std", 1)
            dve.add(nc.vector.reciprocal(rstd, std))
            dve.settle()
            G.wait(dve.eng, "square", KD)
            for k in range(KD):
                nc.vector.tensor_tensor(cen[:, k, :], cen[:, k, :], rstd, ALU.mult).then_inc(G["scaled"], 1)

        def scalar(act):
            for k in range(KD):
                G.wait(act.eng, "centred", k + 1)
                nc.scalar.activation(sq[:, k, :], cen[:, k, :], ACT.Square).then_inc(G["square"], 1)
            G.wait(act.eng, "var", 1)
            nc.scalar.activation(std, ps[:, 1, 0:T], ACT.Sqrt, bias=col("eps5")).then_inc(G["std"], 1)
            g = col("ln2_g").rearrange("p (n k) -> p n k", n=4)
            b = col("ln2_b").rearrange("p (n k) -> p n k", n=4)
            for k in range(KD):
                G.wait(act.eng, "scaled", k + 1)
                nc.scalar.activation(x[:, k, T:NTOK], cen[:, k, :], ACT.Identity, scale=g[:, which, k:k + 1],
                                     bias=b[:, which, k:k + 1]).then_inc(G["x"], 1)

        return dict(name=name, tensor=tensor, scalar=scalar, vector=vector)

    def swa():
        name = "swa_in"
        q, k, v, qr, kr, t1 = carve(KD * T, 2 * T, TT * T, KD * T, KV2 * T, 4 * T)
        q = q.rearrange("p (b t) -> p b t", b=KD)
        k = k.rearrange("p (b t) -> p b t", b=2)
        v = v.rearrange("p (t c) -> p t c", t=TT)
        qr = qr.rearrange("p (b t) -> p b t", b=KD)
        kr = kr.rearrange("p (b t) -> p b t", b=KV2)
        t1 = t1.rearrange("p (n t) -> p n t", n=4)
        S = lambda s: sem(f"swa_{s}")
        jobs = [(q[:, b, :], ident, col("rot"), qr[:, b, :]) for b in range(KD)] + \
               [(k[:, g // 2, :], col(f"dup{g % 2}"), col(f"rdup{g % 2}"), kr[:, g, :]) for g in range(KV2)]
        assert KD * T * 2 + 2 * T + TT * T + KV2 * T + 4 * T <= ATT_BASE

        def tensor(pe):
            for s in range(5):
                w = units(pe.slots.take())
                if s == 4:
                    pe.eng.wait_ge(S("copied"), 2)
                for u in range(UPS):
                    for kk in range(KD):
                        if s == 0 and u == 0:
                            signals["ffn1"].wait(pe.eng, "x", kk + 1)
                        mm = nc.tensor.matmul(ps[:, (2 * s + u) % 8, 0:T], w[:, u, kk, :], x[:, kk, T:NTOK],
                                              start=(kk == 0), stop=(kk == KD - 1))
                mm.then_inc(slot_read, 1)
            w = pe.slots.take().rearrange("p (k c) -> p k c", k=KD)
            pe.eng.wait_ge(S("copied"), 4)
            for t in range(TT):
                for kk in range(KD):
                    mm = nc.tensor.matmul(ps[:, 2 + t, 0:T], x[:, kk, T + t * P:T + (t + 1) * P], w[:, kk, :],
                                          start=(kk == 0), stop=(kk == KD - 1))
            mm.then_inc(slot_read, 1)
            rotate_tensor(pe, name, jobs, lambda n: pe.eng.wait_ge(S("copied"), 10), (4, 5, 6, 7))

        def scalar(act):
            for b in range(10):
                slots_read(act.eng, "swa_in", b // 2 + 1)
                dst = q[:, b, :] if b < 8 else k[:, b - 8, :]
                nc.scalar.activation(dst, ps[:, b % 8, 0:T], ACT.Copy).then_inc(S("copied"), 1)
            slots_read(act.eng, "swa_in", 6)
            for t in range(TT):
                nc.scalar.activation(v[:, t, :], ps[:, 2 + t, 0:T], ACT.Copy).then_inc(S("v"), 1)

        def vector(dve):
            rotate_vector(dve, name, jobs, t1, (4, 5, 6, 7))

        def scores(it):
            head, i = it // TT, it % TT
            half = slice(64 * (head % 2), 64 * (head % 2) + 64)
            W = (i + 1) * P
            nc.tensor.matmul(ps[:, it % 2, 0:W], qr[half, head // 2, i * P:(i + 1) * P], kr[half, head // G2, 0:W],
                             start=True, stop=False)
            if i:
                nc.tensor.matmul(ps[:, it % 2, 0:P], ident_b[:, :], band_b[:, :], start=False, stop=False)
            return nc.tensor.matmul(ps[:, it % 2, i * P:W], ident_b[:, :], causal_b[:, :], start=False, stop=True)

        def before(eng):
            eng.wait_ge(sem("swa_in_rotated"), len(jobs))
            eng.wait_ge(S("v"), TT)
            eng.wait_ge(masks_ready, 1)

        att = attention("swa", H2 * TT, scores, lambda it: [(it % 2, 0, (it % TT + 1) * P, 0)],
                        lambda dve, it, rec: None,
                        lambda it: [(j * P, P, v[:, j, HD * (it // TT // G2):HD * (it // TT // G2) + HD])
                                    for j in range(it % TT + 1)],
                        HD ** -0.5, before)
        return dict(name=name, tensor=tensor, scalar=scalar, vector=vector), att

    def rotate_tensor(pe, name, jobs, ready, banks):
        for n, (src, plain, rot, dst) in enumerate(jobs):
            if n == 0:
                ready(n)
            if n >= 2:
                pe.eng.wait_ge(sem(f"{name}_rotated"), n - 1)
            a = banks[2 * (n % 2)]
            if plain is not None:
                mm = nc.tensor.matmul(ps[:, a, 0:T], plain, src, start=True, stop=True)
            if rot is not None:
                mm = nc.tensor.matmul(ps[:, a + 1, 0:T], rot, src, start=True, stop=True)
            mm.then_inc(sem(f"{name}_turn"), 1)

    def rotate_vector(dve, name, jobs, t1, banks):
        for n, (src, plain, rot, dst) in enumerate(jobs):
            a = banks[2 * (n % 2)]
            dve.eng.wait_ge(sem(f"{name}_turn"), n + 1)
            signal = sem(f"{name}_rotated")
            if rot is None:
                pieces = [(slice(0, P), 0, T, dst)] if not isinstance(dst, list) else dst
                for part, c0, c1, d in pieces:
                    ins = nc.vector.tensor_copy(d, ps[part, a, c0:c1])
                ins.then_inc(signal, 1)
                continue
            u, w = t1[:, 2 * (n % 2), :], t1[:, 2 * (n % 2) + 1, :]
            dve.add(nc.vector.tensor_tensor(u, ps[:, a, 0:T], col("cos2"), ALU.mult))
            dve.add(nc.vector.tensor_tensor(w, ps[:, a + 1, 0:T], col("sin2"), ALU.mult))
            dve.settle()
            pieces = [(slice(0, P), 0, T, dst)] if not isinstance(dst, list) else dst
            for part, c0, c1, d in pieces:
                ins = nc.vector.tensor_tensor(d, u[part, c0:c1], w[part, c0:c1], ALU.add)
            ins.then_inc(signal, 1)

    def nsa():
        name = "nsa_in"
        q, kk_, v, gates, ksr, kwr, t1, cmpk, cmpv, blk, hidc, vcc, kcc = carve(
            KD * T, 8 * T, TT * 512, TT * 48, KV2 * T, KV2 * T, 4 * T, KV2 * T, KV2 * T,
            2 * LP * KV2 * NCMP, 2 * 2 * KV2 * NCMP, KV2 * HD, KV2 * NCMP)
        q = q.rearrange("p (b t) -> p b t", b=KD)
        kvs = kk_.rearrange("p (n b t) -> p n b t", n=4, b=2)
        v = v.rearrange("p (t n c) -> p t n c", t=TT, n=2)
        gates = gates.rearrange("p (t c) -> p t c", t=TT)
        ksr = ksr.rearrange("p (b t) -> p b t", b=KV2)
        kwr = kwr.rearrange("p (b t) -> p b t", b=KV2)
        t1 = t1.rearrange("p (n t) -> p n t", n=4)
        cmpk = cmpk.rearrange("p (g t) -> p g t", g=KV2)
        cmpv = cmpv.rearrange("p (g t) -> p g t", g=KV2)
        NB = KV2 * NCMP
        blk = blk.rearrange("p (n l c) -> p n l c", n=2, l=LP)
        hidc = hidc.rearrange("p (n m c) -> p n m c", n=2, m=2)
        vcc = vcc.rearrange("p (g c) -> p g c", g=KV2)
        S = lambda s: sem(f"nsa_{s}")
        jobs = []

        def shifted(dst, g):
            return [(slice(0, 64), 0, T, dst[0:64, g, :]), (slice(64, P), 1, T, dst[64:P, g, 0:T - 1])]

        for g in range(KV2):
            jobs.append((kvs[:, 0, g // 2, :], col(f"dup{g % 2}"), col(f"rdup{g % 2}"), shifted(cmpk, g)))
        for g in range(KV2):
            jobs.append((kvs[:, 1, g // 2, :], col(f"dup{g % 2}"), None, shifted(cmpv, g)))
        for g in range(KV2):
            jobs.append((kvs[:, 2, g // 2, :], col(f"dup{g % 2}"), col(f"rdup{g % 2}"), ksr[:, g, :]))
        for g in range(KV2):
            jobs.append((kvs[:, 3, g // 2, :], col(f"dup{g % 2}"), col(f"rdup{g % 2}"), kwr[:, g, :]))
        for b in range(KD):
            jobs.append((q[:, b, :], ident, col("rot"), q[:, b, :]))

        def tensor(pe):
            eng = pe.eng
            for s in range(8):
                w = units(pe.slots.take())
                if s >= 4:
                    eng.wait_ge(S("copied"), 2 * (s - 3))
                for u in range(UPS):
                    for k in range(KD):
                        if s == 0 and u == 0:
                            signals["ln2"].wait(eng, "x", k + 1)
                        mm = nc.tensor.matmul(ps[:, (2 * s + u) % 8, 0:T], w[:, u, k, :], x[:, k, T:NTOK],
                                              start=(k == 0), stop=(k == KD - 1))
                mm.then_inc(slot_read, 1)
            eng.wait_ge(S("copied"), 10)
            for s in range(2):
                w = pe.slots.take().rearrange("p (k c) -> p k c", k=4)
                for t in range(TT):
                    for k in range(4):
                        mm = nc.tensor.matmul(ps[:, t, :], x[:, 4 * s + k, T + t * P:T + (t + 1) * P], w[:, k, :],
                                              start=(s == 0 and k == 0), stop=(s == 1 and k == 3))
                mm.then_inc(slot_read, 1)
            eng.wait_ge(S("copied"), 11)
            gw = col("ng_w").rearrange("p (k c) -> p k c", k=KD)
            for t in range(TT):
                for k in range(KD):
                    mm = nc.tensor.matmul(ps[:, 2, t * 48:(t + 1) * 48], x[:, k, T + t * P:T + (t + 1) * P], gw[:, k, :],
                                          start=(k == 0), stop=(k == KD - 1))
            mm.then_inc(S("gates_done"), 1)
            rotate_tensor(pe, name, jobs, lambda n: eng.wait_ge(S("copied"), 16), (4, 5, 6, 7))
            for n in range(2):
                if n == 0:
                    eng.wait_ge(S("v"), 2)
                eng.wait_ge(S("blk"), n + 1)
                for m in range(2):
                    w = pe.slots.take().rearrange("p (l c) -> p l c", l=LP)
                    for l in range(LP):
                        mm = nc.tensor.matmul(ps[:, n, m * 64:m * 64 + NB], w[:, l, :], blk[:, n, l, :],
                                              start=(l == 0), stop=(l == LP - 1))
                    mm.then_inc(slot_read, 1)
            w2k = col("w2k").rearrange("p (m c) -> p m c", m=2)
            w2v = col("w2v").rearrange("p (m c) -> p m c", m=2)
            eng.wait_ge(S("hid"), 1)
            eng.wait_ge(S("gates"), 1)
            for m in range(2):
                mm = nc.tensor.matmul(ps[:, 3, 0:NB], w2k[:, m, :], hidc[:, 0, m, :], start=(m == 0), stop=(m == 1))
            mm.then_inc(S("kcc_done"), 1)
            eng.wait_ge(S("hid"), 2)
            for g in range(KV2):
                for m in range(2):
                    mm = nc.tensor.matmul(ps[0:NCMP, 2, g * HD:(g + 1) * HD],
                                          hidc[:, 1, m, g * NCMP:(g + 1) * NCMP], w2v[:, m, :],
                                          start=(m == 0), stop=(m == 1))
            mm.then_inc(S("vcc_done"), 1)

        def scalar(act):
            eng = act.eng
            for b in range(16):
                slots_read(eng, "nsa_in", b // 2 + 1)
                dst = q[:, b, :] if b < 8 else kvs[:, (b - 8) // 2, b % 2, :]
                nc.scalar.activation(dst, ps[:, b % 8, 0:T], ACT.Copy).then_inc(S("copied"), 1)
            slots_read(eng, "nsa_in", 10)
            for t in range(TT):
                nc.scalar.activation(v[:, t, :, :], ps[:, t, :].rearrange("p (n c) -> p n c", n=2), ACT.Copy)\
                  .then_inc(S("v"), 1)
            eng.wait_ge(S("gates_done"), 1)
            nc.scalar.activation(gates[:, :, :], ps[:, 2, 0:TT * 48].rearrange("p (t c) -> p t c", t=TT), ACT.Sigmoid)\
              .then_inc(S("gates"), 1)
            for n in range(2):
                slots_read(eng, "nsa_cmp", 2 * (n + 1))
                nc.scalar.activation(hidc[:, n, :, :], ps[:, n, 0:P].rearrange("p (m c) -> p m c", m=2)[:, :, 0:NB],
                                     ACT.Gelu_apprx_tanh).then_inc(S("hid"), 1)
            eng.wait_ge(S("kcc_done"), 1)
            nc.scalar.activation(kcc, ps[:, 3, 0:NB], ACT.Copy).then_inc(S("kcc"), 1)
            eng.wait_ge(S("vcc_done"), 1)
            nc.scalar.activation(vcc[0:NCMP, :, :], ps[0:NCMP, 2, 0:KV2 * HD].rearrange("p (g c) -> p g c", g=KV2),
                                 ACT.Copy).then_inc(S("vcc"), 1)

        def vector(dve):
            eng = dve.eng
            eng.wait_ge(S("gates"), 1)
            for t in range(TT):
                gc = gates[:, t, :].rearrange("p (h n) -> p h n", n=3)[:, :, 0]
                dve.add(nc.vector.tensor_scalar(gc, gc, col("cmp_valid")[:, t:t + 1], None, ALU.mult))
            rotate_vector(dve, name, jobs, t1, (4, 5, 6, 7))
            dve.eng.wait_ge(sem(f"{name}_rotated"), 8)
            for n, (src, pos) in enumerate([(cmpk, "pos_k"), (cmpv, "pos_v")]):
                for l in range(LP):
                    ins = nc.vector.tensor_scalar(
                        blk[:, n, l, :].rearrange("p (g c) -> p g c", g=KV2),
                        src[:, :, 2 * l:2 * l + CMP_STRIDE * (NCMP - 1) + 1:CMP_STRIDE],
                        col(pos)[:, l:l + 1], None, ALU.add)
                ins.then_inc(S("blk"), 1)

        def scores(it):
            head, i = it // TT, it % TT
            half = slice(64 * (head % 2), 64 * (head % 2) + 64)
            g = head // G2
            W = (i + 1) * P
            qh = q[half, head // 2, i * P:(i + 1) * P]
            cm = cmpm_b[:, :].rearrange("p (t c) -> p t c", t=TT)
            for n, kr in enumerate((ksr, kwr)):
                nc.tensor.matmul(ps[:, it % 2, n * W:(n + 1) * W], qh, kr[half, g, 0:W], start=True, stop=False)
                nc.tensor.matmul(ps[:, it % 2, n * W + i * P:(n + 1) * W], ident_b[:, :], causal_b[:, :],
                                 start=False, stop=True)
            nc.tensor.matmul(ps[:, 2 + it % 2, 0:NCMP], qh, kcc[half, g * NCMP:(g + 1) * NCMP], start=True, stop=False)
            return nc.tensor.matmul(ps[:, 2 + it % 2, 0:NCMP], ident_b[:, :], cm[:, i, 0:NCMP], start=False, stop=True)

        def segments(it):
            W = (it % TT + 1) * P
            return [(it % 2, 0, W, 0), (it % 2, W, W, W), (2 + it % 2, 0, NCMP, 2 * W)]

        def factors(dve, it, rec):
            head, i = it // TT, it % TT
            dve.add(nc.vector.tensor_tensor(rec[:, 0:2], rec[:, 0:2], gates[:, i, 3 * head + 1:3 * head + 3], ALU.mult))
            dve.add(nc.vector.tensor_tensor(rec[:, 2:3], rec[:, 2:3], gates[:, i, 3 * head:3 * head + 1], ALU.mult))
            dve.settle()

        def values(it):
            head, i = it // TT, it % TT
            g = head // G2
            W = (i + 1) * P
            vals = [(n * W + j * P, P, v[:, j, n, g * HD:(g + 1) * HD]) for n in range(2) for j in range(i + 1)]
            return vals + [(2 * W, NCMP, vcc[0:NCMP, g, :])]

        def before(eng):
            eng.wait_ge(sem("nsa_in_rotated"), len(jobs))
            eng.wait_ge(S("kcc"), 1)
            eng.wait_ge(S("vcc"), 1)

        att = attention("nsa", H2 * TT, scores, segments, factors, values, HD ** -0.5,
                        before)
        return dict(name=name, tensor=tensor, scalar=scalar, vector=vector), att

    def moe():
        gbc, hid, t1, t2, lg, mx8, ix8, gT, gate, sm = carve(
            NEXP * T, F2 * T, 2 * T, 2 * T, TT * NEXP, TT * NEXP, TT * NEXP, T, TT * NEXP, 64)
        gbc = gbc.rearrange("p (e t) -> p e t", e=NEXP)
        hid = hid.rearrange("p (f t) -> p f t", f=F2)
        t1 = t1.rearrange("p (b t) -> p b t", b=2)
        t2 = t2.rearrange("p (b t) -> p b t", b=2)
        lg = lg.rearrange("p (t e) -> p t e", t=TT)
        mx8 = mx8.rearrange("p (t e) -> p t e", t=TT)
        ix8u = ix8.bitcast(U32).rearrange("p (t e) -> p t e", t=TT)
        gate = gate.rearrange("p (t e) -> p t e", t=TT)
        NU, ND = F2, F2 * DQ // DPS
        S = lambda s: sem(f"moe_{s}")

        def tensor(pe):
            eng = pe.eng
            rw = col("router").rearrange("p (k e) -> p k e", k=KD)
            for k in range(KD):
                signals["ln3"].wait(eng, "x", k + 1)
            for t in range(TT):
                for k in range(KD):
                    mm = nc.tensor.matmul(ps[:, 7, t * NEXP:(t + 1) * NEXP], x[:, k, T + t * P:T + (t + 1) * P],
                                          rw[:, k, :], start=(k == 0), stop=(k == KD - 1))
            mm.then_inc(S("logits"), 1)
            eng.wait_ge(S("gate"), 1)
            for t in range(TT):
                mm = nc.tensor.transpose(ps[0:NEXP, 6, t * P:(t + 1) * P], gate[:, t, :], ident)
            mm.then_inc(S("gate_turn"), 1)
            eng.wait_ge(S("gT"), 1)
            for e in range(NEXP):
                mm = nc.tensor.matmul(ps[:, e // 2, (e % 2) * T:(e % 2 + 1) * T],
                                      ident[0:NEXP, e:e + 1].to_broadcast([NEXP, P]), gT[0:NEXP, :],
                                      start=True, stop=True)
            mm.then_inc(S("spread"), 1)
            first = pe.slots.n
            assert first == BASE["moe"]
            eng.wait_ge(S("gbc"), 1)
            with eng.Fori(0, NEXP) as e:
                def slot(i):
                    n = first + i
                    eng.wait_ge(weights_ready[n % NS], e * (16 * (NU + ND) // NS) + 16 * (n // NS + 1))
                    return ring[:, n % NS, :]

                for f in range(NU):
                    w = units(slot(f))
                    eng.wait_ge(S("hidden"), e * NU + (f + 1))
                    for c in range(2):
                        for k in range(KD):
                            mm = nc.tensor.matmul(ps[:, 2 * (f % 2) + c, 0:T], w[:, c, k, :], x[:, k, T:NTOK],
                                                  start=(k == 0), stop=(k == KD - 1))
                    mm.then_inc(slot_read, 1)
                eng.wait_ge(S("hidden"), e * NU + (NU + 2))
                w = None
                for qd in range(DQ):
                    eng.wait_ge(S("quarter"), e * DQ + (qd + 1))
                    for f in range(F2):
                        n = qd * F2 + f
                        if n % DPS == 0:
                            w = slot(NU + n // DPS).rearrange("p (n m c) -> p n m c", n=DPS, m=2)
                        for m in range(2):
                            mm = nc.tensor.matmul(ps[:, 4 + 2 * (qd % 2) + m, 0:T], w[:, n % DPS, m, :], hid[:, f, :],
                                                  start=(f == 0), stop=(f == F2 - 1))
                        if n % DPS == DPS - 1:
                            mm.then_inc(slot_read, 1)

        def scalar(act):
            eng = act.eng
            eng.wait_ge(S("logits"), 1)
            nc.scalar.activation(lg[:, :, :], ps[:, 7, 0:TT * NEXP].rearrange("p (t e) -> p t e", t=TT), ACT.Copy)\
              .then_inc(S("lg"), 1)
            eng.wait_ge(S("diff"), 1)
            nc.scalar.activation(sm[:, 2:4], sm[:, 0:2], ACT.Exp).then_inc(S("exp"), 1)
            eng.wait_ge(S("gate_turn"), 1)
            nc.scalar.activation(gT[0:NEXP, :], ps[0:NEXP, 6, 0:T], ACT.Copy).then_inc(S("gT"), 1)
            eng.wait_ge(S("spread"), 1)
            nc.scalar.activation(gbc[:, :, :], ps[:, 0:4, :].rearrange("p a (b t) -> p (a b) t", b=2), ACT.Copy)\
              .then_inc(S("gbc"), 1)
            first = BASE["moe"]
            with eng.Fori(0, NEXP) as e:
                for f in range(NU):
                    eng.wait_ge(slot_read, e * (NU + ND) + (first + f + 1))
                    eng.wait_ge(S("hidden"), e * NU + (f + 1))
                    nc.scalar.activation(t1[:, f % 2, :], ps[:, 2 * (f % 2), 0:T], ACT.Silu).then_inc(S("silu"), 1)

        def vector(dve):
            eng = dve.eng
            eng.wait_ge(S("lg"), 1)
            for t in range(TT):
                dve.add(nc.vector.max(mx8[:, t, :], lg[:, t, :]))
            dve.settle()
            for t in range(TT):
                dve.add(nc.vector.max_index(ix8u[:, t, :], mx8[:, t, :], lg[:, t, :]))
            dve.settle()
            nc.vector.tensor_tensor(sm[:, 0:2], mx8[:, :, 1], mx8[:, :, 0], ALU.subtract).then_inc(S("diff"), 1)
            dve.add(nc.vector.tensor_copy(sm[:, 4:8].rearrange("p (t n) -> p t n", t=TT), ix8u[:, :, 0:2]))
            eng.wait_ge(S("exp"), 1)
            dve.add(nc.vector.tensor_scalar(sm[:, 8:10], sm[:, 2:4], 1.0, None, ALU.add))
            dve.settle()
            dve.add(nc.vector.reciprocal(sm[:, 10:12], sm[:, 8:10]))
            dve.settle()
            dve.add(nc.vector.tensor_tensor(sm[:, 12:14], sm[:, 10:12], sm[:, 2:4], ALU.mult))
            dve.settle()
            for t in range(TT):
                dve.add(nc.vector.tensor_scalar(gate[:, t, :], col("iota"), sm[:, 4 + 2 * t:5 + 2 * t],
                                                sm[:, 10 + t:11 + t], ALU.is_equal, ALU.mult))
                dve.add(nc.vector.tensor_scalar(sm[:, 16 + 8 * t:24 + 8 * t], col("iota"), sm[:, 5 + 2 * t:6 + 2 * t],
                                                sm[:, 12 + t:13 + t], ALU.is_equal, ALU.mult))
            dve.settle()
            nc.vector.tensor_tensor(gate[:, :, :], gate[:, :, :], sm[:, 16:32].rearrange("p (t e) -> p t e", t=TT),
                                    ALU.add).then_inc(S("gate"), 1)
            signals["ln3"].wait(eng, "x", KD)
            for n in range(2):
                ins = nc.vector.tensor_scalar(x[:, 4 * n:4 * n + 4, 0:T], x[:, 4 * n:4 * n + 4, T:NTOK], ALPHA, None,
                                              ALU.mult)
                ins.then_inc(S("quarter"), 1)
            for n in range(2):
                nc.vector.memset(sm[:, 32 + n:33 + n], 0.0).then_inc(S("hidden"), 1)
            eng.wait_ge(S("gbc"), 1)
            first = BASE["moe"]
            with eng.Fori(0, NEXP) as e:
                for f in range(NU):
                    eng.wait_ge(S("silu"), e * NU + (f + 1))
                    eng.wait_ge(S("hidden"), e * NU + (f + 1))
                    nc.vector.tensor_tensor(t2[:, f % 2, :], t1[:, f % 2, :], ps[:, 2 * (f % 2) + 1, 0:T], ALU.mult)\
                      .then_inc(S("product"), 1)
                    eng.wait_ge(S("product"), e * NU + (f + 1))
                    nc.vector.tensor_tensor(hid[:, f, :], t2[:, f % 2, :], gbc[:, bass.ds(e, 1), :].rearrange("p o t -> p (o t)"),
                                            ALU.mult).then_inc(S("hidden"), 1)
                for qd in range(DQ):
                    eng.wait_ge(slot_read, e * (NU + ND) + (first + NU + -(-(qd + 1) * F2 // DPS)))
                    eng.wait_ge(S("quarter"), e * DQ + 2)
                    acc = x[:, 2 * qd:2 * qd + 2, 0:T]
                    b0 = 4 + 2 * (qd % 2)
                    nc.vector.tensor_tensor(acc, ps[:, b0:b0 + 2, 0:T], acc, ALU.add).then_inc(S("quarter"), 1)
            eng.wait_ge(S("quarter"), NEXP * DQ + 2)
            for k in range(KD):
                nc.vector.tensor_copy(x[:, k, T:NTOK], x[:, k, 0:T]).then_inc(S("x"), 1)

        return dict(name="moe", tensor=tensor, scalar=scalar, vector=vector)

    def add(*items):
        for s in items:
            stages.append(s)

    def done(name, key):
        return lambda eng, n=None: signals[name].wait(eng, key, KD if n is None else n)

    def mixer0_ready(eng):
        eng.wait_ge(sem("mix0_cat"), 4)
        eng.wait_ge(sem("mix0_cat_h"), 4)

    def moe_ready(eng, n):
        eng.wait_ge(sem("moe_x"), n)

    add(start(), ada0())
    add(modulate("mix0_mod", 0, 0, 0, lambda eng: eng.wait_ge(x_ready, 16)), mixer0())
    add(out_proj("mix0_out", "ab_out", 0, mixer0_ready, 0, 2))
    add(modulate("ffn0_mod", 0, 0, 3, done("mix0_out", "x")))
    add(ffn("ffn0", FC, 0, True, 0, 5, lambda pe, k: h_block_ready(pe, "ffn0_mod", 0, k), h))
    add(modulate("mla_mod", 1, 0, 0, done("ffn0", "x")), mla_proj(), mla_attention())
    add(out_proj("mla_out", "mla_out", T, done("mla_att", "pair"), 1, 2))
    add(modulate("ffn1_mod", 1, T, 3, done("mla_out", "x")))
    add(ffn("ffn1", FC, T, True, 1, 5, lambda pe, k: h_block_ready(pe, "ffn1_mod", T, k), h))
    add(*swa())
    add(out_proj("swa_out", "swa_out", T, done("swa", "pair")))
    add(layer_norm("ln1", done("swa_out", "x"), 0))
    add(ffn("swiglu", F2, T, False, None, None, lambda pe, k: signals["ln1"].wait(pe.eng, "x", k + 1), x))
    add(layer_norm("ln2", done("swiglu", "x"), 1))
    add(*nsa())
    add(out_proj("nsa_out", "nsa_out", T, done("nsa", "pair")))
    add(layer_norm("ln3", done("nsa_out", "x"), 2))
    add(moe())
    add(layer_norm("ln4", moe_ready, 3))
    final = "ln4"
    used = NSLOT
    if upto is not None:
        n = [s["name"] for s in stages].index(upto[0])
        stages = stages[:n + 1]
        final, used = upto[1], upto[2]

    class Engine:

        def __init__(self, eng, steps):
            self.eng = eng
            own = Steps(eng, steps)
            self.add, self.settle = own.add, own.settle
            self.slots = Slots(eng)

    def run(engine, part):
        for s in stages:
            if part in s:
                s[part](engine)

    with nc.Block() as block:

        @block.sync
        def _(sp):
            sp.dma_start(tab[:, :], table).then_inc(table_ready, 16)
            sp.dma_start(ring[:, 0, :], stream[0]).then_inc(weights_ready[0], 16)
            sp.dma_start(x[:, :, :], x_in).then_inc(x_ready, 16)
            for s in range(1, NS):
                sp.dma_start(ring[:, s, :], stream[s]).then_inc(weights_ready[s], 16)
            with sp.Fori(1, used // NS) as r:
                for s in range(NS):
                    sp.wait_ge(slot_read, r * NS + (s + 1 - NS))
                    sp.dma_start(ring[:, s, :], stream[bass.ds(r * NS + s, 1), :, :].rearrange("o p c -> (o p) c"))\
                      .then_inc(weights_ready[s], 16)
            for n in range(used // NS * NS, used):
                sp.wait_ge(slot_read, n + 1 - NS)
                sp.dma_start(ring[:, n % NS, :], stream[n]).then_inc(weights_ready[n % NS], 16)
            signals[final].wait(sp, "x", KD)
            sp.dma_start(out, x[:, :, T:NTOK] if upto is None else x[:, :, :]).then_inc(out_stored, 16)
            sp.wait_ge(out_stored, 16)

        @block.tensor
        def _(pe):
            run(Engine(pe, "tensor_steps"), "tensor")

        @block.scalar
        def _(act):
            run(Engine(act, "scalar_steps"), "scalar")

        @block.vector
        def _(dve):
            run(Engine(dve, "vector_steps"), "vector")

        @block.gpsimd
        def _(pool):
            run(Engine(pool, "gpsimd_steps"), "gpsimd")


def blocks(w):
    k, m = w.shape[0] // P, w.shape[1] // P
    return w.reshape(k, P, m, P).transpose(2, 1, 0, 3).reshape(m, P, k * P)


def slots_of(u):
    per = SLOT // u.shape[2]
    if u.shape[0] % per:
        u = np.concatenate([u, np.zeros((per - u.shape[0] % per,) + u.shape[1:], u.dtype)])
    return u.reshape(-1, per, P, u.shape[2]).transpose(0, 2, 1, 3).reshape(-1, P, SLOT)


def rows_of(w, k):
    n = w.shape[0] // (k * P)
    return w.reshape(n, k, P, w.shape[1]).transpose(0, 2, 1, 3).reshape(n, P, k * w.shape[1])


def pairs(g, v):
    a, b = blocks(g), blocks(v)
    return np.stack([a, b], 1).reshape(-1, P, a.shape[2])


def down(w):
    f = w.shape[0] // P
    return w.reshape(f, P, DQ, DUNIT).transpose(2, 0, 1, 3).reshape(DQ * f, P, DUNIT)


def weight_stream(i):
    ab = i["ab_w_in"][0]
    cuts = np.cumsum([0, 512, 512, 256, 256, 512, 512, 16])
    a, g, q, k, v, o, gt = (ab[:, cuts[n]:cuts[n + 1]] for n in range(7))
    gp = np.zeros((D, P), ab.dtype)
    for n in range(4):
        gp[:, 32 * n:32 * n + HEADS_M] = gt[:, HEADS_M * n:HEADS_M * (n + 1)]
    mi = i["mla_w_in"][0]
    uq, ukv = i["mla_w_uq"][0], i["mla_w_ukv"][0]
    sw = i["a_w_in_2"][0]
    ns = i["b_w_in_2"][0]
    qn, kc, vc, ks, vs, kw, vw = (ns[:, a:b] for a, b in
                                  [(0, 1024)] + [(1024 + 256 * n, 1280 + 256 * n) for n in range(6)])
    parts = {
        "ada0": [blocks(i["ada_w"][0])],
        "ada1": [blocks(i["ada_w"][1])],
        "ab": [pairs(a, g), np.concatenate([blocks(gp), np.zeros((1, P, UNIT), ab.dtype)]), blocks(q), blocks(k),
               rows_of(v, 4), blocks(o)],
        "ab_out": [blocks(i["ab_w_out"][0])],
        "mla_in": [blocks(mi[:, 0:QL]), blocks(mi[:, QL:QL + KVL])],
        "mla_uq": [rows_of(uq[:, 512 * n:512 * n + 512], 4) for n in range(3)],
        "mla_ukv": [np.concatenate([rows_of(ukv[:, 512 * n:512 * n + 512], 2) for n in range(4)])],
        "mla_out": [blocks(i["mla_w_out"][0])],
        "swa_in": [blocks(sw[:, 0:1280]), rows_of(sw[:, 1280:1536], 8)],
        "swa_out": [blocks(i["a_w_out_2"][0])],
        "swiglu_up": [pairs(i["ffn_w_gate_2"][0], i["ffn_w_up_2"][0])],
        "swiglu_down": [down(i["ffn_w_down_2"][0])],
        "nsa_in": [blocks(qn), blocks(kc), blocks(vc), blocks(ks), blocks(kw),
                   rows_of(np.concatenate([vs, vw], 1), 4)],
        "nsa_cmp": [blocks(i["b_cmp_k_w1_2"][0]), blocks(i["b_cmp_v_w1_2"][0])],
        "nsa_out": [blocks(i["b_w_out_2"][0])],
        "moe": sum(([pairs(i["moe_w_gate_2"][0][e], i["moe_w_up_2"][0][e]), down(i["moe_w_down_2"][0][e])]
                    for e in range(NEXP)), []),
    }
    for n in range(2):
        w = i["ffn_w_in"][n]
        parts[f"ffn{n}_up"] = [pairs(w[:, 0:FFN], w[:, FFN:2 * FFN])]
        parts[f"ffn{n}_down"] = [down(i["ffn_w_out"][n])]
    stream = np.zeros((NSLOT, P, SLOT), np.float32)
    for name, count in PLAN:
        at = BASE[name]
        for u in parts[name]:
            s = slots_of(u)
            stream[at:at + len(s)] = s
            at += len(s)
        assert at == BASE[name] + count, (name, at - BASE[name], count)
    return stream


def columns(v):
    return v.reshape(-1, P).T


def resident_table(i):
    t = np.zeros((P, NTAB), np.float32)

    def put(name, a):
        c, n = COL[name]
        a = np.asarray(a, np.float32).reshape(-1, n)
        t[0:a.shape[0], c:c + n] = a

    put("c", np.stack([columns(i["c_ctx"]), columns(i["c"][0])], 2))
    put("ada_b", np.concatenate([columns(i["ada_b"][n]) for n in range(2)], 1))
    put("conv_w", i["ab_conv_w"][0].T.reshape(4, P, TAPS).transpose(1, 0, 2))
    put("conv_b", columns(i["ab_conv_b"][0]))
    put("ln_g", columns(i["ab_ln_g"][0]))
    put("ln_b", columns(i["ab_ln_b"][0]))
    put("head_gain", columns(i["ab_head_gain"][0]))
    gb = np.zeros((P, 1), np.float32)
    for n in range(4):
        gb[32 * n:32 * n + HEADS_M, 0] = i["ab_gate_bias"][0][HEADS_M * n:HEADS_M * (n + 1)]
    put("gate_b", gb)
    put("q_norm", columns(i["mla_q_norm"][0]))
    put("kv_norm", columns(i["mla_kv_norm"][0]))
    put("q_gain", np.broadcast_to(i["mla_q_gain"][0], (P, QK_MLA)))
    put("k_gain", np.broadcast_to(i["mla_k_gain"][0], (P, QK_MLA)))
    put("ffn_cw", i["ffn_conv_w"].transpose(0, 2, 1).reshape(2, FC, P, 3).transpose(2, 0, 1, 3))
    put("ffn_cb", i["ffn_conv_b"].reshape(2, FC, P).transpose(2, 0, 1))
    put("kr_w", i["mla_w_in"][0][:, QL + KVL:].reshape(KD, P, ROPE).transpose(1, 0, 2))
    put("ng_w", i["b_w_in_2"][0][:, 2560:2608].reshape(KD, P, 48).transpose(1, 0, 2))
    w2k = i["b_cmp_k_w2_2"][0].reshape(2, P, HD).transpose(1, 0, 2)
    put("w2k", np.concatenate([w2k, w2k], 2))
    put("w2v", i["b_cmp_v_w2_2"][0].reshape(2, P, HD).transpose(1, 0, 2))
    put("router", i["moe_router_2"][0].reshape(KD, P, NEXP).transpose(1, 0, 2))
    put("sinks", np.broadcast_to(i["a_sinks_2"][0], (P, H2)))
    put("pos_k", i["b_cmp_pos_k_2"][0].reshape(LP, P).T)
    put("pos_v", i["b_cmp_pos_v_2"][0].reshape(LP, P).T)
    put("ln2_g", i["ln_gain_2"].reshape(4, KD, P).transpose(2, 0, 1))
    put("ln2_b", i["ln_bias_2"].reshape(4, KD, P).transpose(2, 0, 1))
    eye = np.eye(P, dtype=np.float32)
    put("ident", eye)
    for n in (1024, 512, 256):
        put(f"over{n}", np.full((P, P), 1.0 / n))
    turn = np.zeros((HD, HD), np.float32)
    for d in range(HD // 2):
        turn[d + HD // 2, d], turn[d, d + HD // 2] = -1.0, 1.0
    rot = np.zeros((P, P), np.float32)
    rot[0:HD, 0:HD] = rot[HD:, HD:] = turn
    put("rot", rot)
    for n in range(2):
        for name, m in (("dup", np.eye(HD)), ("rdup", turn)):
            a = np.zeros((P, P), np.float32)
            a[HD * n:HD * (n + 1)] = np.concatenate([m, m], 1)
            put(f"{name}{n}", a)
    f32 = np.float32
    inv = f32(1) / (f32(10000.0) ** (np.arange(0, HD, 2, dtype=f32) / f32(HD)))
    ang = (np.arange(T, dtype=f32)[:, None] * inv[None, :]).astype(f32)
    put("cos2", np.tile(np.cos(ang).T, (4, 1)))
    put("sin2", np.tile(np.sin(ang).T, (4, 1)))
    grid, half = 64, ROPE // 2
    row = np.repeat(np.arange(T // grid, dtype=f32), grid)
    pos = np.tile(np.arange(grid, dtype=f32), T // grid)
    inv = f32(10000.0) ** (-np.arange(0, half, 2, dtype=f32) / f32(half))
    ang = np.concatenate([row[:, None] * inv, pos[:, None] * inv], 1).astype(f32)
    put("cos1", np.cos(ang).reshape(TT, P, 16).transpose(1, 0, 2))
    put("sin1", np.sin(ang).reshape(TT, P, 16).transpose(1, 0, 2))
    a, b = np.arange(P)[:, None], np.arange(P)[None, :]
    put("causal", np.where(b <= a, 0.0, NEG))
    put("band", np.where(b > a, 0.0, NEG))
    put("m_mask", np.stack([np.where(a <= b, 0.0, NEG), np.where(a >= b, 0.0, NEG)], 1))
    end = CMP_STRIDE * np.arange(16) + CMP_LEN - 1
    q = np.arange(T).reshape(TT, P).T[:, :, None]
    ok = (end[None, None, :] <= q) & (np.arange(16) < NCMP)
    put("cmp_mask", np.where(ok, 0.0, NEG))
    put("cmp_valid", ok.any(2))
    put("iota", np.broadcast_to(np.arange(NEXP), (P, NEXP)))
    put("eps6", np.full((P, 1), 1e-6))
    put("eps5", np.full((P, 1), 1e-5))
    return t


def kernel(**inputs):
    import concourse.bacc as bacc
    from concourse.bass_utils import run_bass_kernel_spmd

    i = {n: np.asarray(a) for n, a in inputs.items()}
    tokens = np.concatenate([i["ctx"][0], i["x"][0]], 0)
    arrays = {
        "in_stream_dram": weight_stream(i),
        "in_table_dram": resident_table(i),
        "in_x_dram": np.ascontiguousarray(tokens.reshape(NTOK, KD, P).transpose(2, 1, 0)),
    }
    nc = bacc.Bacc("TRN2", target_bir_lowering=False, num_devices=1)
    args = [nc.dram_tensor(n, a.shape, F32, kind="ExternalInput").ap() for n, a in arrays.items()]
    out = nc.dram_tensor("out_dram", [P, KD, T], F32, kind="ExternalOutput").ap()
    program(nc, *args, out)
    r = run_bass_kernel_spmd(nc, [arrays], core_ids=[0])
    y = r.results[0]["out_dram"]
    return np.ascontiguousarray(y.transpose(2, 1, 0).reshape(1, T, D))
```

```python
import math

import numpy as np

import concourse.bass as bass
from concourse import mybir
from concourse.alu_op_type import AluOpType as ALU

F32 = mybir.dt.float32
F32R = mybir.dt.float32r
BF16 = mybir.dt.bfloat16
U32 = mybir.dt.uint32
ACT = mybir.ActivationFunctionType
AX = mybir.AxisListType

P = 128
D = 1024
KD = D // P
T = 256
TT = T // P
NTOK = 2 * T
CONV, TAPS = 512, 31
PAD = (TAPS - 1) // 2
HEADS_M, QK_M, V_M = 4, 64, 128
H_MLA, NOPE, ROPE, V_MLA = 16, 64, 32, 64
QK_MLA = NOPE + ROPE
QL, KVL = 512, 256
FFN = 2816
FC = FFN // P
H2, HD, KV2 = 16, 64, 4
G2 = H2 // KV2
FF2 = 3584
F2 = FF2 // P
NEXP = 8
ADA_CHUNKS = 6 * D // 512
EXTRA = (2 * T - 1) // (P + 1)
CMP_LEN, CMP_STRIDE, CMP_HID = 32, 16, 256
NCMP = (T - CMP_LEN) // CMP_STRIDE + 1
LP = CMP_LEN * HD // P
ALPHA = (2 * 2) ** 0.25
NEG = -1e30

NS = 3
SLOT = 2048
UNIT = KD * P
DUNIT = 256
UPS = SLOT // UNIT
DPS = SLOT // DUNIT
DQ = D // DUNIT

PLAN = [
    ("ada0", 24), ("ab", 11), ("ada1", 24), ("ab_out", 4),
    ("ffn0_up", FC), ("ffn0_down", FC * DQ // DPS),
    ("mla_in", 3), ("mla_uq", 3), ("mla_ukv", 2), ("mla_out", 4),
    ("ffn1_up", FC), ("ffn1_down", FC * DQ // DPS),
    ("swa_in", 6), ("swa_out", 4),
    ("swiglu_up", F2), ("swiglu_down", F2 * DQ // DPS),
    ("nsa_in", 10), ("nsa_cmp", 4), ("nsa_out", 4),
    ("moe", NEXP * (F2 + F2 * DQ // DPS)),
]
BASE = {}
NSLOT = 0
for _name, _count in PLAN:
    BASE[_name] = NSLOT
    NSLOT += _count

TABLE = [
    ("c", 16), ("ada_b", 96), ("conv_w", 4 * TAPS), ("conv_b", 4), ("ln_g", 4), ("ln_b", 4),
    ("head_gain", 4), ("gate_b", 1), ("q_norm", 4), ("kv_norm", 2), ("q_gain", QK_MLA),
    ("k_gain", QK_MLA), ("ffn_cw", 2 * FC * 3), ("ffn_cb", 2 * FC), ("kr_w", KD * ROPE),
    ("ng_w", KD * 48), ("w2k", 2 * P), ("w2v", 2 * HD), ("router", KD * NEXP), ("sinks", H2),
    ("pos_k", LP), ("pos_v", LP), ("ln2_g", 4 * KD), ("ln2_b", 4 * KD),
    ("ident", P), ("over1024", P), ("over512", P), ("over256", P),
    ("rot", P), ("dup0", P), ("dup1", P), ("rdup0", P), ("rdup1", P),
    ("cos2", T), ("sin2", T), ("cos1", TT * 16), ("sin1", TT * 16),
    ("m_mask", 2 * P), ("cmp_valid", TT), ("iota", P), ("before", P), ("eps6", 1), ("eps5", 1),
    ("causal", P), ("band", P), ("cmp_mask", TT * 16),
]
COL = {}
NTAB = 0
for _name, _count in TABLE:
    COL[_name] = (NTAB, _count)
    NTAB += _count

NRES = COL["causal"][0]
ARENA = 21280


def program(nc, stream, table, x_in, out, upto=None):
    ctx_sems = {}

    def sem(name):
        if name not in ctx_sems:
            ctx_sems[name] = nc.alloc_semaphore(name)
        return ctx_sems[name]

    ring = nc.alloc_sbuf_tensor("ring", [P, NS, SLOT], F32)
    x = nc.alloc_sbuf_tensor("x", [P, KD, NTOK], F32)
    h = nc.alloc_sbuf_tensor("h", [P, KD, NTOK], F32)
    tab = nc.alloc_sbuf_tensor("tab", [P, NRES], F32)
    mods = nc.alloc_sbuf_tensor("mods", [P, 2, 48, 2], F32)
    ada_rows = nc.alloc_sbuf_tensor("ada_rows", [34, 512], F32)
    silu_c = nc.alloc_sbuf_tensor("silu_c", [P, KD, 2], F32)
    ident_b = nc.alloc_sbuf_tensor("ident_b", [P, P], BF16)
    causal_b = nc.alloc_sbuf_tensor("causal_b", [P, P], BF16)
    band_b = nc.alloc_sbuf_tensor("band_b", [P, P], BF16)
    cmpm_b = nc.alloc_sbuf_tensor("cmpm_b", [P, TT * 16], BF16)
    arena = nc.alloc_sbuf_tensor("arena", [P, ARENA], F32)
    ps = nc.alloc_psum_tensor("ps", [P, 8, 512], F32)

    def col(name):
        a, n = COL[name]
        if a >= NRES:
            return arena[:, ARENA - NTAB + a:ARENA - NTAB + a + n]
        return tab[:, a:a + n]

    def carve(*sizes):
        at, found = 0, []
        for n in sizes:
            found.append(arena[:, at:at + n])
            at += n
        assert at <= ARENA, at
        return found

    ident = col("ident")
    table_ready, x_ready = sem("table_ready"), sem("x_ready")
    masks_ready, slot_read, out_stored = sem("masks_ready"), sem("slot_read"), sem("out_stored")
    weights_ready = [sem(f"weights_ready_{s}") for s in range(NS)]

    class Steps:

        def __init__(self, eng, name):
            self.eng, self.sem, self.n = eng, sem(name), 0

        def add(self, ins):
            ins.then_inc(self.sem, 1)
            self.n += 1
            return self.n

        def settle(self, n=None):
            self.eng.wait_ge(self.sem, self.n if n is None else n)

    class Slots:

        def __init__(self, pe):
            self.pe, self.n = pe, 0

        def take(self):
            s = self.n % NS
            self.pe.wait_ge(weights_ready[s], 16 * (self.n // NS + 1))
            self.n += 1
            return ring[:, s, :]

    taken = {}
    signals = {}

    class Signals:

        def __init__(self, kind, name, **adds):
            self.kind = kind
            self.base = {k: taken.get((kind, k), 0) for k in adds}
            for k, n in adds.items():
                taken[kind, k] = self.base[k] + n
            signals[name] = self

        def __getitem__(self, key):
            return sem(f"{self.kind}_{key}")

        def wait(self, eng, key, n):
            eng.wait_ge(self[key], self.base[key] + n)

    def slots_read(eng, stage, n):
        eng.wait_ge(slot_read, BASE[stage] + n)

    def units(slot):
        return slot.rearrange("p (u k c) -> p u k c", u=UPS, k=KD)

    PARTS = 12 * UNIT
    parts = nc.alloc_sbuf_tensor("parts", [P, PARTS], F32R)

    class Cut:

        def __init__(self, name, stage, W, nu):
            self.stage, self.nu = stage, nu
            self.buffers = nb = (PARTS - 2 * KD * W) // (2 * UNIT)
            at = KD * W
            self.x_lead = parts[:, 0:at].rearrange("p (k t) -> p k t", k=KD)
            self.x_rest = parts[:, at:2 * at].rearrange("p (k t) -> p k t", k=KD)
            w = parts[:, 2 * at:2 * at + 2 * nb * UNIT].rearrange("p (a b k c) -> p a b k c", a=2, b=nb, k=KD)
            self.w_lead, self.w_rest = w[:, 0], w[:, 1]
            self.G = Signals("cut", name + "_cut", x_lead=KD, x_rest=KD, lead=nu, rest=nu // 2, product=nu)

        def lead(self, act, g):
            if g >= self.nu:
                return
            n = BASE[self.stage] + g // UPS
            act.eng.wait_ge(weights_ready[n % NS], 16 * (n // NS + 1))
            if g >= self.buffers:
                self.G.wait(act.eng, "product", g - self.buffers + 1)
            nc.scalar.activation(self.w_lead[:, g % self.buffers], units(ring[:, n % NS, :])[:, g % UPS], ACT.Copy)\
              .then_inc(self.G["lead"], 1)

        def rest(self, dve, g):
            if g >= self.nu:
                return
            n = BASE[self.stage] + g // UPS
            self.G.wait(dve.eng, "lead", g + 1)
            nc.vector.tensor_tensor(self.w_rest[:, g % self.buffers], units(ring[:, n % NS, :])[:, g % UPS],
                                    self.w_lead[:, g % self.buffers].bitcast(F32), ALU.subtract)\
              .then_inc(slot_read if g % UPS == UPS - 1 else self.G["rest"], 1)

        def input_lead(self, act, k, src):
            nc.scalar.activation(self.x_lead[:, k, :], src, ACT.Copy).then_inc(self.G["x_lead"], 1)

        def input_rest(self, dve, k, src):
            self.G.wait(dve.eng, "x_lead", k + 1)
            nc.vector.tensor_tensor(self.x_rest[:, k, :], src, self.x_lead[:, k, :].bitcast(F32), ALU.subtract)\
              .then_inc(self.G["x_rest"], 1)

        def unit(self, pe, g, dst, t0=0):
            if g % UPS == UPS - 1:
                slots_read(pe.eng, self.stage, g // UPS + 1)
            else:
                assert pe.slots.n == BASE[self.stage] + g // UPS
                pe.slots.n += 1
                self.G.wait(pe.eng, "rest", g // UPS + 1)
            wl, wr = self.w_lead[:, g % self.buffers], self.w_rest[:, g % self.buffers]
            for k in range(KD):
                if g == 0:
                    self.G.wait(pe.eng, "x_rest", k + 1)
                xl, xr = self.x_lead[:, k, t0:], self.x_rest[:, k, t0:]
                nc.tensor.matmul(dst, wl[:, k, :], xl, start=(k == 0), stop=False)
                nc.tensor.matmul(dst, wl[:, k, :], xr, start=False, stop=False)
                mm = nc.tensor.matmul(dst, wr[:, k, :], xl, start=False, stop=(k == KD - 1))
            mm.then_inc(self.G["product"], 1)

        def done(self, eng, g):
            self.G.wait(eng, "product", g)

    stages = []

    def start():
        def scalar(act):
            act.eng.wait_ge(table_ready, 16)
            nc.scalar.activation(silu_c[:, :, :], col("c").rearrange("p (k s) -> p k s", k=KD),
                                 ACT.Silu).then_inc(sem("silu_c_ready"), 1)

        def vector(dve):
            dve.eng.wait_ge(table_ready, 16)
            dve.eng.wait_ge(sem("start_masks_in"), 16)
            nc.vector.tensor_copy(ident_b[:, :], ident)
            nc.vector.tensor_copy(causal_b[:, :], col("causal"))
            nc.vector.tensor_copy(band_b[:, :], col("band"))
            nc.vector.tensor_copy(cmpm_b[:, :], col("cmp_mask")).then_inc(masks_ready, 1)

        def tensor(pe):
            pe.eng.wait_ge(table_ready, 16)

        return dict(name="start", scalar=scalar, vector=vector, tensor=tensor)

    def ada_row_bank(layer, chunk):
        return chunk % 2 if layer == 0 else 7

    def ada_columns(layer):
        return ps[:, 7, 0:96] if layer == 0 else ps[:, 5, 400:496]

    def ada_products(pe, layer, first, count):
        if first == 0:
            pe.eng.wait_ge(sem("silu_c_ready"), 1)
            if layer == 1:
                pe.eng.wait_ge(sem("mods0_ready"), 1)
        for s in range(first, first + count):
            chunk, half = s // 2, s % 2
            free = chunk - 1 if layer == 0 else chunk
            if half == 0 and free > 0:
                pe.eng.wait_ge(sem(f"ada{layer}_row"), free)
            w = pe.slots.take().rearrange("p (k c) -> p k c", k=4)
            for k in range(4):
                mm = nc.tensor.matmul(ps[0:2, ada_row_bank(layer, chunk), :], silu_c[:, 4 * half + k, :], w[:, k, :],
                                      start=(half == 0 and k == 0), stop=(half == 1 and k == 3))
            mm.then_inc(slot_read, 1)

    def ada_turns(pe, layer, first, count):
        for chunk in range(first, first + count):
            pe.eng.wait_ge(sem(f"ada{layer}_row"), chunk + 1)
            if chunk:
                pe.eng.wait_ge(sem(f"ada{layer}_turned"), chunk)
            g = 32 * (chunk % 2)
            for j in range(4):
                blk = 4 * chunk + j
                mm = nc.tensor.transpose(ada_columns(layer)[:, 2 * blk:2 * blk + 2],
                                         ada_rows[g:g + 2, j * P:(j + 1) * P], ident[g:g + 2, g:g + 2])
            mm.then_inc(sem(f"ada{layer}_turned"), 1)

    def ada_rows_out(eng, copy, layer, first, count):
        for chunk in range(first, first + count):
            slots_read(eng, f"ada{layer}", 2 * (chunk + 1))
            if chunk >= 2:
                eng.wait_ge(sem(f"ada{layer}_turned"), chunk - 1)
            g = 32 * (chunk % 2)
            copy(ada_rows[g:g + 2, :], ps[0:2, ada_row_bank(layer, chunk), :]).then_inc(sem(f"ada{layer}_row"), 1)

    def ada_vectors(dve, layer):
        dve.eng.wait_ge(sem(f"ada{layer}_turned"), ADA_CHUNKS)
        b = col("ada_b").rearrange("p (l j o) -> p l j o", l=2, o=1)[:, layer]
        dve.add(nc.vector.tensor_tensor(mods[:, layer, :, :], ada_columns(layer).rearrange("p (j s) -> p j s", s=2),
                                        b.to_broadcast([P, 48, 2]), ALU.add))
        dve.settle()
        v = mods[:, layer, :, :].rearrange("p (a b) s -> p a b s", a=2)[:, :, 8:16, :]
        nc.vector.tensor_scalar(v, v, 1.0, None, ALU.add).then_inc(sem(f"mods{layer}_ready"), 1)

    def ada0(norm_products, norm_scaling):
        def tensor(pe):
            for chunk in range(ADA_CHUNKS):
                if chunk == ADA_CHUNKS // 2:
                    norm_products(pe)
                ada_products(pe, 0, 2 * chunk, 2)
                if chunk:
                    ada_turns(pe, 0, chunk - 1, 1)
            ada_turns(pe, 0, ADA_CHUNKS - 1, 1)

        def vector(dve):
            most = ADA_CHUNKS - 2
            ada_rows_out(dve.eng, nc.vector.tensor_copy, 0, 0, most)
            norm_scaling(dve)
            ada_rows_out(dve.eng, nc.vector.tensor_copy, 0, most, ADA_CHUNKS - most)
            ada_vectors(dve, 0)

        return dict(name="ada0", tensor=tensor, vector=vector)

    def modulate(name, layer, c0, shift, after):
        W = NTOK - c0
        G = Signals("norm", name, square=KD, meansq=1, std=1, scaled=KD, h=KD * (2 if c0 == 0 else 1))
        segs = [(0, 0), (T, 1)] if c0 == 0 else [(T, 1)]
        sq, std, rstd, tmp = carve(KD * W, W, W, KD * W)
        sq = sq.rearrange("p (k t) -> p k t", k=KD)
        tmp = tmp.rearrange("p (k t) -> p k t", k=KD)

        def scalar(act):
            after(act.eng)
            for k in range(KD):
                nc.scalar.activation(sq[:, k, :], x[:, k, c0:NTOK], ACT.Square)\
                  .then_inc(G["square"], 1)
            G.wait(act.eng, "meansq", 1)
            nc.scalar.activation(std, ps[:, 6, 0:W], ACT.Sqrt, bias=col("eps6")).then_inc(G["std"], 1)
            act.eng.wait_ge(sem(f"mods{layer}_ready"), 1)
            for k in range(KD):
                G.wait(act.eng, "scaled", k + 1)
                for t0, s in segs:
                    nc.scalar.activation(h[:, k, t0:t0 + T], tmp[:, k, t0 - c0:t0 - c0 + T], ACT.Identity,
                                         scale=mods[:, layer, (shift + 1) * 8 + k, s:s + 1],
                                         bias=mods[:, layer, shift * 8 + k, s:s + 1])\
                      .then_inc(G["h"], 1)

        def tensor(pe):
            for k in range(KD):
                G.wait(pe.eng, "square", k + 1)
                mm = nc.tensor.matmul(ps[:, 6, 0:W], col("over1024"), sq[:, k, :],
                                      start=(k == 0), stop=(k == KD - 1))
            mm.then_inc(G["meansq"], 1)

        def vector(dve):
            after(dve.eng)
            G.wait(dve.eng, "std", 1)
            dve.add(nc.vector.reciprocal(rstd, std))
            dve.settle()
            for k in range(KD):
                nc.vector.tensor_tensor(tmp[:, k, :], x[:, k, c0:NTOK], rstd, ALU.mult)\
                  .then_inc(G["scaled"], 1)

        return dict(name=name, tensor=tensor, scalar=scalar, vector=vector)

    def h_block_ready(pe, name, c0, k):
        signals[name].wait(pe.eng, "h", (k + 1) * (2 if c0 == 0 else 1))

    def mixer0():
        UW = T + 2 * PAD
        (u0, u, qk, v1, sig_o, gi, lfs, cum, rows, mx, neg, zero, gcol, ecol, dg, dec, hs, tmp) = carve(
            4 * 2 * UW, 4 * NTOK, 4 * NTOK, 4 * HEADS_M * (V_M + 1), 4 * NTOK, NTOK, NTOK, NTOK, NTOK,
            NTOK, NTOK, NTOK, 4 * P, 32, 4 * P, 2 * 4 * NTOK // 2 * 1, 4 * NTOK, 4 * NTOK)
        u0 = u0.rearrange("p (b s t) -> p b s t", b=4, s=2)
        u = u.rearrange("p (b t) -> p b t", b=4)
        qk = qk.rearrange("p (b t) -> p b t", b=4)
        v1 = v1.rearrange("p (t h v) -> p t h v", t=4, h=HEADS_M)
        sig_o = sig_o.rearrange("p (b t) -> p b t", b=4)
        gcol = gcol.rearrange("p (t r) -> p t r", t=4)
        ecol = ecol.rearrange("p (t d h) -> p t d h", t=4, d=2)
        dg = dg.rearrange("p (j t) -> p j t", j=4)
        dec = dec.rearrange("p (j t) -> p j t", j=4)
        hs = hs.rearrange("p (t h v) -> p t h v", t=4, h=HEADS_M)
        tmp4 = tmp.rearrange("p (t h v) -> p t h v", t=4, h=HEADS_M)
        sg = tmp.rearrange("p (b t) -> p b t", b=4)
        sm = col("m_mask").rearrange("p (d t) -> p d t", d=2)
        small = nc.alloc_sbuf_tensor("m_small", [P, 64], F32)
        spans = {0: {0: [(0, 4)], 1: [(1, 4)], 2: [(2, 4)], 3: [(3, 4)]},
                 1: {0: [(0, 1), (2, 4)], 1: [(0, 4)], 2: [(2, 3)], 3: [(2, 4)]}}
        off = {0: {0: [(1, 4)], 1: [(2, 4)], 2: [(3, 4)], 3: []},
               1: {0: [(2, 4)], 1: [(0, 1), (2, 4)], 2: [], 3: [(2, 3)]}}
        sources = {d: {t: [j for j in range(4) if any(a <= t < b for a, b in spans[d][j])]
                       for t in range(4)} for d in (0, 1)}
        name = "mix0"
        C = Cut(name, "ab", NTOK, 8)

        def tensor(pe):
            eng = pe.eng
            for b in range(4):
                if b >= 2:
                    eng.wait_ge(sem("conv_in_ready"), b - 1)
                for c in range(2):
                    C.unit(pe, 2 * b + c, ps[:, 2 * (b % 2) + c, :])
            w = units(pe.slots.take())
            for k in range(KD):
                mm = nc.tensor.matmul(ps[:, 4, :], w[:, 0, k, :], h[:, k, :], start=(k == 0), stop=(k == KD - 1))
            mm.then_inc(slot_read, 1)
            for s, banks in enumerate([(5, 6), (0, 1)]):
                w = units(pe.slots.take())
                if s == 1:
                    eng.wait_ge(sem("conv_in_ready"), 3)
                for c in range(2):
                    for k in range(KD):
                        mm = nc.tensor.matmul(ps[:, banks[c], :], w[:, c, k, :], h[:, k, :],
                                              start=(k == 0), stop=(k == KD - 1))
                mm.then_inc(slot_read, 1)
            eng.wait_ge(sem("conv_in_ready"), 4)
            eng.wait_ge(sem("m_qk_ready"), 2)
            for s in range(2):
                w = pe.slots.take().rearrange("p (k c) -> p k c", k=4)
                for t, bank in enumerate((2, 3, 5, 6)):
                    for k in range(4):
                        mm = nc.tensor.matmul(ps[:, bank, :], h[:, 4 * s + k, t * P:(t + 1) * P], w[:, k, :],
                                              start=(s == 0 and k == 0), stop=(s == 1 and k == 3))
                mm.then_inc(slot_read, 1)
            eng.wait_ge(sem("m_qk_ready"), 4)
            eng.wait_ge(sem("gates_taken"), 1)
            eng.wait_ge(sem("m_v_ready"), 1)
            for s, banks in enumerate([(0, 1), (4, 2)]):
                w = units(pe.slots.take())
                for c in range(2):
                    for k in range(KD):
                        mm = nc.tensor.matmul(ps[:, banks[c], :], w[:, c, k, :], h[:, k, :],
                                              start=(k == 0), stop=(k == KD - 1))
                mm.then_inc(slot_read, 1)
            eng.wait_ge(sem("m_v_ready"), 4)
            eng.wait_ge(sem("m_rows_ready"), 1)
            for t in range(4):
                mm = nc.tensor.transpose(ps[:, 3, t * P:(t + 1) * P], rows[:, t * P:(t + 1) * P], ident)
            mm.then_inc(sem("m_cols_done"), 1)
            for i in range(2 * HEADS_M):
                hd, d = i // 2, i % 2
                half = slice(64 * (hd % 2), 64 * (hd % 2) + 64)
                rr = slice(64 * d, 64 * d + HEADS_M)
                if i == 0:
                    eng.wait_ge(sem("m_sig_o_ready"), 4)
                    eng.wait_ge(sem("m_gcol_ready"), 1)
                if d == 0:
                    if i:
                        eng.wait_ge(sem("m_weights_ready"), i)
                    for j in range(4):
                        t0 = 0 if j < 2 else T
                        mm = nc.tensor.matmul(ps[:, j, t0:NTOK], qk[half, 2 + hd // 2, j * P:(j + 1) * P],
                                              qk[half, hd // 2, t0:NTOK], start=True, stop=True)
                if i:
                    eng.wait_ge(sem("m_decay_ready"), i)
                mm = nc.tensor.matmul(ps[:, 4, :], ident[rr, 64 * d + hd:64 * d + hd + 1].to_broadcast([HEADS_M, P]),
                                      neg[rr, :], start=True, stop=True)
                mm.then_inc(sem("m_scores_done"), 1)
                ada_products(pe, 1, 3 * i, 3)
                eng.wait_ge(sem("m_weights_ready"), i + 1)
                if i:
                    eng.wait_ge(sem("m_h_taken"), i)
                ada_turns(pe, 1, 3 * i // 2, 3 * (i + 1) // 2 - 3 * i // 2)
                for t in range(4):
                    src = sources[d][t]
                    for n, j in enumerate(src):
                        c = (t % 2) * 256
                        mm = nc.tensor.matmul(ps[:, 5 + t // 2, c:c + V_M + 1], dec[:, j, t * P:(t + 1) * P],
                                              v1[:, j, hd, :], start=(n == 0), stop=(n == len(src) - 1))
                mm.then_inc(sem("m_h_done"), 1)
            eng.wait_ge(sem("conv_done"), 1)
            eng.wait_ge(sem("mods1_ready"), 1)
            for b in range(4):
                mm = nc.tensor.matmul(ps[:, 7, :], col("over512"), u[:, b, :], start=(b == 0), stop=(b == 3))
            mm.then_inc(sem("conv_mean_done"), 1)
            for b in range(4):
                eng.wait_ge(sem("conv_square_ready"), b + 1)
                mm = nc.tensor.matmul(ps[:, 4, :], col("over512"), sg[:, b, :], start=(b == 0), stop=(b == 3))
            mm.then_inc(sem("conv_var_done"), 1)
            eng.wait_ge(sem("m_hs_ready"), 1)
            for hd in range(HEADS_M):
                for t in range(4):
                    mm = nc.tensor.transpose(ps[:, hd, t * P:(t + 1) * P], hs[:, t, hd, :], ident)
                mm.then_inc(sem("m_hT_done"), 1)

        def scalar(act):
            eng = act.eng
            C.lead(act, 0)
            for k in range(KD):
                h_block_ready(act, name + "_mod", 0, k)
                C.input_lead(act, k, h[:, k, :])
            C.lead(act, 1)
            for b in range(4):
                for c in range(2):
                    C.lead(act, 2 * b + C.buffers + c)
                C.done(eng, 2 * b + 2)
                nc.scalar.activation(sg[:, b, :], ps[:, 2 * (b % 2) + 1, :], ACT.Sigmoid)\
                  .then_inc(sem("conv_gate_ready"), 1)
            slots_read(eng, "ab", 5)
            nc.scalar.activation(gi, ps[:, 4, :], ACT.Identity, bias=col("gate_b")).then_inc(sem("gates_taken"), 1)
            eng.wait_ge(sem("gates_taken"), 1)
            act.add(nc.scalar.activation(lfs, gi, ACT.Abs))
            act.settle()
            act.add(nc.scalar.activation(rows, lfs, ACT.Exp, scale=-1.0))
            act.settle()
            nc.scalar.activation(lfs, rows, ACT.Ln, bias=1.0).then_inc(sem("m_ln_ready"), 1)
            for n, bank in enumerate((5, 6, 0, 1)):
                slots_read(eng, "ab", 6 + n // 2)
                nc.scalar.activation(qk[:, n, :], ps[:, bank, :], ACT.Copy,
                                     scale=(1.0 if n < 2 else QK_M ** -0.5)).then_inc(sem("m_qk_ready"), 1)
            slots_read(eng, "ab", 9)
            for t, bank in enumerate((2, 3, 5, 6)):
                nc.scalar.activation(v1[:, t, :, 0:V_M], ps[:, bank, :].rearrange("p (h v) -> p h v", h=HEADS_M),
                                     ACT.Copy).then_inc(sem("m_v_ready"), 1)
            for n, bank in enumerate((0, 1, 4, 2)):
                slots_read(eng, "ab", 10 + n // 2)
                nc.scalar.activation(sig_o[:, n, :], ps[:, bank, :], ACT.Sigmoid).then_inc(sem("m_sig_o_ready"), 1)
            eng.wait_ge(sem("m_cols_done"), 1)
            nc.scalar.activation(gcol[:, :, :], ps[:, 3, :].rearrange("p (t r) -> p t r", t=4), ACT.Copy)\
              .then_inc(sem("m_gcol_ready"), 1)
            eng.wait_ge(sem("m_gcol_ready"), 1)
            for d in range(2):
                ins = nc.scalar.activation(ecol[:, :, d, :], gcol[:, :, 32 + 64 * d:32 + 64 * d + HEADS_M], ACT.Exp)
            ins.then_inc(sem("m_ecol_ready"), 1)
            for i in range(2 * HEADS_M):
                hd, d = i // 2, i % 2
                eng.wait_ge(sem("m_scores_done"), i + 1)
                if i:
                    eng.wait_ge(sem("m_h_done"), i)
                eng.wait_ge(sem("m_diag_ready"), i + 1)
                for j in range(4):
                    bias = gcol[:, j, 64 * d + hd:64 * d + hd + 1]
                    for a, b in off[d][j]:
                        nc.scalar.activation(dec[:, j, a * P:b * P], ps[:, 4, a * P:b * P], ACT.Exp, bias=bias)
                for j in range(4):
                    ins = nc.scalar.activation(dec[:, j, j * P:(j + 1) * P], dg[:, j, :], ACT.Exp,
                                               bias=gcol[:, j, 64 * d + hd:64 * d + hd + 1])
                ins.then_inc(sem("m_decay_ready"), 1)
                ada_rows_out(eng, lambda o, v: nc.scalar.activation(o, v, ACT.Copy), 1,
                             3 * i // 2, 3 * (i + 1) // 2 - 3 * i // 2)
            for b in range(4):
                eng.wait_ge(sem("conv_centred"), b + 1)
                nc.scalar.activation(sg[:, b, :], u[:, b, :], ACT.Square).then_inc(sem("conv_square_ready"), 1)
            eng.wait_ge(sem("conv_var_done"), 1)
            nc.scalar.activation(gi, ps[:, 4, :], ACT.Sqrt, bias=col("eps6")).then_inc(sem("conv_std_ready"), 1)
            eng.wait_ge(sem("m_ss_ready"), 1)
            nc.scalar.activation(small[:, 16:32], small[:, 0:16], ACT.Sqrt, scale=1.0 / V_M, bias=col("eps6"))\
              .then_inc(sem("m_rms_ready"), 1)
            for b in range(4):
                eng.wait_ge(sem("conv_scaled"), b + 1)
                nc.scalar.activation(h[:, b, :], u[:, b, :], ACT.Silu, scale=col("ln_g")[:, b:b + 1],
                                     bias=col("ln_b")[:, b:b + 1]).then_inc(sem("mix0_cat"), 1)

        def gpsimd(pool):
            signals["mix0_mod"].wait(pool.eng, "h", 2 * KD)
            nc.gpsimd.memset(u0[:, :, :, 0:PAD], 0.0)
            nc.gpsimd.memset(u0[:, :, :, PAD + T:UW], 0.0)
            nc.gpsimd.memset(v1[:, :, :, V_M:V_M + 1], 1.0)
            nc.gpsimd.memset(zero, 0.0).then_inc(sem("m_borders_ready"), 1)

        def vector(dve):
            eng = dve.eng
            eng.wait_ge(sem("m_borders_ready"), 1)
            C.rest(dve, 0)
            for k in range(KD):
                C.input_rest(dve, k, h[:, k, :])
            C.rest(dve, 1)
            for b in range(4):
                for c in range(2):
                    C.rest(dve, 2 * b + C.buffers + c)
                eng.wait_ge(sem("conv_gate_ready"), b + 1)
                nc.vector.tensor_tensor(u0[:, b, :, PAD:PAD + T],
                                        ps[:, 2 * (b % 2), :].rearrange("p (s t) -> p s t", s=2),
                                        sg[:, b, :].rearrange("p (s t) -> p s t", s=2), ALU.mult)\
                  .then_inc(sem("conv_in_ready"), 1)
            eng.wait_ge(sem("m_ln_ready"), 1)
            dve.add(nc.vector.tensor_scalar(mx, gi, 0.0, None, ALU.min))
            dve.settle()
            dve.add(nc.vector.tensor_tensor(mx, mx, lfs, ALU.subtract))
            dve.settle()
            dve.add(nc.vector.tensor_copy(lfs[0:4, :], mx[32:36, :]))
            dve.add(nc.vector.tensor_copy(lfs[64:68, :], mx[96:100, :]))
            dve.settle()
            f, g = slice(0, 4), slice(64, 68)
            ctx_r, lat_r = slice(T - 1, None, -1), slice(NTOK - 1, T - 1, -1)
            dve.add(nc.vector.memset(rows, 0.0))
            dve.add(nc.vector.tensor_tensor_scan(cum[f, :], lfs[f, :], zero[f, :], 0.0, ALU.add, ALU.add))
            dve.add(nc.vector.tensor_tensor_scan(cum[g, ctx_r], lfs[g, ctx_r], zero[g, ctx_r], 0.0, ALU.add, ALU.add))
            dve.settle()
            dve.add(nc.vector.tensor_tensor_scan(cum[g, lat_r], lfs[g, lat_r], zero[g, lat_r], cum[g, 0:1],
                                                 ALU.add, ALU.add))
            dve.settle()
            for r in (f, g):
                dve.add(nc.vector.tensor_tensor(rows[r, :], gi[r, :], cum[r, :], ALU.subtract))
            dve.settle()
            dve.add(nc.vector.tensor_tensor_scan(mx[f, :], rows[f, :], rows[f, :], 0.0, ALU.max, ALU.max))
            dve.add(nc.vector.tensor_tensor_scan(mx[g, ctx_r], rows[g, ctx_r], rows[g, ctx_r], 0.0, ALU.max, ALU.max))
            dve.settle()
            dve.add(nc.vector.tensor_tensor_scan(mx[g, lat_r], rows[g, lat_r], rows[g, lat_r], mx[g, 0:1],
                                                 ALU.max, ALU.max))
            dve.settle()
            for r in (f, g):
                nc.vector.tensor_scalar(neg[r, :], mx[r, :], -1.0, None, ALU.mult)
            nc.vector.scalar_tensor_tensor(rows[32:36, :], cum[f, :], -1.0, mx[f, :], ALU.mult, ALU.subtract)
            nc.vector.scalar_tensor_tensor(rows[96:100, :], cum[g, :], -1.0, mx[g, :], ALU.mult, ALU.subtract)\
              .then_inc(sem("m_rows_ready"), 1)

            cw = col("conv_w").rearrange("p (b t) -> p b t", b=4)
            last = [0] * 4

            def taps(a, b_):
                for t in range(a, min(b_, TAPS)):
                    for b in range(4):
                        o = u[:, b, :].rearrange("p (s t) -> p s t", s=2)
                        i = u0[:, b, :, t:t + T]
                        if t == 0:
                            last[b] = dve.add(nc.vector.tensor_scalar(o, i, cw[:, b, 0:1], col("conv_b")[:, b:b + 1],
                                                                      ALU.mult, ALU.add))
                        else:
                            dve.settle(last[b])
                            last[b] = dve.add(nc.vector.scalar_tensor_tensor(o, i, cw[:, b, t:t + 1], o,
                                                                             ALU.mult, ALU.add))

            eng.wait_ge(sem("conv_in_ready"), 4)
            taps(0, 3)
            for i in range(2 * HEADS_M):
                hd, d = i // 2, i % 2
                eng.wait_ge(sem("m_scores_done"), i + 1)
                if i:
                    eng.wait_ge(sem("m_decay_ready"), i)
                nc.vector.tensor_tensor(dg[:, :, :], ps[:, 4, :].rearrange("p (j t) -> p j t", j=4),
                                        sm[:, d:d + 1, :].to_broadcast([P, 4, P]), ALU.add)\
                  .then_inc(sem("m_diag_ready"), 1)
                taps(3 + 4 * i, 5 + 4 * i)
                eng.wait_ge(sem("m_decay_ready"), i + 1)
                for j in range(4):
                    for a, b in spans[d][j]:
                        ins = nc.vector.tensor_tensor(dec[:, j, a * P:b * P], dec[:, j, a * P:b * P],
                                                      ps[:, j, a * P:b * P], ALU.mult)
                ins.then_inc(sem("m_weights_ready"), 1)
                taps(5 + 4 * i, 7 + 4 * i)
                eng.wait_ge(sem("m_h_done"), i + 1)
                if i == 0:
                    eng.wait_ge(sem("m_ecol_ready"), 1)
                o = ps[:, 5:7, :].rearrange("p a (b c) -> p (a b) c", b=2)
                sc = small[:, 32:36].rearrange("p (t o) -> p t o", o=1)
                sc2 = small[:, 36:40].rearrange("p (t o) -> p t o", o=1)
                dve.add(nc.vector.tensor_scalar(sc, o[:, :, V_M:V_M + 1], -1.0, None, ALU.mult))
                dve.settle()
                dve.add(nc.vector.tensor_tensor(sc, o[:, :, V_M:V_M + 1], sc, ALU.max))
                dve.settle()
                dve.add(nc.vector.tensor_tensor(sc, sc, ecol[:, :, d, hd:hd + 1], ALU.max))
                dve.settle()
                dve.add(nc.vector.reciprocal(sc2, sc))
                dve.settle()
                dst = hs if d == 0 else tmp4
                nc.vector.tensor_tensor(dst[:, :, hd, :], o[:, :, 0:V_M], sc2.to_broadcast([P, 4, V_M]), ALU.mult)\
                  .then_inc(sem("m_h_taken"), 1)
                if d == 1:
                    eng.wait_ge(sem("m_h_taken"), i + 1)
                    dve.add(nc.vector.tensor_tensor(hs[:, :, hd, :], hs[:, :, hd, :], tmp4[:, :, hd, :], ALU.add))
            dve.settle()
            nc.vector.tensor_copy(small[:, 60:61], u[:, 3, 0:1]).then_inc(sem("conv_done"), 1)
            ada_vectors(dve, 1)
            dve.add(nc.vector.tensor_tensor(tmp, hs.rearrange("p t h v -> p (t h v)"),
                                            hs.rearrange("p t h v -> p (t h v)"), ALU.mult))
            dve.settle()
            nc.vector.tensor_reduce(small[:, 0:16], tmp.rearrange("p (g v) -> p g v", v=V_M), AX.X, ALU.add)\
              .then_inc(sem("m_ss_ready"), 1)
            eng.wait_ge(sem("conv_mean_done"), 1)
            eng.wait_ge(sem("m_ss_ready"), 1)
            for b in range(4):
                nc.vector.tensor_tensor(u[:, b, :], u[:, b, :], ps[:, 7, :], ALU.subtract)\
                  .then_inc(sem("conv_centred"), 1)
            eng.wait_ge(sem("m_rms_ready"), 1)
            dve.add(nc.vector.reciprocal(small[:, 0:16], small[:, 16:32]))
            dve.settle()
            hg = hs.rearrange("p t h v -> p (t h) v")
            nc.vector.tensor_tensor(hg, hg, small[:, 0:16].rearrange("p (g o) -> p g o", o=1).to_broadcast([P, 16, V_M]),
                                    ALU.mult).then_inc(sem("m_hs_ready"), 1)
            eng.wait_ge(sem("conv_std_ready"), 1)
            dve.add(nc.vector.reciprocal(lfs, gi))
            dve.settle()
            eng.wait_ge(sem("conv_square_ready"), 4)
            for b in range(4):
                nc.vector.tensor_tensor(u[:, b, :], u[:, b, :], lfs, ALU.mult).then_inc(sem("conv_scaled"), 1)
            for hd in range(HEADS_M):
                eng.wait_ge(sem("m_hT_done"), hd + 1)
                nc.vector.scalar_tensor_tensor(h[:, 4 + hd, :], ps[:, hd, :], col("head_gain")[:, hd:hd + 1],
                                               sig_o[:, hd, :], ALU.mult, ALU.mult).then_inc(sem("mix0_cat_h"), 1)

        return dict(name=name, tensor=tensor, scalar=scalar, vector=vector, gpsimd=gpsimd)

    def out_proj(name, plan, c0, ready, layer=None, gate=None, src=None):
        G = Signals("residual", name, x=KD)
        W = NTOK - c0
        src = h if src is None else src

        C = Cut(name, plan, W, KD)

        def tensor(pe):
            for m in range(KD):
                C.unit(pe, m, ps[:, m, 0:W])

        def scalar(act):
            for g in range(2):
                C.lead(act, g)
            ready(act.eng)
            for k in range(KD):
                C.input_lead(act, k, src[:, k, c0:NTOK])
            for g in range(2, KD):
                C.lead(act, g)

        def vector(dve):
            for g in range(2):
                C.rest(dve, g)
            for k in range(KD):
                C.input_rest(dve, k, src[:, k, c0:NTOK])
            for g in range(2, C.buffers):
                C.rest(dve, g)
            for m in range(KD):
                C.rest(dve, m + C.buffers)
                C.done(dve.eng, m + 1)
                residual(m, ps[:, m, 0:W], c0, layer, gate, G["x"])

        return dict(name=name, tensor=tensor, scalar=scalar, vector=vector)

    def residual(m, y, c0, layer, gate, signal):
        if gate is None:
            nc.vector.scalar_tensor_tensor(x[:, m, c0:NTOK], x[:, m, c0:NTOK], ALPHA, y, ALU.mult, ALU.add)\
              .then_inc(signal, 1)
            return
        segs = [(0, 0), (T, 1)] if c0 == 0 else [(T, 1)]
        for t0, s in segs:
            ins = nc.vector.scalar_tensor_tensor(x[:, m, t0:t0 + T], y[:, t0 - c0:t0 - c0 + T],
                                                 mods[:, layer, gate * 8 + m, s:s + 1], x[:, m, t0:t0 + T],
                                                 ALU.mult, ALU.add)
        ins.then_inc(signal, 1)

    def ffn(name, nblk, c0, conv, layer, gate, src_ready, src):
        W = NTOK - c0
        nseg = W // T
        G = Signals("ffn", name, hidden=nblk, conv=nblk if conv else 0, act=nblk)
        R = Signals("residual", name, x=KD)
        C = Cut(name, f"{name}_up", W, 2 * nblk)
        hid, t1, t2 = carve(nblk * W, 2 * W, 2 * W)
        hid = hid.rearrange("p (f t) -> p f t", f=nblk)
        t1 = t1.rearrange("p (b t) -> p b t", b=2)
        t2 = t2.rearrange("p (b t) -> p b t", b=2)
        cw = col("ffn_cw").rearrange("p (l f w) -> p l f w", l=2, w=3)
        cb = col("ffn_cb").rearrange("p (l f) -> p l f", l=2)

        def tensor(pe):
            for f in range(nblk):
                if f >= 2:
                    G.wait(pe.eng, "hidden", f - 1)
                for c in range(2):
                    C.unit(pe, 2 * f + c, ps[:, 2 * (f % 2) + c, 0:W])
            G.wait(pe.eng, "hidden", nblk)
            w = None
            for q in range(DQ):
                if q >= 2:
                    R.wait(pe.eng, "x", 2 * (q - 1))
                for f in range(nblk):
                    n = q * nblk + f
                    if n % DPS == 0:
                        w = pe.slots.take().rearrange("p (n m c) -> p n m c", n=DPS, m=2)
                    for m in range(2):
                        mm = nc.tensor.matmul(ps[:, 4 + 2 * (q % 2) + m, 0:W], w[:, n % DPS, m, :], hid[:, f, :],
                                              start=(f == 0), stop=(f == nblk - 1))
                    if n % DPS == DPS - 1:
                        mm.then_inc(slot_read, 1)

        def scalar(act):
            C.lead(act, 0)
            for k in range(KD):
                src_ready(act, k)
                C.input_lead(act, k, src[:, k, c0:NTOK])
            for g in range(1, C.buffers):
                C.lead(act, g)
            for f in range(nblk):
                for c in range(2):
                    C.lead(act, 2 * f + C.buffers + c)
                if conv:
                    G.wait(act.eng, "conv", f + 1)
                    nc.scalar.activation(t2[:, f % 2, :], t1[:, f % 2, :], ACT.Gelu_apprx_tanh)\
                      .then_inc(G["act"], 1)
                else:
                    C.done(act.eng, 2 * f + 2)
                    if f >= 2:
                        G.wait(act.eng, "hidden", f - 1)
                    nc.scalar.activation(t2[:, f % 2, :], ps[:, 2 * (f % 2), 0:W], ACT.Silu)\
                      .then_inc(G["act"], 1)

        def vector(dve):
            C.rest(dve, 0)
            for k in range(KD):
                C.input_rest(dve, k, src[:, k, c0:NTOK])
            for g in range(1, C.buffers):
                C.rest(dve, g)
            for f in range(nblk):
                for c in range(2):
                    C.rest(dve, 2 * f + C.buffers + c)
                C.done(dve.eng, 2 * f + 2)
                if conv:
                    g = ps[:, 2 * (f % 2), 0:W].rearrange("p (s t) -> p s t", s=nseg)
                    t = t1[:, f % 2, :].rearrange("p (s t) -> p s t", s=nseg)
                    dve.add(nc.vector.tensor_scalar(t, g, cw[:, layer, f, 1:2], cb[:, layer, f:f + 1],
                                                    ALU.mult, ALU.add))
                    dve.settle()
                    dve.add(nc.vector.scalar_tensor_tensor(t[:, :, 1:T], g[:, :, 0:T - 1], cw[:, layer, f, 0:1],
                                                           t[:, :, 1:T], ALU.mult, ALU.add))
                    dve.settle()
                    nc.vector.scalar_tensor_tensor(t[:, :, 0:T - 1], g[:, :, 1:T], cw[:, layer, f, 2:3],
                                                   t[:, :, 0:T - 1], ALU.mult, ALU.add)\
                      .then_inc(G["conv"], 1)
                G.wait(dve.eng, "act", f + 1)
                nc.vector.tensor_tensor(hid[:, f, :], t2[:, f % 2, :], ps[:, 2 * (f % 2) + 1, 0:W], ALU.mult)\
                  .then_inc(G["hidden"], 1)
            for q in range(DQ):
                slots_read(dve.eng, f"{name}_down", -(-(q + 1) * nblk // DPS))
                for m in range(2):
                    residual(2 * q + m, ps[:, 4 + 2 * (q % 2) + m, 0:W], c0, layer, gate, R["x"])

        return dict(name=name, tensor=tensor, scalar=scalar, vector=vector)

    def attention(name, n_it, scores, segments, factors, values, exp_scale, before):
        nseg = max(len(segments(i)) for i in range(n_it))
        G = Signals("attention", name, scores=n_it, max=n_it, exp=n_it, probs=n_it, turn=n_it, turned=n_it,
                    out=n_it, pair=n_it // (2 * TT))
        PW = 528
        base = ATT_BASE
        p = arena[:, base:base + 2 * PW].rearrange("p (b c) -> p b c", b=2)
        pt = arena[:, base + 2 * PW:base + 2 * PW + 2 * 640].rearrange("p (b j t) -> p b j t", b=2, j=5)
        st = arena[:, base + 2 * PW + 1280:base + 2 * PW + 1280 + 64].rearrange("p (b c) -> p b c", b=2)

        def tensor(pe):
            before(pe.eng)
            for step in range(n_it + 2):
                if step < n_it:
                    if step >= 2:
                        G.wait(pe.eng, "exp", step - 1)
                        G.wait(pe.eng, "turned", step - 1)
                    scores(step).then_inc(G["scores"], 1)
                if 1 <= step <= n_it:
                    it = step - 1
                    G.wait(pe.eng, "probs", it + 1)
                    if it >= 2:
                        G.wait(pe.eng, "turned", it - 1)
                    for j, (c, n, _) in enumerate(values(it)):
                        dst = ps[0:n, 4 + it % 2, j * P:(j + 1) * P] if j < 4 else ps[0:n, 2 + it % 2, P:2 * P]
                        mm = nc.tensor.transpose(dst, p[:, it % 2, c:c + n], ident)
                    mm.then_inc(G["turn"], 1)
                if step >= 2:
                    it = step - 2
                    head, i = it // TT, it % TT
                    pair = head // 2
                    G.wait(pe.eng, "turned", it + 1)
                    if pair >= 2 and head % 2 == 0 and i == 0:
                        G.wait(pe.eng, "pair", pair - 1)
                    vs = values(it)
                    for j, (c, n, v) in enumerate(vs):
                        mm = nc.tensor.matmul(ps[64 * (head % 2):64 * (head % 2) + 64, 6 + pair % 2, i * P:(i + 1) * P],
                                              v, pt[0:n, it % 2, j, :], start=(j == 0), stop=(j == len(vs) - 1))
                    mm.then_inc(G["out"], 1)

        def scalar(act):
            for step in range(n_it + 2):
                if step < n_it:
                    it = step
                    G.wait(act.eng, "max", it + 1)
                    if it >= 2:
                        G.wait(act.eng, "turn", it - 1)
                    segs = segments(it)
                    for n, (bank, c0, w, pc) in enumerate(segs):
                        ins = nc.scalar.activation(p[:, it % 2, pc:pc + w], ps[:, bank, c0:c0 + w], ACT.Exp,
                                                   scale=exp_scale, bias=st[:, it % 2, 4 + n:5 + n],
                                                   accum_out=st[:, it % 2, 8 + n:9 + n])
                        if n < len(segs) - 1:
                            continue
                        if name == "swa":
                            ins = nc.scalar.activation(st[:, it % 2, 12:13], col("sinks")[:, it // TT:it // TT + 1],
                                                       ACT.Exp, bias=st[:, it % 2, 4:5])
                        ins.then_inc(G["exp"], 1)
                if step >= 2:
                    it = step - 2
                    head, i = it // TT, it % TT
                    if head % 2 == 1 and i == TT - 1:
                        G.wait(act.eng, "out", it + 1)
                        nc.scalar.activation(h[:, head // 2, T:NTOK], ps[:, 6 + (head // 2) % 2, 0:T], ACT.Copy)\
                          .then_inc(G["pair"], 1)

        def vector(dve):
            for step in range(n_it + 2):
                if step >= 2:
                    it = step - 2
                    b = it % 2
                    G.wait(dve.eng, "turn", it + 1)
                    if it >= 2:
                        G.wait(dve.eng, "out", it - 1)
                    vs = values(it)
                    full = [j for j, (_, n, _) in enumerate(vs) if n == P]
                    ins = nc.vector.tensor_copy(pt[:, b, 0:len(full), :],
                                                ps[:, 4 + b, 0:len(full) * P].rearrange("p (j t) -> p j t", t=P))
                    for j, (c, n, _) in enumerate(vs):
                        if n != P:
                            srcp = ps[0:n, 4 + b, j * P:(j + 1) * P] if j < 4 else ps[0:n, 2 + b, P:2 * P]
                            ins = nc.vector.tensor_copy(pt[0:n, b, j, :], srcp)
                    ins.then_inc(G["turned"], 1)
                if 1 <= step <= n_it:
                    it = step - 1
                    b = it % 2
                    G.wait(dve.eng, "exp", it + 1)
                    if name == "swa":
                        dve.add(nc.vector.tensor_tensor(st[:, b, 8:9], st[:, b, 8:9], st[:, b, 12:13], ALU.add))
                        dve.settle()
                    dve.add(nc.vector.reciprocal(st[:, b, 16:16 + nseg], st[:, b, 8:8 + nseg]))
                    dve.settle()
                    factors(dve, it, st[:, b, 16:16 + nseg])
                    segs = segments(it)
                    for n, (bank, c0, w, pc) in enumerate(segs):
                        ins = nc.vector.tensor_scalar(p[:, b, pc:pc + w], p[:, b, pc:pc + w], st[:, b, 16 + n:17 + n],
                                                      None, ALU.mult)
                    ins.then_inc(G["probs"], 1)
                if step < n_it:
                    it = step
                    b = it % 2
                    G.wait(dve.eng, "scores", it + 1)
                    segs = segments(it)
                    n = 0
                    while n < len(segs):
                        bank, c0, w, _ = segs[n]
                        many = 2 if n + 1 < len(segs) and segs[n + 1][0] == bank else 1
                        dve.add(nc.vector.tensor_reduce(st[:, b, n:n + many],
                                                        ps[:, bank, c0:c0 + many * w].rearrange("p (a w) -> p a w", a=many),
                                                        AX.X, ALU.max))
                        n += many
                    dve.settle()
                    if name == "swa":
                        dve.add(nc.vector.tensor_scalar(st[:, b, 0:1], st[:, b, 0:1], exp_scale,
                                                        col("sinks")[:, it // TT:it // TT + 1], ALU.mult, ALU.max))
                        dve.settle()
                        neg_scale = -1.0
                    else:
                        neg_scale = -exp_scale
                    nc.vector.tensor_scalar(st[:, b, 4:4 + nseg], st[:, b, 0:nseg], neg_scale, None, ALU.mult)\
                      .then_inc(G["max"], 1)

        return dict(name=name, tensor=tensor, scalar=scalar, vector=vector)

    KT0, QT0, V0 = 0, H_MLA * NTOK, H_MLA * NTOK + H_MLA * T
    ATT_BASE = V0 + 4 * H_MLA * V_MLA

    def mla_proj():
        name = "mla"
        kT = arena[0:QK_MLA, KT0:QT0].rearrange("p (h t) -> p h t", h=H_MLA)
        qT = arena[0:QK_MLA, QT0:V0].rearrange("p (h t) -> p h t", h=H_MLA)
        v = arena[:, V0:ATT_BASE].rearrange("p (t h c) -> p t h c", t=4, h=H_MLA)
        at = ATT_BASE
        w96 = H_MLA * QK_MLA
        tile2 = arena[:, at:at + 2 * w96].rearrange("p (b h c) -> p b h c", b=2, h=H_MLA)
        sq = arena[:, at + 2 * w96:at + 3 * w96].rearrange("p (h c) -> p h c", h=H_MLA)
        at += 3 * w96
        kr = arena[:, at:at + 4 * ROPE].rearrange("p (t c) -> p t c", t=4)
        st = arena[:, at + 128:at + 128 + 64]
        at += 192
        assert at <= ARENA
        cqn = arena[:, KT0:KT0 + 4 * T].rearrange("p (b t) -> p b t", b=4)
        sqq = arena[:, KT0 + 1024:KT0 + 2048].rearrange("p (b t) -> p b t", b=4)
        sqk = arena[:, KT0 + 2048:KT0 + 3072].rearrange("p (b t) -> p b t", b=2)
        stq, rq = arena[:, KT0 + 3072:KT0 + 3328], arena[:, KT0 + 3328:KT0 + 3584]
        stk, rk = arena[:, KT0 + 3584:KT0 + 4096], arena[:, KT0 + 4096:KT0 + 4608]
        ckn = h
        q_raw = h.rearrange("p k t -> p (k t)")[:, 2 * NTOK:2 * NTOK + 2 * w96].rearrange("p (t c) -> p t c", t=2)
        tiles = [("q", 0), ("q", 1)] + [("k", t) for t in range(4)]
        S = lambda s: sem(f"mla_{s}")

        def tensor(pe):
            eng = pe.eng
            for s in range(2):
                w = units(pe.slots.take())
                for u in range(UPS):
                    for k in range(KD):
                        if s == 0 and u == 0:
                            h_block_ready(pe, "mla_mod", 0, k)
                        mm = nc.tensor.matmul(ps[:, 2 * s + u, 0:T], w[:, u, k, :], h[:, k, T:NTOK],
                                              start=(k == 0), stop=(k == KD - 1))
                mm.then_inc(slot_read, 1)
            w = units(pe.slots.take())
            for u in range(UPS):
                for k in range(KD):
                    mm = nc.tensor.matmul(ps[:, 4 + u, :], w[:, u, k, :], h[:, k, :],
                                          start=(k == 0), stop=(k == KD - 1))
            mm.then_inc(slot_read, 1)
            krw = col("kr_w").rearrange("p (k c) -> p k c", k=KD)
            for t in range(4):
                for k in range(KD):
                    mm = nc.tensor.matmul(ps[:, 6, t * ROPE:(t + 1) * ROPE], h[:, k, t * P:(t + 1) * P], krw[:, k, :],
                                          start=(k == 0), stop=(k == KD - 1))
            mm.then_inc(S("kr_done"), 1)
            for b in range(2):
                eng.wait_ge(S("sqk"), b + 1)
                mm = nc.tensor.matmul(ps[:, 7, :], col("over256"), sqk[:, b, :], start=(b == 0), stop=(b == 1))
            mm.then_inc(S("msk"), 1)
            eng.wait_ge(S("kr"), 1)
            for b in range(4):
                eng.wait_ge(S("sqq"), b + 1)
                mm = nc.tensor.matmul(ps[:, 6, 0:T], col("over512"), sqq[:, b, :], start=(b == 0), stop=(b == 3))
            mm.then_inc(S("msq"), 1)
            eng.wait_ge(S("cqn"), 4)
            eng.wait_ge(S("ckn"), 2)
            for n in range(3):
                w = pe.slots.take().rearrange("p (k c) -> p k c", k=4)
                for t in range(2):
                    for k in range(4):
                        mm = nc.tensor.matmul(ps[:, 2 * n + t, :], cqn[:, k, t * P:(t + 1) * P], w[:, k, :],
                                              start=(k == 0), stop=(k == 3))
                mm.then_inc(slot_read, 1)
            w0 = pe.slots.take().rearrange("p (n k c) -> p n k c", n=2, k=2)
            w1 = pe.slots.take().rearrange("p (n k c) -> p n k c", n=2, k=2)
            for n in range(len(tiles)):
                if n + 1 < len(tiles) and tiles[n + 1][0] == "k":
                    t = tiles[n + 1][1]
                    if t == 0:
                        eng.wait_ge(S("q_raw"), 6)
                    else:
                        eng.wait_ge(S("k_taken"), 4 * t)
                        eng.wait_ge(S("v_taken"), 4 * t)
                    for c in range(4):
                        w = (w0 if c < 2 else w1)[:, c % 2]
                        for k in range(2):
                            mm = nc.tensor.matmul(ps[:, c, :], ckn[:, k, t * P:(t + 1) * P], w[:, k, :],
                                                  start=(k == 0), stop=(k == 1))
                        if t < 3 or c % 2 == 0:
                            mm.then_inc(S("ukv_done"), 1)
                        else:
                            mm.then_inc(slot_read, 1)
                eng.wait_ge(S("rotated"), n + 1)
                for hd in range(H_MLA):
                    if hd % 4 == 0 and n:
                        eng.wait_ge(S("turned"), 4 * (n - 1) + hd // 4 + 1)
                    mm = nc.tensor.transpose(ps[0:QK_MLA, 4 + hd // 4, (hd % 4) * P:(hd % 4 + 1) * P],
                                             tile2[:, n % 2, hd, :], ident)
                    if hd % 4 == 3:
                        mm.then_inc(S("turn"), 1)

        def scalar(act):
            eng = act.eng
            for b in range(2):
                slots_read(eng, "mla_in", 3)
                nc.scalar.activation(sqk[:, b, :], ps[:, 4 + b, :], ACT.Square).then_inc(S("sqk"), 1)
            for b in range(4):
                nc.scalar.activation(sqq[:, b, :], ps[:, b, 0:T], ACT.Square).then_inc(S("sqq"), 1)
            eng.wait_ge(S("kr_done"), 1)
            nc.scalar.activation(kr[:, :, :], ps[:, 6, 0:4 * ROPE].rearrange("p (t c) -> p t c", t=4), ACT.Copy)\
              .then_inc(S("kr"), 1)
            eng.wait_ge(S("msk"), 1)
            nc.scalar.activation(stk, ps[:, 7, :], ACT.Sqrt, bias=col("eps6")).then_inc(S("stk"), 1)
            eng.wait_ge(S("msq"), 1)
            nc.scalar.activation(stq, ps[:, 6, 0:T], ACT.Sqrt, bias=col("eps6")).then_inc(S("stq"), 1)
            for n in range(3):
                slots_read(eng, "mla_uq", n + 1)
                for t in range(2):
                    nc.scalar.activation(q_raw[:, t, n * 512:(n + 1) * 512], ps[:, 2 * n + t, :], ACT.Copy)\
                      .then_inc(S("q_raw"), 1)
            def fill(n):
                kind, t = tiles[n]
                tile = tile2[:, n % 2]
                if n >= 2:
                    eng.wait_ge(S("turn"), 4 * (n - 1))
                if kind == "q":
                    eng.wait_ge(S("q_raw"), 6)
                    nc.scalar.activation(tile.rearrange("p h c -> p (h c)"), q_raw[:, t, :], ACT.Copy)\
                      .then_inc(S("tile"), 1)
                else:
                    for c in range(4):
                        ukv_chunk_done(eng, t, c)
                        nc.scalar.activation(tile[:, 4 * c:4 * c + 4, 0:NOPE],
                                             ps[:, c, :].rearrange("p (h c) -> p h c", h=4)[:, :, 0:NOPE], ACT.Copy)\
                          .then_inc(S("k_taken"), 1)
                    nc.scalar.activation(tile[:, :, NOPE:QK_MLA], kr[:, t:t + 1, :].to_broadcast([P, H_MLA, ROPE]),
                                         ACT.Copy).then_inc(S("tile"), 1)

            def square(n):
                kind, t = tiles[n]
                if n:
                    eng.wait_ge(S("rotated"), n)
                eng.wait_ge(S("tile"), n + 1)
                if kind == "k":
                    eng.wait_ge(S("k_taken"), 4 * t + 4)
                nc.scalar.activation(sq[:, :, :], tile2[:, n % 2], ACT.Square).then_inc(S("sq"), 1)

            fill(0)
            square(0)
            for n in range(len(tiles)):
                eng.wait_ge(S("ss"), n + 1)
                nc.scalar.activation(st[:, 16:32], st[:, 0:16], ACT.Sqrt, scale=1.0 / QK_MLA, bias=col("eps6"))\
                  .then_inc(S("rms"), 1)
                if n + 1 < len(tiles):
                    fill(n + 1)
                    square(n + 1)
                for c in range(0, 4, 2):
                    turned_out(eng, nc.scalar, n, c)

        def ukv_chunk_done(eng, t, c):
            if t == 3 and c % 2 == 1:
                slots_read(eng, "mla_ukv", c // 2 + 1)
            else:
                eng.wait_ge(S("ukv_done"), 4 * t + c + 1 if t < 3 else 13 + c // 2)

        def turned_out(eng, unit, n, c):
            kind, t = tiles[n]
            dst = (qT if kind == "q" else kT)[:, 4 * c:4 * c + 4, t * P:(t + 1) * P]
            src = ps[0:QK_MLA, 4 + c, :].rearrange("p (h t) -> p h t", h=4)
            eng.wait_ge(S("turn"), 4 * n + c + 1)
            if unit is nc.scalar:
                if 4 * n + c:
                    eng.wait_ge(S("turned"), 4 * n + c)
                nc.scalar.activation(dst, src, ACT.Copy).then_inc(S("turned"), 1)
            else:
                eng.wait_ge(S("turned"), 4 * n + c)
                nc.vector.tensor_copy(dst, src).then_inc(S("turned"), 1)

        def vector(dve):
            eng = dve.eng
            slots_read(eng, "mla_in", 3)
            eng.wait_ge(S("stk"), 1)
            dve.add(nc.vector.reciprocal(rk, stk))
            dve.settle()
            eng.wait_ge(S("kr_done"), 1)
            for b in range(2):
                nc.vector.scalar_tensor_tensor(ckn[:, b, :], ps[:, 4 + b, :], col("kv_norm")[:, b:b + 1], rk,
                                               ALU.mult, ALU.mult).then_inc(S("ckn"), 1)
            eng.wait_ge(S("stq"), 1)
            dve.add(nc.vector.reciprocal(rq, stq))
            dve.settle()
            for b in range(4):
                nc.vector.scalar_tensor_tensor(cqn[:, b, :], ps[:, b, 0:T], col("q_norm")[:, b:b + 1], rq,
                                               ALU.mult, ALU.mult).then_inc(S("cqn"), 1)
            c1 = col("cos1").rearrange("p (t o c) -> p t o c", t=TT, o=1)
            s1 = col("sin1").rearrange("p (t o c) -> p t o c", t=TT, o=1)
            for n, (kind, t) in enumerate(tiles):
                if kind == "k":
                    for c in range(4):
                        eng.wait_ge(S("k_taken"), 4 * t + c + 1)
                        nc.vector.tensor_copy(v[:, t, 4 * c:4 * c + 4, :],
                                              ps[:, c, :].rearrange("p (h c) -> p h c", h=4)[:, :, NOPE:2 * NOPE])\
                          .then_inc(S("v_taken"), 1)
                tile = tile2[:, n % 2]
                eng.wait_ge(S("sq"), n + 1)
                nc.vector.tensor_reduce(st[:, 0:16], sq[:, :, :], AX.X, ALU.add).then_inc(S("ss"), 1)
                eng.wait_ge(S("rms"), n + 1)
                dve.add(nc.vector.reciprocal(st[:, 32:48], st[:, 16:32]))
                dve.settle()
                dve.add(nc.vector.tensor_tensor(tile[:, :, :], tile[:, :, :],
                                                st[:, 32:48].rearrange("p (h o) -> p h o", o=1)
                                                .to_broadcast([P, H_MLA, QK_MLA]), ALU.mult))
                dve.settle()
                gain = col("q_gain" if kind == "q" else "k_gain").rearrange("p (o c) -> p o c", o=1)
                rotate = kind == "q" or t >= 2
                ins = nc.vector.tensor_tensor(tile[:, :, :], tile[:, :, :], gain.to_broadcast([P, H_MLA, QK_MLA]),
                                              ALU.mult)
                if not rotate:
                    ins.then_inc(S("rotated"), 1)
                else:
                    dve.add(ins)
                    dve.settle()
                    ti = t if kind == "q" else t - 2
                    r = tile[:, :, NOPE:QK_MLA].rearrange("p h (c two) -> p h c two", two=2)
                    r1, r2 = r[:, :, :, 0], r[:, :, :, 1]
                    tm = sq.rearrange("p h c -> p (h c)")[:, 0:1024].rearrange("p (n h c) -> p n h c", n=4, h=H_MLA)
                    cb, sb = c1[:, ti].to_broadcast([P, H_MLA, 16]), s1[:, ti].to_broadcast([P, H_MLA, 16])
                    for m, (a, b) in enumerate([(r1, cb), (r2, sb), (r1, sb), (r2, cb)]):
                        dve.add(nc.vector.tensor_tensor(tm[:, m], a, b, ALU.mult))
                    dve.settle()
                    nc.vector.tensor_tensor(r1, tm[:, 0], tm[:, 1], ALU.subtract)
                    nc.vector.tensor_tensor(r2, tm[:, 2], tm[:, 3], ALU.add).then_inc(S("rotated"), 1)
                for c in range(1, 4, 2):
                    turned_out(eng, nc.vector, n, c)

        return dict(name=name, tensor=tensor, scalar=scalar, vector=vector)

    def mla_attention():
        kT = arena[0:QK_MLA, KT0:QT0].rearrange("p (h t) -> p h t", h=H_MLA)
        qT = arena[0:QK_MLA, QT0:V0].rearrange("p (h t) -> p h t", h=H_MLA)
        v = arena[:, V0:ATT_BASE].rearrange("p (t h c) -> p t h c", t=4, h=H_MLA)

        def scores(it):
            head, i = it // TT, it % TT
            return nc.tensor.matmul(ps[:, it % 2, :], qT[:, head, i * P:(i + 1) * P], kT[:, head, :],
                                    start=True, stop=True)

        return attention("mla_att", H_MLA * TT, scores, lambda it: [(it % 2, 0, NTOK, 0)],
                         lambda dve, it, rec: None,
                         lambda it: [(j * P, P, v[:, j, it // TT, :]) for j in range(4)],
                         QK_MLA ** -0.5, lambda eng: eng.wait_ge(sem("mla_turned"), 24))

    def layer_norm(name, after, which):
        G = Signals("ln", name, mean=1, square=KD, var=1, centred=KD, std=1, scaled=KD, x=KD)
        sq, cen, std, rstd = carve(KD * T, KD * T, T, T)
        sq = sq.rearrange("p (k t) -> p k t", k=KD)
        cen = cen.rearrange("p (k t) -> p k t", k=KD)

        def tensor(pe):
            for k in range(KD):
                after(pe.eng, k + 1)
                mm = nc.tensor.matmul(ps[:, 0, 0:T], col("over1024"), x[:, k, T:NTOK], start=(k == 0), stop=(k == KD - 1))
            mm.then_inc(G["mean"], 1)
            for k in range(KD):
                G.wait(pe.eng, "square", k + 1)
                mm = nc.tensor.matmul(ps[:, 1, 0:T], col("over1024"), sq[:, k, :], start=(k == 0), stop=(k == KD - 1))
            mm.then_inc(G["var"], 1)

        def vector(dve):
            after(dve.eng, KD)
            G.wait(dve.eng, "mean", 1)
            for k in range(KD):
                nc.vector.tensor_tensor(cen[:, k, :], x[:, k, T:NTOK], ps[:, 0, 0:T], ALU.subtract)\
                  .then_inc(G["centred"], 1)
            G.wait(dve.eng, "std", 1)
            dve.add(nc.vector.reciprocal(rstd, std))
            dve.settle()
            G.wait(dve.eng, "square", KD)
            for k in range(KD):
                nc.vector.tensor_tensor(cen[:, k, :], cen[:, k, :], rstd, ALU.mult).then_inc(G["scaled"], 1)

        def scalar(act):
            for k in range(KD):
                G.wait(act.eng, "centred", k + 1)
                nc.scalar.activation(sq[:, k, :], cen[:, k, :], ACT.Square).then_inc(G["square"], 1)
            G.wait(act.eng, "var", 1)
            nc.scalar.activation(std, ps[:, 1, 0:T], ACT.Sqrt, bias=col("eps5")).then_inc(G["std"], 1)
            g = col("ln2_g").rearrange("p (n k) -> p n k", n=4)
            b = col("ln2_b").rearrange("p (n k) -> p n k", n=4)
            for k in range(KD):
                G.wait(act.eng, "scaled", k + 1)
                nc.scalar.activation(x[:, k, T:NTOK], cen[:, k, :], ACT.Identity, scale=g[:, which, k:k + 1],
                                     bias=b[:, which, k:k + 1]).then_inc(G["x"], 1)

        return dict(name=name, tensor=tensor, scalar=scalar, vector=vector)

    def swa():
        name = "swa_in"
        q, k, v, qr, kr, t1 = carve(KD * T, 2 * T, TT * T, KD * T, KV2 * T, 4 * T)
        q = q.rearrange("p (b t) -> p b t", b=KD)
        k = k.rearrange("p (b t) -> p b t", b=2)
        v = v.rearrange("p (t c) -> p t c", t=TT)
        qr = qr.rearrange("p (b t) -> p b t", b=KD)
        kr = kr.rearrange("p (b t) -> p b t", b=KV2)
        t1 = t1.rearrange("p (n t) -> p n t", n=4)
        S = lambda s: sem(f"swa_{s}")
        jobs = [(q[:, b, :], ident, col("rot"), qr[:, b, :]) for b in range(KD)] + \
               [(k[:, g // 2, :], col(f"dup{g % 2}"), col(f"rdup{g % 2}"), kr[:, g, :]) for g in range(KV2)]
        assert KD * T * 2 + 2 * T + TT * T + KV2 * T + 4 * T <= ATT_BASE
        C = Cut(name, "swa_in", T, 10)

        def tensor(pe):
            for g in range(10):
                if g >= 8:
                    pe.eng.wait_ge(S("copied"), g - 7)
                C.unit(pe, g, ps[:, g % 8, 0:T])
            w = pe.slots.take().rearrange("p (k c) -> p k c", k=KD)
            pe.eng.wait_ge(S("copied"), 4)
            for t in range(TT):
                for kk in range(KD):
                    mm = nc.tensor.matmul(ps[:, 2 + t, 0:T], x[:, kk, T + t * P:T + (t + 1) * P], w[:, kk, :],
                                          start=(kk == 0), stop=(kk == KD - 1))
            mm.then_inc(slot_read, 1)
            rotate_tensor(pe, name, jobs, lambda n: pe.eng.wait_ge(S("copied"), 10), (4, 5, 6, 7))

        def scalar(act):
            C.lead(act, 0)
            for kk in range(KD):
                signals["ffn1"].wait(act.eng, "x", kk + 1)
                C.input_lead(act, kk, x[:, kk, T:NTOK])
            for g in range(1, C.buffers):
                C.lead(act, g)
            for b in range(10):
                C.lead(act, b + C.buffers)
                C.done(act.eng, b + 1)
                dst = q[:, b, :] if b < 8 else k[:, b - 8, :]
                nc.scalar.activation(dst, ps[:, b % 8, 0:T], ACT.Copy).then_inc(S("copied"), 1)
            slots_read(act.eng, "swa_in", 6)
            for t in range(TT):
                nc.scalar.activation(v[:, t, :], ps[:, 2 + t, 0:T], ACT.Copy).then_inc(S("v"), 1)

        def vector(dve):
            C.rest(dve, 0)
            for k in range(KD):
                C.input_rest(dve, k, x[:, k, T:NTOK])
            for g in range(1, 10):
                C.rest(dve, g)
            rotate_vector(dve, name, jobs, t1, (4, 5, 6, 7))

        def scores(it):
            head, i = it // TT, it % TT
            half = slice(64 * (head % 2), 64 * (head % 2) + 64)
            W = (i + 1) * P
            nc.tensor.matmul(ps[:, it % 2, 0:W], qr[half, head // 2, i * P:(i + 1) * P], kr[half, head // G2, 0:W],
                             start=True, stop=False)
            if i:
                nc.tensor.matmul(ps[:, it % 2, 0:P], ident_b[:, :], band_b[:, :], start=False, stop=False)
            return nc.tensor.matmul(ps[:, it % 2, i * P:W], ident_b[:, :], causal_b[:, :], start=False, stop=True)

        def before(eng):
            eng.wait_ge(sem("swa_in_rotated"), len(jobs))
            eng.wait_ge(S("v"), TT)
            eng.wait_ge(masks_ready, 1)

        att = attention("swa", H2 * TT, scores, lambda it: [(it % 2, 0, (it % TT + 1) * P, 0)],
                        lambda dve, it, rec: None,
                        lambda it: [(j * P, P, v[:, j, HD * (it // TT // G2):HD * (it // TT // G2) + HD])
                                    for j in range(it % TT + 1)],
                        HD ** -0.5, before)
        return dict(name=name, tensor=tensor, scalar=scalar, vector=vector), att

    def rotate_tensor(pe, name, jobs, ready, banks):
        for n, (src, plain, rot, dst) in enumerate(jobs):
            if n == 0:
                ready(n)
            if n >= 2:
                pe.eng.wait_ge(sem(f"{name}_rotated"), n - 1)
            a = banks[2 * (n % 2)]
            if plain is not None:
                mm = nc.tensor.matmul(ps[:, a, 0:T], plain, src, start=True, stop=True)
            if rot is not None:
                mm = nc.tensor.matmul(ps[:, a + 1, 0:T], rot, src, start=True, stop=True)
            mm.then_inc(sem(f"{name}_turn"), 1)

    def rotate_vector(dve, name, jobs, t1, banks):
        for n, (src, plain, rot, dst) in enumerate(jobs):
            a = banks[2 * (n % 2)]
            dve.eng.wait_ge(sem(f"{name}_turn"), n + 1)
            signal = sem(f"{name}_rotated")
            if rot is None:
                pieces = [(slice(0, P), 0, T, dst)] if not isinstance(dst, list) else dst
                for part, c0, c1, d in pieces:
                    ins = nc.vector.tensor_copy(d, ps[part, a, c0:c1])
                ins.then_inc(signal, 1)
                continue
            u, w = t1[:, 2 * (n % 2), :], t1[:, 2 * (n % 2) + 1, :]
            dve.add(nc.vector.tensor_tensor(u, ps[:, a, 0:T], col("cos2"), ALU.mult))
            dve.add(nc.vector.tensor_tensor(w, ps[:, a + 1, 0:T], col("sin2"), ALU.mult))
            dve.settle()
            pieces = [(slice(0, P), 0, T, dst)] if not isinstance(dst, list) else dst
            for part, c0, c1, d in pieces:
                ins = nc.vector.tensor_tensor(d, u[part, c0:c1], w[part, c0:c1], ALU.add)
            ins.then_inc(signal, 1)

    def nsa():
        name = "nsa_in"
        q, kk_, v, gates, ksr, kwr, t1, cmpk, cmpv, blk, hidc, vcc, kcc = carve(
            KD * T, 8 * T, TT * 512, TT * 48, KV2 * T, KV2 * T, 4 * T, KV2 * T, KV2 * T,
            2 * LP * KV2 * NCMP, 2 * 2 * KV2 * NCMP, KV2 * HD, KV2 * NCMP)
        q = q.rearrange("p (b t) -> p b t", b=KD)
        kvs = kk_.rearrange("p (n b t) -> p n b t", n=4, b=2)
        v = v.rearrange("p (t n c) -> p t n c", t=TT, n=2)
        gates = gates.rearrange("p (t c) -> p t c", t=TT)
        ksr = ksr.rearrange("p (b t) -> p b t", b=KV2)
        kwr = kwr.rearrange("p (b t) -> p b t", b=KV2)
        t1 = t1.rearrange("p (n t) -> p n t", n=4)
        cmpk = cmpk.rearrange("p (g t) -> p g t", g=KV2)
        cmpv = cmpv.rearrange("p (g t) -> p g t", g=KV2)
        NB = KV2 * NCMP
        blk = blk.rearrange("p (n l c) -> p n l c", n=2, l=LP)
        hidc = hidc.rearrange("p (n m c) -> p n m c", n=2, m=2)
        vcc = vcc.rearrange("p (g c) -> p g c", g=KV2)
        S = lambda s: sem(f"nsa_{s}")
        C = Cut(name, "nsa_in", T, 16)
        jobs = []

        def shifted(dst, g):
            return [(slice(0, 64), 0, T, dst[0:64, g, :]), (slice(64, P), 1, T, dst[64:P, g, 0:T - 1])]

        for g in range(KV2):
            jobs.append((kvs[:, 0, g // 2, :], col(f"dup{g % 2}"), col(f"rdup{g % 2}"), shifted(cmpk, g)))
        for g in range(KV2):
            jobs.append((kvs[:, 1, g // 2, :], col(f"dup{g % 2}"), None, shifted(cmpv, g)))
        for g in range(KV2):
            jobs.append((kvs[:, 2, g // 2, :], col(f"dup{g % 2}"), col(f"rdup{g % 2}"), ksr[:, g, :]))
        for g in range(KV2):
            jobs.append((kvs[:, 3, g // 2, :], col(f"dup{g % 2}"), col(f"rdup{g % 2}"), kwr[:, g, :]))
        for b in range(KD):
            jobs.append((q[:, b, :], ident, col("rot"), q[:, b, :]))

        def tensor(pe):
            eng = pe.eng
            for g in range(16):
                if g >= 8:
                    eng.wait_ge(S("copied"), g - 7)
                C.unit(pe, g, ps[:, g % 8, 0:T])
            eng.wait_ge(S("copied"), 10)
            for s in range(2):
                w = pe.slots.take().rearrange("p (k c) -> p k c", k=4)
                for t in range(TT):
                    for k in range(4):
                        mm = nc.tensor.matmul(ps[:, t, :], x[:, 4 * s + k, T + t * P:T + (t + 1) * P], w[:, k, :],
                                              start=(s == 0 and k == 0), stop=(s == 1 and k == 3))
                mm.then_inc(slot_read, 1)
            eng.wait_ge(S("copied"), 11)
            gw = col("ng_w").rearrange("p (k c) -> p k c", k=KD)
            for t in range(TT):
                for k in range(KD):
                    mm = nc.tensor.matmul(ps[:, 2, t * 48:(t + 1) * 48], x[:, k, T + t * P:T + (t + 1) * P], gw[:, k, :],
                                          start=(k == 0), stop=(k == KD - 1))
            mm.then_inc(S("gates_done"), 1)
            rotate_tensor(pe, name, jobs, lambda n: eng.wait_ge(S("copied"), 16), (4, 5, 6, 7))
            for n in range(2):
                if n == 0:
                    eng.wait_ge(S("v"), 2)
                eng.wait_ge(S("blk"), n + 1)
                for m in range(2):
                    w = pe.slots.take().rearrange("p (l c) -> p l c", l=LP)
                    for l in range(LP):
                        mm = nc.tensor.matmul(ps[:, n, m * 64:m * 64 + NB], w[:, l, :], blk[:, n, l, :],
                                              start=(l == 0), stop=(l == LP - 1))
                    mm.then_inc(slot_read, 1)
            w2k = col("w2k").rearrange("p (m c) -> p m c", m=2)
            w2v = col("w2v").rearrange("p (m c) -> p m c", m=2)
            eng.wait_ge(S("hid"), 1)
            eng.wait_ge(S("gates"), 1)
            for m in range(2):
                mm = nc.tensor.matmul(ps[:, 3, 0:NB], w2k[:, m, :], hidc[:, 0, m, :], start=(m == 0), stop=(m == 1))
            mm.then_inc(S("kcc_done"), 1)
            eng.wait_ge(S("hid"), 2)
            for g in range(KV2):
                for m in range(2):
                    mm = nc.tensor.matmul(ps[0:NCMP, 2, g * HD:(g + 1) * HD],
                                          hidc[:, 1, m, g * NCMP:(g + 1) * NCMP], w2v[:, m, :],
                                          start=(m == 0), stop=(m == 1))
            mm.then_inc(S("vcc_done"), 1)

        def scalar(act):
            eng = act.eng
            C.lead(act, 0)
            for k in range(KD):
                signals["ln2"].wait(eng, "x", k + 1)
                C.input_lead(act, k, x[:, k, T:NTOK])
            for g in range(1, C.buffers):
                C.lead(act, g)
            for b in range(16):
                C.lead(act, b + C.buffers)
                C.done(eng, b + 1)
                dst = q[:, b, :] if b < 8 else kvs[:, (b - 8) // 2, b % 2, :]
                nc.scalar.activation(dst, ps[:, b % 8, 0:T], ACT.Copy).then_inc(S("copied"), 1)
            slots_read(eng, "nsa_in", 10)
            for t in range(TT):
                nc.scalar.activation(v[:, t, :, :], ps[:, t, :].rearrange("p (n c) -> p n c", n=2), ACT.Copy)\
                  .then_inc(S("v"), 1)
            eng.wait_ge(S("gates_done"), 1)
            nc.scalar.activation(gates[:, :, :], ps[:, 2, 0:TT * 48].rearrange("p (t c) -> p t c", t=TT), ACT.Sigmoid)\
              .then_inc(S("gates"), 1)
            for n in range(2):
                slots_read(eng, "nsa_cmp", 2 * (n + 1))
                nc.scalar.activation(hidc[:, n, :, :], ps[:, n, 0:P].rearrange("p (m c) -> p m c", m=2)[:, :, 0:NB],
                                     ACT.Gelu_apprx_tanh).then_inc(S("hid"), 1)
            eng.wait_ge(S("kcc_done"), 1)
            nc.scalar.activation(kcc, ps[:, 3, 0:NB], ACT.Copy).then_inc(S("kcc"), 1)
            eng.wait_ge(S("vcc_done"), 1)
            nc.scalar.activation(vcc[0:NCMP, :, :], ps[0:NCMP, 2, 0:KV2 * HD].rearrange("p (g c) -> p g c", g=KV2),
                                 ACT.Copy).then_inc(S("vcc"), 1)

        def vector(dve):
            eng = dve.eng
            C.rest(dve, 0)
            for k in range(KD):
                C.input_rest(dve, k, x[:, k, T:NTOK])
            for g in range(1, 16):
                C.rest(dve, g)
            eng.wait_ge(S("gates"), 1)
            for t in range(TT):
                gc = gates[:, t, :].rearrange("p (h n) -> p h n", n=3)[:, :, 0]
                dve.add(nc.vector.tensor_scalar(gc, gc, col("cmp_valid")[:, t:t + 1], None, ALU.mult))
            rotate_vector(dve, name, jobs, t1, (4, 5, 6, 7))
            dve.eng.wait_ge(sem(f"{name}_rotated"), 8)
            for n, (src, pos) in enumerate([(cmpk, "pos_k"), (cmpv, "pos_v")]):
                for l in range(LP):
                    ins = nc.vector.tensor_scalar(
                        blk[:, n, l, :].rearrange("p (g c) -> p g c", g=KV2),
                        src[:, :, 2 * l:2 * l + CMP_STRIDE * (NCMP - 1) + 1:CMP_STRIDE],
                        col(pos)[:, l:l + 1], None, ALU.add)
                ins.then_inc(S("blk"), 1)

        def scores(it):
            head, i = it // TT, it % TT
            half = slice(64 * (head % 2), 64 * (head % 2) + 64)
            g = head // G2
            W = (i + 1) * P
            qh = q[half, head // 2, i * P:(i + 1) * P]
            cm = cmpm_b[:, :].rearrange("p (t c) -> p t c", t=TT)
            for n, kr in enumerate((ksr, kwr)):
                nc.tensor.matmul(ps[:, it % 2, n * W:(n + 1) * W], qh, kr[half, g, 0:W], start=True, stop=False)
                nc.tensor.matmul(ps[:, it % 2, n * W + i * P:(n + 1) * W], ident_b[:, :], causal_b[:, :],
                                 start=False, stop=True)
            nc.tensor.matmul(ps[:, 2 + it % 2, 0:NCMP], qh, kcc[half, g * NCMP:(g + 1) * NCMP], start=True, stop=False)
            return nc.tensor.matmul(ps[:, 2 + it % 2, 0:NCMP], ident_b[:, :], cm[:, i, 0:NCMP], start=False, stop=True)

        def segments(it):
            W = (it % TT + 1) * P
            return [(it % 2, 0, W, 0), (it % 2, W, W, W), (2 + it % 2, 0, NCMP, 2 * W)]

        def factors(dve, it, rec):
            head, i = it // TT, it % TT
            dve.add(nc.vector.tensor_tensor(rec[:, 0:2], rec[:, 0:2], gates[:, i, 3 * head + 1:3 * head + 3], ALU.mult))
            dve.add(nc.vector.tensor_tensor(rec[:, 2:3], rec[:, 2:3], gates[:, i, 3 * head:3 * head + 1], ALU.mult))
            dve.settle()

        def values(it):
            head, i = it // TT, it % TT
            g = head // G2
            W = (i + 1) * P
            vals = [(n * W + j * P, P, v[:, j, n, g * HD:(g + 1) * HD]) for n in range(2) for j in range(i + 1)]
            return vals + [(2 * W, NCMP, vcc[0:NCMP, g, :])]

        def before(eng):
            eng.wait_ge(sem("nsa_in_rotated"), len(jobs))
            eng.wait_ge(S("kcc"), 1)
            eng.wait_ge(S("vcc"), 1)

        att = attention("nsa", H2 * TT, scores, segments, factors, values, HD ** -0.5,
                        before)
        return dict(name=name, tensor=tensor, scalar=scalar, vector=vector), att

    def moe():
        NR = NEXP + EXTRA
        NU, ND = F2, F2 * D // SLOT
        NSL = NU + ND
        GRP = 4
        NG = NU // GRP
        FAR = 1e6
        x_tok, hid, t1, hT, S_, Sg, GT, y, lg, mx8, ix8, pick, gate, RK, GV, sel, part, sm = carve(
            TT * D, F2 * P, 2 * GRP * P, 2 * GRP * P, TT * P, TT * P, T, D, TT * NEXP, TT * NEXP, TT * NEXP,
            2 * TT * NEXP, TT * NEXP, TT * (NR + 1), TT * (NR + 1), EXTRA * NEXP, EXTRA * NEXP, 96)
        x_tok = x_tok.rearrange("p (t k c) -> p t k c", t=TT, k=KD)
        CUTS, NC = 4, 2 * NU
        x_lead = parts[:, 0:UNIT].rearrange("p (k s) -> p k s", k=KD)
        x_rest = parts[:, UNIT:2 * UNIT].rearrange("p (k s) -> p k s", k=KD)
        w_cut = parts[:, 2 * UNIT:(2 + 2 * CUTS) * UNIT].rearrange("p (a b k c) -> p a b k c", a=2, b=CUTS, k=2)
        hid = hid.rearrange("p (f s) -> p f s", f=F2)
        t1 = t1.rearrange("p (b c) -> p b c", b=2)
        hT = hT.rearrange("p (b c) -> p b c", b=2)
        S_ = S_.rearrange("p (t s) -> p t s", t=TT)
        Sg = Sg.rearrange("p (t s) -> p t s", t=TT)
        lg = lg.rearrange("p (t e) -> p t e", t=TT)
        mx8 = mx8.rearrange("p (t e) -> p t e", t=TT)
        ix8u = ix8.bitcast(U32).rearrange("p (t e) -> p t e", t=TT)
        pick = pick.rearrange("p (n t e) -> p n t e", n=2, t=TT)
        gate = gate.rearrange("p (t e) -> p t e", t=TT)
        RK = RK.rearrange("p (t r) -> p t r", t=TT)
        GV = GV.rearrange("p (t r) -> p t r", t=TT)
        sel = sel.rearrange("p (j e) -> p j e", j=EXTRA)
        part = part.rearrange("p (j e) -> p j e", j=EXTRA)
        rounds_u = nc.alloc_sbuf_tensor("rounds", [P, 1 + EXTRA], U32)
        first = BASE["moe"]
        S = lambda s: sem(f"moe_{s}")
        iota8 = col("iota")[:, 0:NEXP]

        def round_count(eng):
            eng.wait_ge(S("rounds"), 1)
            return eng.value_load(rounds_u[0:1, 0:1], min_val=NEXP, max_val=NR)

        def extra_slots(sync):
            sp = sync.eng
            n = round_count(sp)
            with sp.If(n > NEXP):
                with sp.Fori(NEXP, n) as r:
                    e = sp.value_load(rounds_u[0:1, bass.ds(r - (NEXP - 1), 1)], min_val=0, max_val=NEXP - 1)
                    for i in range(NSL):
                        s = (first + i) % NS
                        sp.wait_ge(slot_read, r * NSL + (first + i + 1 - NS))
                        sp.dma_start(ring[:, s, :],
                                     stream[bass.ds(e * NSL + (first + i), 1), :, :].rearrange("o p c -> (o p) c"))\
                          .then_inc(weights_ready[s], 16)

        def gather(eng):
            for k in range(KD):
                for t in range(TT):
                    mm = nc.tensor.matmul(ps[:, 2 + k // 4, (k % 4) * P:(k % 4 + 1) * P], x_tok[:, t, k, :],
                                          S_[:, t, :], start=(t == 0), stop=(t == TT - 1))
            mm.then_inc(S("gathered"), 1)

        def tensor(pe):
            eng = pe.eng
            rw = col("router").rearrange("p (k e) -> p k e", k=KD)
            for k in range(KD):
                signals["ln3"].wait(eng, "x", k + 1)
            for t in range(TT):
                for k in range(KD):
                    mm = nc.tensor.matmul(ps[:, 7, t * NEXP:(t + 1) * NEXP], x[:, k, T + t * P:T + (t + 1) * P],
                                          rw[:, k, :], start=(k == 0), stop=(k == KD - 1))
            mm.then_inc(S("logits"), 1)
            for t in range(TT):
                for k in range(KD):
                    mm = nc.tensor.transpose(ps[:, 2 + 2 * t + k // 4, (k % 4) * P:(k % 4 + 1) * P],
                                             x[:, k, T + t * P:T + (t + 1) * P], ident)
                mm.then_inc(S("x_turn"), 1)
            eng.wait_ge(S("picked"), 1)
            R = ps[:, 7, 64:64 + 3 * NEXP].rearrange("p (n e) -> p n e", n=3)
            for c, ops in enumerate([[("before", 0)], [("before", 1), ("over1024", 0)],
                                     [("over1024", 0), ("over1024", 1)]]):
                ops = [(m, n, t) for m, t in ops for n in range(2)]
                for j, (m, n, t) in enumerate(ops):
                    mm = nc.tensor.matmul(R[:, c, :], col(m), pick[:, n, t, :], start=(j == 0), stop=(j == len(ops) - 1))
            mm.then_inc(S("ranked"), 1)
            eng.wait_ge(S("x_tok"), 2)
            eng.wait_ge(S("sel"), 1)
            gather(eng)
            eng.wait_ge(S("GT"), 1)
            for c in range(2):
                mm = nc.tensor.matmul(ps[:, 4 + c, 0:512], GT[:, 0:P], x_tok[:, 0, 4 * c:4 * c + 4, :], start=True, stop=True)
            mm.then_inc(S("zeroed"), 1)
            n = round_count(eng)

            def spread(r):
                eng.wait_ge(S("GT"), r + 1)
                eng.wait_ge(S("y_act"), r + 1)
                eng.wait_ge(S("y_dve"), r + 1)
                for j in range(4):
                    for m in range(2):
                        c = (2 * j + m) * P
                        mm = nc.tensor.matmul(ps[:, (6, 7, 4, 5)[j], m * T:(m + 1) * T], y[:, c:c + P], GT[:, :],
                                              start=True, stop=True)
                    mm.then_inc(S("spread"), 1)

            with eng.Fori(0, n) as r:
                def slot(i):
                    eng.wait_ge(weights_ready[(first + i) % NS], r * (16 * NSL // NS) + 16 * ((first + i) // NS + 1))
                    return ring[:, (first + i) % NS, :]

                def hidden_turn(g):
                    eng.wait_ge(S("hidden"), r * NG + (g + 1))
                    if g:
                        eng.wait_ge(S("hid"), r * NG + g)
                    else:
                        eng.wait_ge(S("sum"), r * 4 + 4)
                    for j in range(GRP):
                        mm = nc.tensor.transpose(ps[:, 7, j * P:(j + 1) * P], hT[:, g % 2, j * P:(j + 1) * P], ident)
                    mm.then_inc(S("turn"), 1)

                eng.wait_ge(S("x_rest"), r * 2 + 2)
                for g in range(NG):
                    if g >= 2:
                        eng.wait_ge(S("hidden"), r * NG + (g - 1))
                    for i in range(8 * g, 8 * g + 8):
                        if i % 2:
                            eng.wait_ge(slot_read, r * NSL + (first + i // 2 + 1))
                        else:
                            eng.wait_ge(S("rest"), r * NU + (i // 2 + 1))
                        dst = ps[:, 2 * (g % 2) + i // 4 % 2, :]
                        for m in range(2):
                            k = 2 * (i % 4) + m
                            wl, wr = w_cut[:, 0, i % CUTS, m, :], w_cut[:, 1, i % CUTS, m, :]
                            nc.tensor.matmul(dst, x_lead[:, k, :], wl, start=(k == 0), stop=False)
                            nc.tensor.matmul(dst, x_lead[:, k, :], wr, start=False, stop=False)
                            mm = nc.tensor.matmul(dst, x_rest[:, k, :], wl, start=False, stop=(k == KD - 1))
                        mm.then_inc(S("product"), 1)
                    if g == 0:
                        spread(r)
                    else:
                        hidden_turn(g - 1)
                    if g == 2:
                        eng.wait_ge(S("sg"), r + 1)
                        for t in range(TT):
                            mm = nc.tensor.transpose(ps[:, 6, t * P:(t + 1) * P], Sg[:, t, :], ident)
                        mm.then_inc(S("sg_turn"), 1)
                eng.wait_ge(S("sum"), r * 4 + 6)
                for f in range(F2):
                    if f == F2 // 2:
                        hidden_turn(NG - 1)
                        eng.wait_ge(S("sel"), r + 2)
                        gather(eng)
                    if f % GRP == 0:
                        eng.wait_ge(S("hid"), r * NG + (f // GRP + 1))
                    if f % 2 == 0:
                        w = slot(NU + f // 2).rearrange("p (f c) -> p f c", f=2)
                    for c in range(2):
                        mm = nc.tensor.matmul(ps[:, 4 + c, :], hid[:, f, :], w[:, f % 2, c * 512:(c + 1) * 512],
                                              start=(f == 0), stop=(f == F2 - 1))
                    if f % 2 == 1:
                        mm.then_inc(slot_read, 1)
            spread(n)

        def scalar(act):
            eng = act.eng
            eng.wait_ge(S("logits"), 1)
            nc.scalar.activation(lg[:, :, :], ps[:, 7, 0:TT * NEXP].rearrange("p (t e) -> p t e", t=TT), ACT.Copy)\
              .then_inc(S("lg"), 1)
            for t in range(TT):
                eng.wait_ge(S("x_turn"), t + 1)
                nc.scalar.activation(x_tok[:, t, :, :], ps[:, 2 + 2 * t:4 + 2 * t, :].rearrange("p a (k c) -> p (a k) c", c=P),
                                     ACT.Copy).then_inc(S("x_tok"), 1)
            eng.wait_ge(S("diff"), 1)
            nc.scalar.activation(sm[:, 2:4], sm[:, 0:2], ACT.Exp).then_inc(S("exp"), 1)
            def tokens_lead(m, r):
                eng.wait_ge(S("gathered"), r + 1)
                nc.scalar.activation(x_lead[:, 4 * m:4 * m + 4, :], ps[:, 2 + m, :].rearrange("p (k s) -> p k s", k=4),
                                     ACT.Copy).then_inc(S("x_lead"), 1)

            def outputs(r):
                eng.wait_ge(S("zeroed"), 1)
                eng.wait_ge(slot_read, r * NSL + first)
                nc.scalar.activation(y[:, 0:512], ps[:, 4, :], ACT.Copy).then_inc(S("y_act"), 1)

            for m in range(2):
                tokens_lead(m, 0)
            n = round_count(eng)
            with eng.Fori(0, n) as r:
                def lead(i):
                    if i >= NC:
                        return
                    q = first + i // 2
                    eng.wait_ge(weights_ready[q % NS], r * (16 * NSL // NS) + 16 * (q // NS + 1))
                    if i >= CUTS:
                        eng.wait_ge(S("product"), r * NC + (i - CUTS + 1))
                    nc.scalar.activation(w_cut[:, 0, i % CUTS], ring[:, q % NS, (i % 2) * UNIT:(i % 2 + 1) * UNIT]
                                         .rearrange("p (k c) -> p k c", k=2), ACT.Copy).then_inc(S("lead"), 1)

                def hidden_out(g):
                    eng.wait_ge(S("turn"), r * NG + (g + 1))
                    nc.scalar.activation(hid[:, GRP * g:GRP * g + GRP, :],
                                         ps[:, 7, :].rearrange("p (j s) -> p j s", j=GRP), ACT.Copy)\
                      .then_inc(S("hid"), 1)

                for i in range(CUTS):
                    lead(i)
                outputs(r)
                for g in range(NG):
                    for j in range(8):
                        lead(8 * g + CUTS + j)
                    eng.wait_ge(S("product"), r * NC + 8 * (g + 1))
                    if g >= 2:
                        eng.wait_ge(S("hidden"), r * NG + (g - 1))
                    nc.scalar.activation(t1[:, g % 2, :], ps[:, 2 * (g % 2), :], ACT.Silu).then_inc(S("silu"), 1)
                    if g >= 1:
                        hidden_out(g - 1)
                    if g == 3:
                        eng.wait_ge(S("sg_turn"), r + 1)
                        nc.scalar.activation(GT[:, :], ps[:, 6, 0:T], ACT.Copy).then_inc(S("GT"), 1)
                hidden_out(NG - 1)
                for m in range(2):
                    tokens_lead(m, r + 1)
            outputs(n)

        def select(r, signal):
            for t in range(TT):
                ins = nc.vector.tensor_scalar(S_[:, t, :], col("iota"), RK[:, t, r], None, ALU.is_equal)
            ins.then_inc(signal, 1)

        def vector(dve):
            eng = dve.eng
            eng.wait_ge(S("lg"), 1)
            for t in range(TT):
                dve.add(nc.vector.max(mx8[:, t, :], lg[:, t, :]))
            dve.settle()
            for t in range(TT):
                dve.add(nc.vector.max_index(ix8u[:, t, :], mx8[:, t, :], lg[:, t, :]))
            dve.settle()
            nc.vector.tensor_tensor(sm[:, 0:2], mx8[:, :, 1], mx8[:, :, 0], ALU.subtract).then_inc(S("diff"), 1)
            dve.add(nc.vector.tensor_copy(sm[:, 4:8].rearrange("p (t n) -> p t n", t=TT), ix8u[:, :, 0:2]))
            dve.settle()
            for t in range(TT):
                for m in range(2):
                    ins = nc.vector.tensor_scalar(pick[:, m, t, :], iota8, sm[:, 4 + 2 * t + m:5 + 2 * t + m], None,
                                                  ALU.is_equal)
            ins.then_inc(S("picked"), 1)
            eng.wait_ge(S("picked"), 1)
            eng.wait_ge(S("exp"), 1)
            dve.add(nc.vector.tensor_scalar(sm[:, 8:10], sm[:, 2:4], 1.0, None, ALU.add))
            dve.settle()
            dve.add(nc.vector.reciprocal(sm[:, 10:12], sm[:, 8:10]))
            dve.settle()
            dve.add(nc.vector.tensor_tensor(sm[:, 12:14], sm[:, 10:12], sm[:, 2:4], ALU.mult))
            dve.settle()
            for t in range(TT):
                dve.add(nc.vector.tensor_scalar(gate[:, t, :], pick[:, 0, t, :], sm[:, 10 + t:11 + t], None, ALU.mult))
            dve.settle()
            for t in range(TT):
                dve.add(nc.vector.scalar_tensor_tensor(GV[:, t, 0:NEXP], pick[:, 1, t, :], sm[:, 12 + t:13 + t],
                                                       gate[:, t, :], ALU.mult, ALU.add))
            dve.settle()
            dve.add(nc.vector.tensor_tensor(gate[:, :, :], pick[:, 0, :, :], pick[:, 1, :, :], ALU.add))
            dve.settle()
            dve.add(nc.vector.tensor_scalar(gate[:, :, :], gate[:, :, :], -FAR, FAR, ALU.mult, ALU.add))
            dve.add(nc.vector.memset(RK[:, :, NR:NR + 1], FAR))
            dve.add(nc.vector.memset(GV[:, :, NR:NR + 1], 0.0))
            dve.settle()
            eng.wait_ge(S("ranked"), 1)
            R = ps[:, 7, 64:64 + 3 * NEXP].rearrange("p (n e) -> p n e", n=3)
            dve.add(nc.vector.scalar_tensor_tensor(RK[:, :, 0:NEXP], R[:, 0:2, :], float(D), gate[:, :, :],
                                                   ALU.mult, ALU.add))
            ovf, num, zero = sm[:, 24:32], sm[:, 32:40], sm[:, 40:48]
            dve.add(nc.vector.tensor_scalar(ovf, R[:, 2, :], float(D), P + 0.5, ALU.mult, ALU.is_gt))
            dve.add(nc.vector.memset(zero, 0.0))
            dve.settle()
            select(slice(0, 1), S("sel"))
            dve.add(nc.vector.tensor_tensor_scan(num, ovf, zero, 0.0, ALU.add, ALU.add))
            dve.settle()
            for j in range(EXTRA):
                dve.add(nc.vector.scalar_tensor_tensor(sel[:, j, :], num, float(j + 1), ovf, ALU.is_equal, ALU.mult))
            dve.settle()
            dve.add(nc.vector.tensor_scalar(sm[:, 48:49], num[:, NEXP - 1:NEXP], float(NEXP), None, ALU.add))

            def chosen(row, out_):
                dve.add(nc.vector.tensor_tensor(part[:, :, :], sel[:, :, :], row.to_broadcast([P, EXTRA, NEXP]), ALU.mult))
                dve.settle()
                dve.add(nc.vector.tensor_reduce(out_, part[:, :, :], AX.X, ALU.add))
                dve.settle()

            chosen(iota8.rearrange("p (o e) -> p o e", o=1), sm[:, 49:49 + EXTRA])
            nc.vector.tensor_copy(rounds_u[:, :], sm[:, 48:49 + EXTRA]).then_inc(S("rounds"), 1)
            for t in range(TT):
                chosen(RK[:, t:t + 1, 0:NEXP], sm[:, 56:56 + EXTRA])
                dve.add(nc.vector.tensor_scalar(RK[:, t, NEXP:NR], sm[:, 56:56 + EXTRA], float(P), None, ALU.subtract))
                chosen(GV[:, t:t + 1, 0:NEXP], GV[:, t, NEXP:NR])
            dve.settle()
            signals["ln3"].wait(eng, "x", KD)
            for m in range(2):
                nc.vector.tensor_scalar(x[:, 4 * m:4 * m + 4, 0:T], x[:, 4 * m:4 * m + 4, T:NTOK], ALPHA, None,
                                        ALU.mult).then_inc(S("sum"), 1)
            nc.vector.memset(GT[:, :], 0.0).then_inc(S("GT"), 1)

            def tokens_rest(m, r):
                eng.wait_ge(S("x_lead"), r * 2 + (m + 1))
                nc.vector.tensor_tensor(x_rest[:, 4 * m:4 * m + 4, :], ps[:, 2 + m, :].rearrange("p (k s) -> p k s", k=4),
                                        x_lead[:, 4 * m:4 * m + 4, :].bitcast(F32), ALU.subtract)\
                  .then_inc(S("x_rest"), 1)

            def outputs(r):
                eng.wait_ge(S("zeroed"), 1)
                eng.wait_ge(slot_read, r * NSL + first)
                nc.vector.tensor_copy(y[:, 512:D], ps[:, 5, :]).then_inc(S("y_dve"), 1)

            def sums(r):
                eng.wait_ge(S("sum"), r * 4 + 2)
                for j in range(4):
                    eng.wait_ge(S("spread"), r * 4 + (j + 1))
                    acc = x[:, 2 * j:2 * j + 2, 0:T]
                    nc.vector.tensor_tensor(acc, ps[:, (6, 7, 4, 5)[j], :].rearrange("p (m t) -> p m t", m=2), acc,
                                            ALU.add).then_inc(S("sum"), 1)

            for m in range(2):
                tokens_rest(m, 0)
            n = round_count(eng)
            with eng.Fori(0, n) as r:
                def rest(i):
                    if i >= NC:
                        return
                    eng.wait_ge(S("lead"), r * NC + (i + 1))
                    nc.vector.tensor_tensor(w_cut[:, 1, i % CUTS],
                                            ring[:, (first + i // 2) % NS, (i % 2) * UNIT:(i % 2 + 1) * UNIT]
                                            .rearrange("p (k c) -> p k c", k=2),
                                            w_cut[:, 0, i % CUTS].bitcast(F32), ALU.subtract)\
                      .then_inc(slot_read if i % 2 else S("rest"), 1)

                rest(0)
                eng.wait_ge(slot_read, r * NSL + first)
                for i in range(1, CUTS):
                    rest(i)
                outputs(r)
                for t in range(TT):
                    ins = nc.vector.tensor_scalar(Sg[:, t, :], col("iota"), RK[:, t, bass.ds(r, 1)],
                                                  GV[:, t, bass.ds(r, 1)], ALU.is_equal, ALU.mult)
                ins.then_inc(S("sg"), 1)
                for g in range(NG):
                    for j in range(8):
                        rest(8 * g + CUTS + j)
                    eng.wait_ge(S("silu"), r * NG + (g + 1))
                    if g >= 2:
                        eng.wait_ge(S("turn"), r * NG + (g - 1))
                    nc.vector.tensor_tensor(hT[:, g % 2, :], t1[:, g % 2, :], ps[:, 2 * (g % 2) + 1, :], ALU.mult)\
                      .then_inc(S("hidden"), 1)
                    if g == 0:
                        sums(r)
                select(bass.ds(r + 1, 1), S("sel"))
                for m in range(2):
                    tokens_rest(m, r + 1)
            outputs(n)
            sums(n)
            eng.wait_ge(S("sum"), n * 4 + 6)
            for k in range(KD):
                nc.vector.tensor_copy(x[:, k, T:NTOK], x[:, k, 0:T]).then_inc(S("x"), 1)

        return dict(name="moe", tensor=tensor, scalar=scalar, vector=vector, sync=extra_slots)

    def add(*items):
        for s in items:
            stages.append(s)

    def done(name, key):
        return lambda eng, n=None: signals[name].wait(eng, key, KD if n is None else n)

    def mixer0_ready(eng):
        eng.wait_ge(sem("mix0_cat"), 4)
        eng.wait_ge(sem("mix0_cat_h"), 4)

    def moe_ready(eng, n):
        eng.wait_ge(sem("moe_x"), n)

    norm0 = modulate("mix0_mod", 0, 0, 0, lambda eng: eng.wait_ge(x_ready, 16))
    add(start(), ada0(norm0.pop("tensor"), norm0.pop("vector")))
    add(norm0, mixer0())
    add(out_proj("mix0_out", "ab_out", 0, mixer0_ready, 0, 2))
    add(modulate("ffn0_mod", 0, 0, 3, done("mix0_out", "x")))
    add(ffn("ffn0", FC, 0, True, 0, 5, lambda act, k: h_block_ready(act, "ffn0_mod", 0, k), h))
    add(modulate("mla_mod", 1, 0, 0, done("ffn0", "x")), mla_proj(), mla_attention())
    add(out_proj("mla_out", "mla_out", T, done("mla_att", "pair"), 1, 2))
    add(modulate("ffn1_mod", 1, T, 3, done("mla_out", "x")))
    add(ffn("ffn1", FC, T, True, 1, 5, lambda act, k: h_block_ready(act, "ffn1_mod", T, k), h))
    add(*swa())
    add(out_proj("swa_out", "swa_out", T, done("swa", "pair")))
    add(layer_norm("ln1", done("swa_out", "x"), 0))
    add(ffn("swiglu", F2, T, False, None, None, lambda act, k: signals["ln1"].wait(act.eng, "x", k + 1), x))
    add(layer_norm("ln2", done("swiglu", "x"), 1))
    add(*nsa())
    add(out_proj("nsa_out", "nsa_out", T, done("nsa", "pair")))
    add(layer_norm("ln3", done("nsa_out", "x"), 2))
    add(moe())
    add(layer_norm("ln4", moe_ready, 3))
    final = "ln4"
    used = NSLOT
    if upto is not None:
        n = [s["name"] for s in stages].index(upto[0])
        stages = stages[:n + 1]
        final, used = upto[1], upto[2]

    class Engine:

        def __init__(self, eng, steps):
            self.eng = eng
            own = Steps(eng, steps)
            self.add, self.settle = own.add, own.settle
            self.slots = Slots(eng)

    def run(engine, part):
        for s in stages:
            if part in s:
                s[part](engine)

    with nc.Block() as block:

        @block.sync
        def _(sp):
            sp.dma_start(tab[:, :], table[:, 0:NRES]).then_inc(table_ready, 16)
            sp.dma_start(arena[:, ARENA - NTAB + NRES:ARENA], table[:, NRES:NTAB]).then_inc(sem("start_masks_in"), 16)
            sp.dma_start(ring[:, 0, :], stream[0]).then_inc(weights_ready[0], 16)
            sp.dma_start(x[:, :, :], x_in).then_inc(x_ready, 16)
            for s in range(1, NS):
                sp.dma_start(ring[:, s, :], stream[s]).then_inc(weights_ready[s], 16)
            with sp.Fori(1, used // NS) as r:
                for s in range(NS):
                    sp.wait_ge(slot_read, r * NS + (s + 1 - NS))
                    sp.dma_start(ring[:, s, :], stream[bass.ds(r * NS + s, 1), :, :].rearrange("o p c -> (o p) c"))\
                      .then_inc(weights_ready[s], 16)
            for n in range(used // NS * NS, used):
                sp.wait_ge(slot_read, n + 1 - NS)
                sp.dma_start(ring[:, n % NS, :], stream[n]).then_inc(weights_ready[n % NS], 16)
            run(Engine(sp, "sync_steps"), "sync")
            signals[final].wait(sp, "x", KD)
            sp.dma_start(out, x[:, :, T:NTOK] if upto is None else x[:, :, :]).then_inc(out_stored, 16)
            sp.wait_ge(out_stored, 16)

        @block.tensor
        def _(pe):
            run(Engine(pe, "tensor_steps"), "tensor")

        @block.scalar
        def _(act):
            run(Engine(act, "scalar_steps"), "scalar")

        @block.vector
        def _(dve):
            run(Engine(dve, "vector_steps"), "vector")

        @block.gpsimd
        def _(pool):
            run(Engine(pool, "gpsimd_steps"), "gpsimd")


def blocks(w):
    k, m = w.shape[0] // P, w.shape[1] // P
    return w.reshape(k, P, m, P).transpose(2, 1, 0, 3).reshape(m, P, k * P)


def slots_of(u):
    per = SLOT // u.shape[2]
    if u.shape[0] % per:
        u = np.concatenate([u, np.zeros((per - u.shape[0] % per,) + u.shape[1:], u.dtype)])
    return u.reshape(-1, per, P, u.shape[2]).transpose(0, 2, 1, 3).reshape(-1, P, SLOT)


def rows_of(w, k):
    n = w.shape[0] // (k * P)
    return w.reshape(n, k, P, w.shape[1]).transpose(0, 2, 1, 3).reshape(n, P, k * w.shape[1])


def pairs(g, v):
    a, b = blocks(g), blocks(v)
    return np.stack([a, b], 1).reshape(-1, P, a.shape[2])


def down(w):
    f = w.shape[0] // P
    return w.reshape(f, P, DQ, DUNIT).transpose(2, 0, 1, 3).reshape(DQ * f, P, DUNIT)


def weight_stream(i):
    ab = i["ab_w_in"][0]
    cuts = np.cumsum([0, 512, 512, 256, 256, 512, 512, 16])
    a, g, q, k, v, o, gt = (ab[:, cuts[n]:cuts[n + 1]] for n in range(7))
    gp = np.zeros((D, P), ab.dtype)
    for n in range(4):
        gp[:, 32 * n:32 * n + HEADS_M] = gt[:, HEADS_M * n:HEADS_M * (n + 1)]
    mi = i["mla_w_in"][0]
    uq, ukv = i["mla_w_uq"][0], i["mla_w_ukv"][0]
    sw = i["a_w_in_2"][0]
    ns = i["b_w_in_2"][0]
    qn, kc, vc, ks, vs, kw, vw = (ns[:, a:b] for a, b in
                                  [(0, 1024)] + [(1024 + 256 * n, 1280 + 256 * n) for n in range(6)])
    parts = {
        "ada0": [rows_of(i["ada_w"][0][:, 512 * c:512 * (c + 1)], 4) for c in range(ADA_CHUNKS)],
        "ada1": [rows_of(i["ada_w"][1][:, 512 * c:512 * (c + 1)], 4) for c in range(ADA_CHUNKS)],
        "ab": [pairs(a, g), np.concatenate([blocks(gp), np.zeros((1, P, UNIT), ab.dtype)]), blocks(q), blocks(k),
               rows_of(v, 4), blocks(o)],
        "ab_out": [blocks(i["ab_w_out"][0])],
        "mla_in": [blocks(mi[:, 0:QL]), blocks(mi[:, QL:QL + KVL])],
        "mla_uq": [rows_of(uq[:, 512 * n:512 * n + 512], 4) for n in range(3)],
        "mla_ukv": [np.concatenate([rows_of(ukv[:, 512 * n:512 * n + 512], 2) for n in range(4)])],
        "mla_out": [blocks(i["mla_w_out"][0])],
        "swa_in": [blocks(sw[:, 0:1280]), rows_of(sw[:, 1280:1536], 8)],
        "swa_out": [blocks(i["a_w_out_2"][0])],
        "swiglu_up": [pairs(i["ffn_w_gate_2"][0], i["ffn_w_up_2"][0])],
        "swiglu_down": [down(i["ffn_w_down_2"][0])],
        "nsa_in": [blocks(qn), blocks(kc), blocks(vc), blocks(ks), blocks(kw),
                   rows_of(np.concatenate([vs, vw], 1), 4)],
        "nsa_cmp": [blocks(i["b_cmp_k_w1_2"][0]), blocks(i["b_cmp_v_w1_2"][0])],
        "nsa_out": [blocks(i["b_w_out_2"][0])],
        "moe": sum(([rows_of(w[0][e][:, c:c + 512], 4) for c in range(0, FF2, 512)
                     for w in (i["moe_w_gate_2"], i["moe_w_up_2"])] + [rows_of(i["moe_w_down_2"][0][e], 1)]
                    for e in range(NEXP)), []),
    }
    for n in range(2):
        w = i["ffn_w_in"][n]
        parts[f"ffn{n}_up"] = [pairs(w[:, 0:FFN], w[:, FFN:2 * FFN])]
        parts[f"ffn{n}_down"] = [down(i["ffn_w_out"][n])]
    stream = np.zeros((NSLOT, P, SLOT), np.float32)
    for name, count in PLAN:
        at = BASE[name]
        for u in parts[name]:
            s = slots_of(u)
            stream[at:at + len(s)] = s
            at += len(s)
        assert at == BASE[name] + count, (name, at - BASE[name], count)
    return stream


def columns(v):
    return v.reshape(-1, P).T


def resident_table(i):
    t = np.zeros((P, NTAB), np.float32)

    def put(name, a):
        c, n = COL[name]
        a = np.asarray(a, np.float32).reshape(-1, n)
        t[0:a.shape[0], c:c + n] = a

    put("c", np.stack([columns(i["c_ctx"]), columns(i["c"][0])], 2))
    put("ada_b", np.concatenate([columns(i["ada_b"][n]) for n in range(2)], 1))
    put("conv_w", i["ab_conv_w"][0].T.reshape(4, P, TAPS).transpose(1, 0, 2))
    put("conv_b", columns(i["ab_conv_b"][0]))
    put("ln_g", columns(i["ab_ln_g"][0]))
    put("ln_b", columns(i["ab_ln_b"][0]))
    put("head_gain", columns(i["ab_head_gain"][0]))
    gb = np.zeros((P, 1), np.float32)
    for n in range(4):
        gb[32 * n:32 * n + HEADS_M, 0] = i["ab_gate_bias"][0][HEADS_M * n:HEADS_M * (n + 1)]
    put("gate_b", gb)
    put("q_norm", columns(i["mla_q_norm"][0]))
    put("kv_norm", columns(i["mla_kv_norm"][0]))
    put("q_gain", np.broadcast_to(i["mla_q_gain"][0], (P, QK_MLA)))
    put("k_gain", np.broadcast_to(i["mla_k_gain"][0], (P, QK_MLA)))
    put("ffn_cw", i["ffn_conv_w"].transpose(0, 2, 1).reshape(2, FC, P, 3).transpose(2, 0, 1, 3))
    put("ffn_cb", i["ffn_conv_b"].reshape(2, FC, P).transpose(2, 0, 1))
    put("kr_w", i["mla_w_in"][0][:, QL + KVL:].reshape(KD, P, ROPE).transpose(1, 0, 2))
    put("ng_w", i["b_w_in_2"][0][:, 2560:2608].reshape(KD, P, 48).transpose(1, 0, 2))
    w2k = i["b_cmp_k_w2_2"][0].reshape(2, P, HD).transpose(1, 0, 2)
    put("w2k", np.concatenate([w2k, w2k], 2))
    put("w2v", i["b_cmp_v_w2_2"][0].reshape(2, P, HD).transpose(1, 0, 2))
    put("router", i["moe_router_2"][0].reshape(KD, P, NEXP).transpose(1, 0, 2))
    put("sinks", np.broadcast_to(i["a_sinks_2"][0], (P, H2)))
    put("pos_k", i["b_cmp_pos_k_2"][0].reshape(LP, P).T)
    put("pos_v", i["b_cmp_pos_v_2"][0].reshape(LP, P).T)
    put("ln2_g", i["ln_gain_2"].reshape(4, KD, P).transpose(2, 0, 1))
    put("ln2_b", i["ln_bias_2"].reshape(4, KD, P).transpose(2, 0, 1))
    eye = np.eye(P, dtype=np.float32)
    put("ident", eye)
    for n in (1024, 512, 256):
        put(f"over{n}", np.full((P, P), 1.0 / n))
    turn = np.zeros((HD, HD), np.float32)
    for d in range(HD // 2):
        turn[d + HD // 2, d], turn[d, d + HD // 2] = -1.0, 1.0
    rot = np.zeros((P, P), np.float32)
    rot[0:HD, 0:HD] = rot[HD:, HD:] = turn
    put("rot", rot)
    for n in range(2):
        for name, m in (("dup", np.eye(HD)), ("rdup", turn)):
            a = np.zeros((P, P), np.float32)
            a[HD * n:HD * (n + 1)] = np.concatenate([m, m], 1)
            put(f"{name}{n}", a)
    f32 = np.float32
    inv = f32(1) / (f32(10000.0) ** (np.arange(0, HD, 2, dtype=f32) / f32(HD)))
    ang = (np.arange(T, dtype=f32)[:, None] * inv[None, :]).astype(f32)
    put("cos2", np.tile(np.cos(ang).T, (4, 1)))
    put("sin2", np.tile(np.sin(ang).T, (4, 1)))
    grid, half = 64, ROPE // 2
    row = np.repeat(np.arange(T // grid, dtype=f32), grid)
    pos = np.tile(np.arange(grid, dtype=f32), T // grid)
    inv = f32(10000.0) ** (-np.arange(0, half, 2, dtype=f32) / f32(half))
    ang = np.concatenate([row[:, None] * inv, pos[:, None] * inv], 1).astype(f32)
    put("cos1", np.cos(ang).reshape(TT, P, 16).transpose(1, 0, 2))
    put("sin1", np.sin(ang).reshape(TT, P, 16).transpose(1, 0, 2))
    a, b = np.arange(P)[:, None], np.arange(P)[None, :]
    put("causal", np.where(b <= a, 0.0, NEG))
    put("band", np.where(b > a, 0.0, NEG))
    put("m_mask", np.stack([np.where(a <= b, 0.0, NEG), np.where(a >= b, 0.0, NEG)], 1))
    end = CMP_STRIDE * np.arange(16) + CMP_LEN - 1
    q = np.arange(T).reshape(TT, P).T[:, :, None]
    ok = (end[None, None, :] <= q) & (np.arange(16) < NCMP)
    put("cmp_mask", np.where(ok, 0.0, NEG))
    put("cmp_valid", ok.any(2))
    put("iota", np.broadcast_to(np.arange(P), (P, P)))
    put("before", np.where(a < b, 1.0 / D, 0.0))
    put("eps6", np.full((P, 1), 1e-6))
    put("eps5", np.full((P, 1), 1e-5))
    return t


def kernel(**inputs):
    import concourse.bacc as bacc
    from concourse.bass_utils import run_bass_kernel_spmd

    i = {n: np.asarray(a) for n, a in inputs.items()}
    tokens = np.concatenate([i["ctx"][0], i["x"][0]], 0)
    arrays = {
        "in_stream_dram": weight_stream(i),
        "in_table_dram": resident_table(i),
        "in_x_dram": np.ascontiguousarray(tokens.reshape(NTOK, KD, P).transpose(2, 1, 0)),
    }
    nc = bacc.Bacc("TRN2", target_bir_lowering=False, num_devices=1)
    args = [nc.dram_tensor(n, a.shape, F32, kind="ExternalInput").ap() for n, a in arrays.items()]
    out = nc.dram_tensor("out_dram", [P, KD, T], F32, kind="ExternalOutput").ap()
    program(nc, *args, out)
    r = run_bass_kernel_spmd(nc, [arrays], core_ids=[0])
    y = r.results[0]["out_dram"]
    return np.ascontiguousarray(y.transpose(2, 1, 0).reshape(1, T, D))
```
